# Optimizing a Trainium2 kernel written in Bass

```python
import jax, jax.numpy as jnp
from jax import lax
import numpy as np
import math

D_MODEL = 1024
BATCH = 1
SEQ = 512
DEPTH = 1

CHUNK = 64
QBLK = 128
N_MIXERS = 4
N_MEM = 256

ATT_HEADS = 16
ATT_HD = D_MODEL // ATT_HEADS
ML_HEADS = 4
ML_DK = D_MODEL // 2 // ML_HEADS
ML_DV = D_MODEL // ML_HEADS
GLA_HEADS = 4
GLA_DK = D_MODEL // 2 // GLA_HEADS
GLA_DV = D_MODEL // GLA_HEADS
GLA_RANK = 16
GLA_TAU = 16.0
XA_HEADS = 4
XA_HD = D_MODEL // XA_HEADS
D_FF = 2816
CONV_W = 3

DN_ALPHA = (2.0 * DEPTH) ** 0.25
DN_BETA = (8.0 * DEPTH) ** -0.25
LN_EPS = 1e-5
RMS_EPS = 1e-6
FOX_F_BIAS = 2.0
ML_F_BIAS = 3.0

SB_IN = 3 * D_MODEL
FOX_IN = 3 * D_MODEL + ATT_HEADS
ML_WIDTHS = [ML_HEADS * ML_DK, ML_HEADS * ML_DK, ML_HEADS * ML_DV, ML_HEADS * ML_DV, ML_HEADS, ML_HEADS]
GLA_WIDTHS = [GLA_HEADS * GLA_DK, GLA_HEADS * GLA_DK, GLA_HEADS * GLA_DV, GLA_HEADS * GLA_DV, GLA_RANK]


F32 = jnp.float32

def _split_cols(t, widths):
    idx = [int(i) for i in np.cumsum(widths)[:-1]]
    return jnp.split(t, idx, axis=-1)

def _heads(t, n):
    b, s, _ = t.shape
    return t.reshape(b, s, n, -1).transpose(0, 2, 1, 3)

def _merge(t):
    b, n, s, d = t.shape
    return t.transpose(0, 2, 1, 3).reshape(b, s, n * d)

def _to_chunks(t):
    b, hh, s = t.shape[:3]
    return jnp.moveaxis(t.reshape(b, hh, s // CHUNK, CHUNK, *t.shape[3:]), 2, 0)

def _from_chunks(t):
    t = jnp.moveaxis(t, 0, 2)
    return t.reshape(t.shape[0], t.shape[1], -1, *t.shape[4:])

def layer_norm(x, g, b):
    xf = x.astype(F32)
    mu = jnp.mean(xf, -1, keepdims=True)
    var = jnp.mean(jnp.square(xf - mu), -1, keepdims=True)
    return ((xf - mu) * lax.rsqrt(var + LN_EPS) * g + b).astype(x.dtype)

def stick_breaking_core(q, k, v):
    seq = q.shape[2]
    scale = q.shape[-1] ** -0.5
    qf, kf, vf = q.astype(F32), k.astype(F32), v.astype(F32)
    outs = []
    for start in range(0, seq, QBLK):
        end = start + QBLK
        z = jnp.einsum('bhtd,bhsd->bhts', qf[:, :, start:end], kf[:, :, :end]) * scale
        earlier = jnp.arange(end)[None, :] < jnp.arange(start, end)[:, None]
        log_keep = jnp.where(earlier, jax.nn.log_sigmoid(-z), 0.0)
        csum = jnp.cumsum(log_keep, axis=-1)
        log_w = jax.nn.log_sigmoid(z) + (csum[..., -1:] - csum)
        w = jnp.where(earlier, jnp.exp(log_w), 0.0)
        outs.append(jnp.einsum('bhts,bhsd->bhtd', w, vf[:, :, :end]))
    return jnp.concatenate(outs, axis=2).astype(v.dtype)

def mixer_stick_breaking(h, w_in):
    q, k, v = jnp.split(h @ w_in, 3, axis=-1)
    o = stick_breaking_core(_heads(q, ATT_HEADS), _heads(k, ATT_HEADS), _heads(v, ATT_HEADS))
    return _merge(o)

def forgetting_core(q, k, v, log_f):
    seq = q.shape[2]
    scale = q.shape[-1] ** -0.5
    qf, kf, vf = q.astype(F32), k.astype(F32), v.astype(F32)
    cum = jnp.cumsum(log_f.astype(F32), axis=-1)
    outs = []
    for start in range(0, seq, QBLK):
        end = start + QBLK
        z = jnp.einsum('bhtd,bhsd->bhts', qf[:, :, start:end], kf[:, :, :end]) * scale
        z = z + cum[:, :, start:end, None] - cum[:, :, None, :end]
        allowed = jnp.arange(end)[None, :] <= jnp.arange(start, end)[:, None]
        p = jax.nn.softmax(jnp.where(allowed, z, -jnp.inf), axis=-1)
        outs.append(jnp.einsum('bhts,bhsd->bhtd', p, vf[:, :, :end]))
    return jnp.concatenate(outs, axis=2).astype(v.dtype)

def mixer_forgetting(h, w_in, b_f):
    qkv, f_pre = _split_cols(h @ w_in, [3 * D_MODEL, ATT_HEADS])
    q, k, v = jnp.split(qkv, 3, axis=-1)
    log_f = jnp.swapaxes(jax.nn.log_sigmoid((f_pre + b_f).astype(F32)), 1, 2)
    o = forgetting_core(_heads(q, ATT_HEADS), _heads(k, ATT_HEADS), _heads(v, ATT_HEADS), log_f)
    return _merge(o)

def mlstm_core(q, k, v, i_pre, f_pre):
    b, nh, _, dk = q.shape
    dv = v.shape[-1]
    causal = jnp.tril(jnp.ones((CHUNK, CHUNK), dtype=bool))
    xs = (_to_chunks(q.astype(F32)), _to_chunks(k.astype(F32)), _to_chunks(v.astype(F32)),
          _to_chunks(i_pre.astype(F32)), _to_chunks(jax.nn.log_sigmoid(f_pre.astype(F32))))

    def step(carry, blk):
        c_st, n_st, m_st = carry
        qb, kb, vb, ib, lfb = blk
        bcum = jnp.cumsum(lfb, axis=-1)
        d = jnp.where(causal, bcum[..., :, None] - bcum[..., None, :] + ib[..., None, :], -jnp.inf)
        inter = bcum + m_st[..., None]
        m_t = jnp.maximum(inter, jnp.max(d, axis=-1))
        w_intra = jnp.exp(d - m_t[..., None])
        w_inter = jnp.exp(inter - m_t)
        qk = jnp.einsum('bhtd,bhsd->bhts', qb, kb) * w_intra
        num = w_inter[..., None] * jnp.einsum('bhtd,bhde->bhte', qb, c_st) + jnp.einsum('bhts,bhse->bhte', qk, vb)
        den = w_inter * jnp.einsum('bhtd,bhd->bht', qb, n_st) + jnp.sum(qk, axis=-1)
        h_out = num / jnp.maximum(jnp.abs(den), jnp.exp(-m_t))[..., None]
        m_new = m_t[..., -1]
        decay = jnp.exp(bcum[..., -1] + m_st - m_new)
        kw = kb * jnp.exp(bcum[..., -1:] - bcum + ib - m_new[..., None])[..., None]
        c_new = decay[..., None, None] * c_st + jnp.einsum('bhsd,bhse->bhde', kw, vb)
        n_new = decay[..., None] * n_st + jnp.sum(kw, axis=2)
        return (c_new, n_new, m_new), h_out

    init = (jnp.zeros((b, nh, dk, dv), F32), jnp.zeros((b, nh, dk), F32), jnp.zeros((b, nh), F32))
    _, hs = lax.scan(step, init, xs)
    return _from_chunks(hs).astype(v.dtype)

def mixer_mlstm(h, w_in, b_i, b_f):
    q, k, v, o, i_pre, f_pre = _split_cols(h @ w_in, ML_WIDTHS)
    i_pre = jnp.swapaxes((i_pre + b_i).astype(F32), 1, 2)
    f_pre = jnp.swapaxes((f_pre + b_f).astype(F32), 1, 2)
    hh = mlstm_core(_heads(q, ML_HEADS), _heads(k, ML_HEADS) * (ML_DK ** -0.5), _heads(v, ML_HEADS), i_pre, f_pre)
    return _merge(hh) * jax.nn.sigmoid(o)

def gla_core(q, k, v, log_a):
    b, nh, _, dk = q.shape
    dv = v.shape[-1]
    causal = jnp.tril(jnp.ones((CHUNK, CHUNK), dtype=bool))[:, :, None]
    xs = (_to_chunks(q.astype(F32)), _to_chunks(k.astype(F32)), _to_chunks(v.astype(F32)), _to_chunks(log_a.astype(F32)))

    def step(state, blk):
        qb, kb, vb, lab = blk
        bcum = jnp.cumsum(lab, axis=2)
        rel = jnp.where(causal, bcum[:, :, :, None, :] - bcum[:, :, None, :, :], -jnp.inf)
        att = jnp.einsum('bhtd,bhsd,bhtsd->bhts', qb, kb, jnp.exp(rel))
        o = jnp.einsum('bhts,bhse->bhte', att, vb) + jnp.einsum('bhtd,bhde->bhte', qb * jnp.exp(bcum), state)
        blast = bcum[:, :, -1:, :]
        new_state = jnp.exp(blast[:, :, 0, :])[..., None] * state + jnp.einsum('bhsd,bhse->bhde', kb * jnp.exp(blast - bcum), vb)
        return new_state, o

    _, os_ = lax.scan(step, jnp.zeros((b, nh, dk, dv), F32), xs)
    return _from_chunks(os_)

def mixer_gla(h, w_in, w_a2, b_a, norm_g):
    q, k, v, r, a_low = _split_cols(h @ w_in, GLA_WIDTHS)
    log_a = jax.nn.log_sigmoid((a_low @ w_a2 + b_a).astype(F32)) / GLA_TAU
    o = gla_core(_heads(q, GLA_HEADS) * (GLA_DK ** -0.5), _heads(k, GLA_HEADS), _heads(v, GLA_HEADS), _heads(log_a, GLA_HEADS))
    o = o * lax.rsqrt(jnp.mean(jnp.square(o), -1, keepdims=True) + RMS_EPS) * norm_g
    return _merge(o.astype(h.dtype)) * jax.nn.silu(r)

def mem_cross_attn(h, mem, w_q, w_kv, w_o):
    q = _heads(h @ w_q, XA_HEADS).astype(F32)
    k, v = jnp.split(mem @ w_kv, 2, axis=-1)
    k = _heads(k, XA_HEADS).astype(F32)
    v = _heads(v, XA_HEADS).astype(F32)
    p = jax.nn.softmax(jnp.einsum('bhtd,bhmd->bhtm', q, k) * (XA_HD ** -0.5), axis=-1)
    o = jnp.einsum('bhtm,bhmd->bhtd', p, v).astype(h.dtype)
    return _merge(o) @ w_o

def conv_ffn(h, w_up, conv_w, conv_b, w_down):
    u = h @ w_up
    ch = u.shape[-1]
    u = lax.conv_general_dilated(u, conv_w, window_strides=(1,), padding=((CONV_W - 1, 0),),
                                 dimension_numbers=('NWC', 'WIO', 'NWC'), feature_group_count=ch) + conv_b
    g, val = jnp.split(u, 2, axis=-1)
    return (jax.nn.gelu(g) * val) @ w_down

def _dense(key, shape, fan_in, gain=1.0):
    return jax.random.normal(key, shape, F32) * (gain * fan_in ** -0.5)

def first_inputs(seed: int = 0) -> dict:
    key = jax.random.key(seed)
    ks = iter(jax.random.split(key, 32))
    D = D_MODEL
    n_occ = [len(range(m, DEPTH, N_MIXERS)) for m in range(N_MIXERS)]
    nrm = lambda shape, s: jax.random.normal(next(ks), shape, F32) * s
    return {
        'x': jax.random.normal(next(ks), (BATCH, SEQ, D), F32),
        'mem': jax.random.normal(next(ks), (BATCH, N_MEM, D), F32),
        'ln_g': 1.0 + nrm((DEPTH, 3, D), 0.02),
        'ln_b': nrm((DEPTH, 3, D), 0.02),
        'mix_wo': _dense(next(ks), (DEPTH, D, D), D, DN_BETA),
        'sb_win': _dense(next(ks), (n_occ[0], D, SB_IN), D),
        'fox_win': _dense(next(ks), (n_occ[1], D, FOX_IN), D),
        'fox_bf': FOX_F_BIAS + nrm((n_occ[1], ATT_HEADS), 0.1),
        'ml_win': _dense(next(ks), (n_occ[2], D, sum(ML_WIDTHS)), D),
        'ml_bi': nrm((n_occ[2], ML_HEADS), 0.1),
        'ml_bf': ML_F_BIAS + nrm((n_occ[2], ML_HEADS), 0.1),
        'gla_win': _dense(next(ks), (n_occ[3], D, sum(GLA_WIDTHS)), D),
        'gla_wa2': _dense(next(ks), (n_occ[3], GLA_RANK, GLA_HEADS * GLA_DK), GLA_RANK),
        'gla_ba': nrm((n_occ[3], GLA_HEADS * GLA_DK), 0.1),
        'gla_norm_g': 1.0 + nrm((n_occ[3], GLA_DV), 0.02),
        'xa_wq': _dense(next(ks), (DEPTH, D, D), D),
        'xa_wkv': _dense(next(ks), (DEPTH, D, 2 * D), D),
        'xa_wo': _dense(next(ks), (DEPTH, D, D), D, DN_BETA),
        'ffn_up': _dense(next(ks), (DEPTH, D, 2 * D_FF), D),
        'ffn_conv': _dense(next(ks), (DEPTH, CONV_W, 1, 2 * D_FF), CONV_W),
        'ffn_conv_b': nrm((DEPTH, 2 * D_FF), 0.02),
        'ffn_down': _dense(next(ks), (DEPTH, D_FF, D), D_FF, DN_BETA),
    }

def first_block(x, mem, ln_g, ln_b, mix_wo, sb_win, fox_win, fox_bf, ml_win, ml_bi, ml_bf,
              gla_win, gla_wa2, gla_ba, gla_norm_g, xa_wq, xa_wkv, xa_wo,
              ffn_up, ffn_conv, ffn_conv_b, ffn_down):
    h = x
    for layer in range(DEPTH):
        kind = layer % N_MIXERS
        occ = layer // N_MIXERS
        if kind == 0:
            y = mixer_stick_breaking(h, sb_win[occ])
        elif kind == 1:
            y = mixer_forgetting(h, fox_win[occ], fox_bf[occ])
        elif kind == 2:
            y = mixer_mlstm(h, ml_win[occ], ml_bi[occ], ml_bf[occ])
        else:
            y = mixer_gla(h, gla_win[occ], gla_wa2[occ], gla_ba[occ], gla_norm_g[occ])
        h = layer_norm(DN_ALPHA * h + y @ mix_wo[layer], ln_g[layer, 0], ln_b[layer, 0])
        h = layer_norm(DN_ALPHA * h + mem_cross_attn(h, mem, xa_wq[layer], xa_wkv[layer], xa_wo[layer]),
                       ln_g[layer, 1], ln_b[layer, 1])
        h = layer_norm(DN_ALPHA * h + conv_ffn(h, ffn_up[layer], ffn_conv[layer], ffn_conv_b[layer], ffn_down[layer]),
                       ln_g[layer, 2], ln_b[layer, 2])
    return h


DEPTH_2 = 2

N_A = DEPTH_2 // 2
N_B = DEPTH_2 - N_A
EPS = 1e-6

D_FF_2 = ((8 * D_MODEL + 3 * 256 - 1) // (3 * 256)) * 256

SSM_EXPAND = 2
D_INNER = SSM_EXPAND * D_MODEL
SSM_HEADDIM = 64
SSM_HEADS = D_INNER // SSM_HEADDIM
SSM_STATE = 128
SSM_GROUPS = 4
SSM_HPG = SSM_HEADS // SSM_GROUPS
CONV_W_2 = 4
SSD_CHUNK = 256
D_XBC = D_INNER + 2 * SSM_GROUPS * SSM_STATE
D_SSM_IN = D_INNER + D_XBC + SSM_HEADS

NSA_HEADS = 16
NSA_KV_HEADS = 4
NSA_GROUP = NSA_HEADS // NSA_KV_HEADS
NSA_HEAD_DIM = 64
CMP_BLOCK = 32
CMP_STRIDE = 16
CMP_HIDDEN = 256
SEL_BLOCK = 64
N_SEL = 16
WINDOW = 512
Q_BLOCK = 128
N_BRANCH = 3
D_NSA_Q = NSA_HEADS * NSA_HEAD_DIM + NSA_HEADS * N_BRANCH
D_KV = 6 * NSA_KV_HEADS * NSA_HEAD_DIM

ROPE_THETA = 500000.0
ROT_DIMS = NSA_HEAD_DIM // 4


def rmsnorm(x, g):
    xf = x.astype(jnp.float32)
    y = xf * lax.rsqrt(jnp.mean(xf * xf, axis=-1, keepdims=True) + EPS)
    return (y * g.astype(jnp.float32)).astype(x.dtype)

def adaln(x, g, shift, scale):
    return rmsnorm(x, g) * (1 + scale[:, None, :]) + shift[:, None, :]

def partial_rope(x, pos):
    half = ROT_DIMS // 2
    inv_freq = ROPE_THETA ** (-jnp.arange(half, dtype=jnp.float32) / half)
    ang = pos.astype(jnp.float32)[:, None] * inv_freq[None, :]
    bshape = (1, pos.shape[0]) + (1,) * (x.ndim - 3) + (half,)
    cos = jnp.cos(ang).reshape(bshape)
    sin = jnp.sin(ang).reshape(bshape)
    x1 = x[..., :half].astype(jnp.float32)
    x2 = x[..., half:ROT_DIMS].astype(jnp.float32)
    rot = jnp.concatenate([x1 * cos - x2 * sin, x2 * cos + x1 * sin], axis=-1).astype(x.dtype)
    return jnp.concatenate([rot, x[..., ROT_DIMS:]], axis=-1)

def masked_softmax(s, mask, axis):
    s = jnp.where(mask, s.astype(jnp.float32), -jnp.inf)
    m = jnp.max(s, axis=axis, keepdims=True)
    m = jnp.where(jnp.isfinite(m), m, 0.0)
    p = jnp.exp(s - m)
    d = jnp.sum(p, axis=axis, keepdims=True)
    return p / jnp.where(d > 0, d, 1.0)

def swiglu(h, w_in, w_out):
    a, b = jnp.split(h @ w_in, 2, axis=-1)
    return (jax.nn.silu(a) * b) @ w_out

def causal_dwconv(x, w, b):
    y = lax.conv_general_dilated(
        x, w[:, None, :].astype(x.dtype), window_strides=(1,),
        padding=[(CONV_W_2 - 1, 0)], dimension_numbers=("NWC", "WIO", "NWC"),
        feature_group_count=x.shape[-1])
    return y + b

def ssd_scan(x, bm, cm, dt_raw, dt_bias, a_log):
    f32 = jnp.float32
    bsz, s_len, n_h, p_dim = x.shape
    L = math.gcd(s_len, SSD_CHUNK)
    nc = s_len // L
    G, J, N = SSM_GROUPS, SSM_HPG, SSM_STATE
    A = -jnp.exp(a_log.astype(f32))
    dt = jax.nn.softplus(dt_raw.astype(f32) + dt_bias.astype(f32))

    def to_chunks(a):
        return jnp.moveaxis(a.astype(f32).reshape((bsz, nc, L) + a.shape[2:]), 1, 0)

    causal = jnp.tril(jnp.ones((L, L), dtype=bool))

    def step(state, inp):
        xk, bk, ck, dtk = inp
        acs = jnp.cumsum(dtk * A, axis=1)
        seg = acs[:, :, None, :] - acs[:, None, :, :]
        decay = jnp.exp(jnp.where(causal[None, :, :, None], seg, -jnp.inf)).reshape(bsz, L, L, G, J)
        xdt = (xk * dtk[..., None]).reshape(bsz, L, G, J, p_dim)
        cb = jnp.einsum("blgn,bsgn->blsg", ck, bk)
        y_intra = jnp.einsum("blsg,blsgj,bsgjp->blgjp", cb, decay, xdt)
        y_inter = jnp.einsum("blgn,bgjpn->blgjp", ck, state) * jnp.exp(acs).reshape(bsz, L, G, J)[..., None]
        tail = jnp.exp(acs[:, -1:, :] - acs).reshape(bsz, L, G, J)
        state = (state * jnp.exp(acs[:, -1]).reshape(bsz, G, J)[..., None, None]
                 + jnp.einsum("bsgn,bsgj,bsgjp->bgjpn", bk, tail, xdt))
        return state, (y_intra + y_inter).reshape(bsz, L, n_h, p_dim)

    state0 = jnp.zeros((bsz, G, J, p_dim, N), f32)
    _, ys = lax.scan(step, state0, (to_chunks(x), to_chunks(bm), to_chunks(cm), to_chunks(dt)))
    return jnp.moveaxis(ys, 0, 1).reshape(bsz, s_len, n_h, p_dim)

def mamba2_mixer(h, w_in, conv_w, conv_b, dt_bias, a_log, d_skip, norm_g, w_out):
    bsz, s_len, _ = h.shape
    proj = h @ w_in
    z, xbc, dt = jnp.split(proj, [D_INNER, D_INNER + D_XBC], axis=-1)
    xbc = jax.nn.silu(causal_dwconv(xbc, conv_w, conv_b))
    xs, bm, cm = jnp.split(xbc, [D_INNER, D_INNER + SSM_GROUPS * SSM_STATE], axis=-1)
    xs = xs.reshape(bsz, s_len, SSM_HEADS, SSM_HEADDIM)
    y = ssd_scan(xs, bm.reshape(bsz, s_len, SSM_GROUPS, SSM_STATE),
                 cm.reshape(bsz, s_len, SSM_GROUPS, SSM_STATE), dt, dt_bias, a_log)
    y = (y + d_skip.astype(jnp.float32)[:, None] * xs.astype(jnp.float32)).astype(h.dtype)
    y = y.reshape(bsz, s_len, D_INNER) * jax.nn.silu(z)
    y = rmsnorm(y.reshape(bsz, s_len, SSM_GROUPS, D_INNER // SSM_GROUPS),
                norm_g.reshape(SSM_GROUPS, D_INNER // SSM_GROUPS))
    return y.reshape(bsz, s_len, D_INNER) @ w_out

def nsa_shared_kv(stream, cs, kv_norm, kv_mod_w, kv_mod_b, w_kv,
                  cmp_pos_k, cmp_w1_k, cmp_w2_k, cmp_pos_v, cmp_w1_v, cmp_w2_v):
    bsz, s_len, _ = stream.shape
    shift, scale = jnp.split(cs @ kv_mod_w + kv_mod_b, 2, axis=-1)
    h = adaln(stream, kv_norm, shift, scale)
    kv = (h @ w_kv).reshape(bsz, s_len, 6, NSA_KV_HEADS, NSA_HEAD_DIM)
    k_c, v_c, k_s, v_s, k_w, v_w = [kv[:, :, i] for i in range(6)]
    pos = jnp.arange(s_len)
    n_cmp = (s_len - CMP_BLOCK) // CMP_STRIDE + 1
    idx = jnp.arange(n_cmp)[:, None] * CMP_STRIDE + jnp.arange(CMP_BLOCK)[None, :]

    def compress(t, pe, w1, w2):
        blk = t[:, idx] + pe[None, None, :, None, :]
        blk = jnp.moveaxis(blk, 3, 2).reshape(bsz, n_cmp, NSA_KV_HEADS, CMP_BLOCK * NSA_HEAD_DIM)
        return jax.nn.silu(blk @ w1) @ w2

    k_cmp = compress(k_c, cmp_pos_k, cmp_w1_k, cmp_w2_k)
    v_cmp = compress(v_c, cmp_pos_v, cmp_w1_v, cmp_w2_v)
    nsb = s_len // SEL_BLOCK
    k_sel = partial_rope(k_s, pos).reshape(bsz, nsb, SEL_BLOCK, NSA_KV_HEADS, NSA_HEAD_DIM).transpose(0, 3, 1, 2, 4)
    v_sel = v_s.reshape(bsz, nsb, SEL_BLOCK, NSA_KV_HEADS, NSA_HEAD_DIM).transpose(0, 3, 1, 2, 4)
    pad = ((0, 0), (WINDOW, 0), (0, 0), (0, 0))
    k_win = jnp.pad(partial_rope(k_w, pos), pad)
    v_win = jnp.pad(v_w, pad)
    return k_cmp, v_cmp, k_sel, v_sel, k_win, v_win

def nsa_mixer(h, w_q, w_o, k_cmp, v_cmp, k_sel, v_sel, k_win, v_win):
    bsz, s_len, _ = h.shape
    nq = s_len // Q_BLOCK
    nsb = s_len // SEL_BLOCK
    n_sel = min(N_SEL, nsb)
    n_cmp = k_cmp.shape[1]
    n_units = s_len // CMP_STRIDE
    units = CMP_BLOCK // CMP_STRIDE
    scale = NSA_HEAD_DIM ** -0.5
    proj = h @ w_q
    q = proj[..., :NSA_HEADS * NSA_HEAD_DIM].reshape(bsz, s_len, NSA_KV_HEADS, NSA_GROUP, NSA_HEAD_DIM)
    gates = jax.nn.sigmoid(proj[..., NSA_HEADS * NSA_HEAD_DIM:].astype(jnp.float32)).reshape(
        bsz, s_len, NSA_KV_HEADS, NSA_GROUP, N_BRANCH)
    q_rot = partial_rope(q, jnp.arange(s_len))
    cmp_end = jnp.arange(n_cmp) * CMP_STRIDE + CMP_BLOCK - 1

    def blocks(a):
        return jnp.moveaxis(a.reshape((bsz, nq, Q_BLOCK) + a.shape[2:]), 1, 0)

    def one_block(args):
        qi, qc, qr, g = args
        t = qi * Q_BLOCK + jnp.arange(Q_BLOCK)
        s = jnp.einsum("bqhgd,bchd->bhgqc", qc, k_cmp) * scale
        p_cmp = masked_softmax(s, (cmp_end[None, :] <= t[:, None])[None, None, None], axis=-1)
        o_cmp = jnp.einsum("bhgqc,bchd->bqhgd", p_cmp.astype(v_cmp.dtype), v_cmp)
        p_grp = p_cmp.sum(axis=2)
        u = sum(jnp.pad(p_grp, ((0, 0), (0, 0), (0, 0), (r, n_units - n_cmp - r))) for r in range(units))
        imp = u.reshape(bsz, NSA_KV_HEADS, Q_BLOCK, nsb, SEL_BLOCK // CMP_STRIDE).sum(axis=-1)
        qblk = t // SEL_BLOCK
        j = jnp.arange(nsb)
        forced = (j[None] == 0) | (j[None] == qblk[:, None]) | (j[None] == qblk[:, None] - 1)
        causal_blk = j[None] <= qblk[:, None]
        score = jnp.where(forced, jnp.inf, jnp.where(causal_blk, imp, -1.0))
        _, sel = lax.top_k(score, n_sel)
        gather = jax.vmap(jax.vmap(lambda kk, ii: kk[ii]))
        ks = gather(k_sel, sel)
        vs = gather(v_sel, sel)
        tok = sel[..., None] * SEL_BLOCK + jnp.arange(SEL_BLOCK)
        s = jnp.einsum("bqhgd,bhqnkd->bhgqnk", qr, ks) * scale
        p = masked_softmax(s, (tok <= t[None, None, :, None, None])[:, :, None], axis=(-2, -1))
        o_sel = jnp.einsum("bhgqnk,bhqnkd->bqhgd", p.astype(vs.dtype), vs)
        kw = lax.dynamic_slice_in_dim(k_win, qi * Q_BLOCK, WINDOW + Q_BLOCK, axis=1)
        vw = lax.dynamic_slice_in_dim(v_win, qi * Q_BLOCK, WINDOW + Q_BLOCK, axis=1)
        kp = qi * Q_BLOCK - WINDOW + jnp.arange(WINDOW + Q_BLOCK)
        wmask = (kp[None] <= t[:, None]) & (kp[None] > t[:, None] - WINDOW) & (kp[None] >= 0)
        s = jnp.einsum("bqhgd,bkhd->bhgqk", qr, kw) * scale
        p = masked_softmax(s, wmask[None, None, None], axis=-1)
        o_win = jnp.einsum("bhgqk,bkhd->bqhgd", p.astype(vw.dtype), vw)
        o = g[..., 0:1] * o_cmp + g[..., 1:2] * o_sel + g[..., 2:3] * o_win
        return o.astype(h.dtype)

    o = lax.map(one_block, (jnp.arange(nq), blocks(q), blocks(q_rot), blocks(gates)))
    o = jnp.moveaxis(o, 0, 1).reshape(bsz, s_len, NSA_HEADS * NSA_HEAD_DIM)
    return o @ w_o

def second_inputs(seed: int = 0) -> dict:
    key = jax.random.key(seed)
    ks = iter(jax.random.split(key, 48))
    f32 = jnp.float32
    D = D_MODEL

    def nrm(shape, scale):
        return jax.random.normal(next(ks), shape, f32) * scale

    def gain(shape):
        return 1.0 + nrm(shape, 0.05)

    x = nrm((BATCH, SEQ, D), 1.0)
    c = nrm((BATCH, D), 1.0)
    gate_offset = jnp.tile(jnp.repeat(jnp.array([0.0, 0.0, 1.0], f32), D), 2)
    mod_w = nrm((DEPTH_2, D, 6 * D), 0.1 * D ** -0.5)
    mod_b = nrm((DEPTH_2, 6 * D), 0.02) + gate_offset
    norm_pre_mix = gain((DEPTH_2, D))
    norm_post_mix = gain((DEPTH_2, D))
    norm_pre_ffn = gain((DEPTH_2, D))
    norm_post_ffn = gain((DEPTH_2, D))
    ffn_w_in = nrm((DEPTH_2, D, 2 * D_FF_2), D ** -0.5)
    ffn_w_out = nrm((DEPTH_2, D_FF_2, D), D_FF_2 ** -0.5)
    ssm_w_in = nrm((N_A, D, D_SSM_IN), D ** -0.5)
    ssm_conv_w = nrm((N_A, CONV_W_2, D_XBC), CONV_W_2 ** -0.5)
    ssm_conv_b = nrm((N_A, D_XBC), 0.02)
    dt0 = jnp.exp(jax.random.uniform(next(ks), (N_A, SSM_HEADS), f32, math.log(1e-3), math.log(1e-1)))
    ssm_dt_bias = dt0 + jnp.log(-jnp.expm1(-dt0))
    ssm_a_log = jnp.log(jax.random.uniform(next(ks), (N_A, SSM_HEADS), f32, 1.0, 16.0))
    ssm_d = gain((N_A, SSM_HEADS))
    ssm_norm = gain((N_A, D_INNER))
    ssm_w_out = nrm((N_A, D_INNER, D), D_INNER ** -0.5)
    kv_norm = gain((D,))
    kv_mod_w = nrm((D, 2 * D), 0.1 * D ** -0.5)
    kv_mod_b = nrm((2 * D,), 0.02)
    w_kv = nrm((D, D_KV), D ** -0.5)
    cmp_pos_k = nrm((CMP_BLOCK, NSA_HEAD_DIM), 0.1)
    cmp_w1_k = nrm((CMP_BLOCK * NSA_HEAD_DIM, CMP_HIDDEN), (CMP_BLOCK * NSA_HEAD_DIM) ** -0.5)
    cmp_w2_k = nrm((CMP_HIDDEN, NSA_HEAD_DIM), CMP_HIDDEN ** -0.5)
    cmp_pos_v = nrm((CMP_BLOCK, NSA_HEAD_DIM), 0.1)
    cmp_w1_v = nrm((CMP_BLOCK * NSA_HEAD_DIM, CMP_HIDDEN), (CMP_BLOCK * NSA_HEAD_DIM) ** -0.5)
    cmp_w2_v = nrm((CMP_HIDDEN, NSA_HEAD_DIM), CMP_HIDDEN ** -0.5)
    nsa_w_q = nrm((N_B, D, D_NSA_Q), D ** -0.5)
    nsa_w_o = nrm((N_B, NSA_HEADS * NSA_HEAD_DIM, D), (NSA_HEADS * NSA_HEAD_DIM) ** -0.5)
    return {"x": x, "c": c, "mod_w": mod_w, "mod_b": mod_b,
            "norm_pre_mix": norm_pre_mix, "norm_post_mix": norm_post_mix,
            "norm_pre_ffn": norm_pre_ffn, "norm_post_ffn": norm_post_ffn,
            "ffn_w_in": ffn_w_in, "ffn_w_out": ffn_w_out,
            "ssm_w_in": ssm_w_in, "ssm_conv_w": ssm_conv_w, "ssm_conv_b": ssm_conv_b,
            "ssm_dt_bias": ssm_dt_bias, "ssm_a_log": ssm_a_log, "ssm_d": ssm_d,
            "ssm_norm": ssm_norm, "ssm_w_out": ssm_w_out,
            "kv_norm": kv_norm, "kv_mod_w": kv_mod_w, "kv_mod_b": kv_mod_b, "w_kv": w_kv,
            "cmp_pos_k": cmp_pos_k, "cmp_w1_k": cmp_w1_k, "cmp_w2_k": cmp_w2_k,
            "cmp_pos_v": cmp_pos_v, "cmp_w1_v": cmp_w1_v, "cmp_w2_v": cmp_w2_v,
            "nsa_w_q": nsa_w_q, "nsa_w_o": nsa_w_o}

def second_block(x, c, mod_w, mod_b, norm_pre_mix, norm_post_mix, norm_pre_ffn, norm_post_ffn,
              ffn_w_in, ffn_w_out, ssm_w_in, ssm_conv_w, ssm_conv_b, ssm_dt_bias, ssm_a_log,
              ssm_d, ssm_norm, ssm_w_out, kv_norm, kv_mod_w, kv_mod_b, w_kv,
              cmp_pos_k, cmp_w1_k, cmp_w2_k, cmp_pos_v, cmp_w1_v, cmp_w2_v, nsa_w_q, nsa_w_o):
    cs = jax.nn.silu(c)
    shared = None
    for i in range(DEPTH_2):
        sh_m, sc_m, g_m, sh_f, sc_f, g_f = jnp.split(cs @ mod_w[i] + mod_b[i], 6, axis=-1)
        if i == N_A:
            shared = nsa_shared_kv(x, cs, kv_norm, kv_mod_w, kv_mod_b, w_kv,
                                   cmp_pos_k, cmp_w1_k, cmp_w2_k, cmp_pos_v, cmp_w1_v, cmp_w2_v)
        h = adaln(x, norm_pre_mix[i], sh_m, sc_m)
        if i < N_A:
            y = mamba2_mixer(h, ssm_w_in[i], ssm_conv_w[i], ssm_conv_b[i], ssm_dt_bias[i],
                             ssm_a_log[i], ssm_d[i], ssm_norm[i], ssm_w_out[i])
        else:
            y = nsa_mixer(h, nsa_w_q[i - N_A], nsa_w_o[i - N_A], *shared)
        x = x + g_m[:, None, :] * rmsnorm(y, norm_post_mix[i])
        h = adaln(x, norm_pre_ffn[i], sh_f, sc_f)
        x = x + g_f[:, None, :] * rmsnorm(swiglu(h, ffn_w_in[i], ffn_w_out[i]), norm_post_ffn[i])
    return x


def setup_inputs(seed=0):
    out = dict(first_inputs(seed))
    for name, value in second_inputs(seed + 1).items():
        if name != "x":
            out[name + "_2"] = value
    return out


def reference(
    x, mem, ln_g, ln_b, mix_wo, sb_win, fox_win, fox_bf, ml_win, ml_bi, ml_bf, gla_win, gla_wa2,
    gla_ba, gla_norm_g, xa_wq, xa_wkv, xa_wo, ffn_up, ffn_conv, ffn_conv_b, ffn_down, c_2,
    mod_w_2, mod_b_2, norm_pre_mix_2, norm_post_mix_2, norm_pre_ffn_2, norm_post_ffn_2,
    ffn_w_in_2, ffn_w_out_2, ssm_w_in_2, ssm_conv_w_2, ssm_conv_b_2, ssm_dt_bias_2, ssm_a_log_2,
    ssm_d_2, ssm_norm_2, ssm_w_out_2, kv_norm_2, kv_mod_w_2, kv_mod_b_2, w_kv_2, cmp_pos_k_2,
    cmp_w1_k_2, cmp_w2_k_2, cmp_pos_v_2, cmp_w1_v_2, cmp_w2_v_2, nsa_w_q_2, nsa_w_o_2,
):
    x = first_block(
        x, mem, ln_g, ln_b, mix_wo, sb_win, fox_win, fox_bf, ml_win, ml_bi, ml_bf, gla_win,
        gla_wa2, gla_ba, gla_norm_g, xa_wq, xa_wkv, xa_wo, ffn_up, ffn_conv, ffn_conv_b,
        ffn_down,
    )
    return second_block(
        x, c_2, mod_w_2, mod_b_2, norm_pre_mix_2, norm_post_mix_2, norm_pre_ffn_2,
        norm_post_ffn_2, ffn_w_in_2, ffn_w_out_2, ssm_w_in_2, ssm_conv_w_2, ssm_conv_b_2,
        ssm_dt_bias_2, ssm_a_log_2, ssm_d_2, ssm_norm_2, ssm_w_out_2, kv_norm_2, kv_mod_w_2,
        kv_mod_b_2, w_kv_2, cmp_pos_k_2, cmp_w1_k_2, cmp_w2_k_2, cmp_pos_v_2, cmp_w1_v_2,
        cmp_w2_v_2, nsa_w_q_2, nsa_w_o_2,
    )


_drawn_inputs = setup_inputs


def setup_inputs(seed=0):
    import zlib

    import numpy as np

    out = dict(_drawn_inputs(seed))
    spreads = {}
    factors = {'ffn_conv_b': 3.667, 'cmp_pos_k_2': 7.18}
    for name, (base, spread) in spreads.items():
        noise = np.random.default_rng([zlib.crc32(name.encode()), seed]).standard_normal(out[name].shape)
        drawn = base * np.exp(spread * noise) if base else spread * noise
        out[name] = __import__('jax').numpy.asarray(drawn.astype(out[name].dtype))
    for name, factor in factors.items():
        out[name] = (out[name] * factor).astype(out[name].dtype)
    return out
```

```python
from contextlib import ExitStack, contextmanager

import numpy as np
import concourse.bass as bass
from concourse import mybir

F32 = mybir.dt.float32
F32R = mybir.dt.float32r
BF16 = mybir.dt.bfloat16
ALU = mybir.AluOpType
ACT = mybir.ActivationFunctionType
AX = mybir.AxisListType

P = 128
SEQ, D = 512, 1024
TB = SEQ // P
KC = D // P
MEM = 256
MB = MEM // P
DFF = 2816
FC = DFF // P
XA_HEADS = 4
DI = 2048
SSM_H, SSM_G, HPG = 32, 4, 8
HD, ROT = 64, 16
KV, QG = 4, 4
N_CMP, CMP = 31, 32
ALPHA = 2.0 ** 0.25
NEG = -1.0e30
LN_EPS = 1e-5
SOFTPLUS_MAX = 40.0


class Turns:

    def __init__(self):
        self.seen, self.turn, self.step = {}, None, {}

    def __call__(self, sem, n=1):
        self.seen[sem.name] = self.seen.get(sem.name, 0) + n
        value = self.seen[sem.name]
        if self.turn is not None:
            if sem.name not in self.step:
                raise ValueError(f"{sem.name}: no step per turn given")
            value = self.turn * self.step[sem.name] + value
        return value

    @contextmanager
    def loop(self, eng, count, steps):
        before = dict(self.seen)
        self.step = {s.name: n for s, n in steps.items()}
        with eng.Fori(0, count) as turn:
            self.turn = turn
            yield turn
            self.turn = None
        grown = {k: v - before.get(k, 0) for k, v in self.seen.items() if v != before.get(k, 0)}
        assert grown == {k: v for k, v in self.step.items() if v}, f"a turn waits for {grown}, given {self.step}"
        for k, v in grown.items():
            self.seen[k] = before.get(k, 0) + v * count
        self.step = {}


def shape_constants():
    p = np.arange(P)[:, None]
    f = np.arange(P)[None, :]
    upper = (p <= f).astype(np.float32)
    ones = np.ones((P, P), np.float32)
    return {
        "c_ident": np.eye(P, dtype=np.float32),
        "c_neg_suffix": -(p >= f).astype(np.float32),
        "c_causal6": np.concatenate([upper, ones, upper, upper, ones, upper], axis=1),
        "c_select": head_selections(),
        "c_rotary": rotary_tables(),
        "c_compressed": compressed_masks(),
    }


def swap(d):
    return d + ROT // 2 if d < ROT // 2 else d - ROT // 2


def head_selections():
    m = np.zeros((P, 5, P), np.float32)
    for half in range(2):
        for out_half in range(2):
            for d in range(HD):
                m[HD * half + d, half, HD * out_half + d] = 1
                if d < ROT:
                    m[HD * half + swap(d), 2 + half, HD * out_half + d] = 1
        for d in range(ROT):
            m[HD * half + swap(d), 4, HD * half + d] = 1
    return m.reshape(P, 5 * P)


def rotary_tables():
    half = ROT // 2
    inv = np.float32(500000.0) ** (-np.arange(half, dtype=np.float32) / np.float32(half))
    angle = np.arange(SEQ, dtype=np.float32)[:, None] * inv[None, :]
    cos, sin = np.cos(angle).T, np.sin(angle).T
    table = np.zeros((P, 2, SEQ), np.float32)
    table[:, 0] = 1
    for head in range(2):
        r = HD * head
        table[r:r + half, 0], table[r + half:r + ROT, 0] = cos, cos
        table[r:r + half, 1], table[r + half:r + ROT, 1] = sin, -sin
    return table.reshape(P, 2 * SEQ)


def compressed_masks():
    t = np.arange(SEQ).reshape(TB, P).T[:, :, None]
    c = np.arange(CMP)[None, None, :]
    mask = np.where((16 * c + 31 <= t) & (c < N_CMP), 0.0, NEG).astype(np.float32)
    same = (np.arange(P)[:, None] // CMP == np.arange(4)[None, :]).astype(np.float32)
    return np.concatenate([mask.reshape(P, TB * CMP), same], axis=1)


def param_rows(a):
    rows = lambda x: x.rearrange("(r c) -> r c", c=P)
    plan = [
        [("tap0", rows(a["ffn_conv"][0, 0, 0])), ("tap1", rows(a["ffn_conv"][0, 1, 0])),
         ("pre_mix", a["norm_pre_mix_2"].rearrange("l (r c) -> (l r) c", c=P)),
         ("pre_ffn", a["norm_pre_ffn_2"].rearrange("l (r c) -> (l r) c", c=P)), ("kv_norm", rows(a["kv_norm_2"]))],
        [("tap2", rows(a["ffn_conv"][0, 2, 0])), ("conv_b", rows(a["ffn_conv_b"][0])),
         ("ssm_conv_b", rows(a["ssm_conv_b_2"][0])), ("ssm_norm", rows(a["ssm_norm_2"][0]))],
        [("ssm_taps", a["ssm_conv_w_2"][0].rearrange("w (r c) -> (w r) c", c=P)), ("c", rows(a["c_2"][0])),
         ("cmp_pos_v", a["cmp_pos_v_2"].rearrange("(r two) d -> r (two d)", two=2))],
        [("mod_b", a["mod_b_2"].rearrange("l (r c) -> (l r) c", c=P)), ("kv_mod_b", rows(a["kv_mod_b_2"])),
         ("cmp_pos_k", a["cmp_pos_k_2"].rearrange("(r two) d -> r (two d)", two=2))],
    ]
    for tile, entries in enumerate(plan):
        row = 0
        for name, src in entries:
            yield tile, row, name, src
            row += src.shape[0]


N_PARAMS = 3 + 15
N_MOD = 2 * 48 + 16
NSA_PARAMS = 7
SET_UP = 5
FREE0 = 4
SLOTS = 2
HID0 = 2
DONE0 = 1
TURNED0 = 4
MODS = 2
RMS_EPS = 1e-6


def build(nc, a, out):
    ctx = ExitStack()

    def sem(name):
        return ctx.enter_context(nc.semaphore(name))

    top = [16512]

    def place(name, shape, dt=F32, at=None):
        size = int(np.prod(shape[1:])) * (2 if dt == BF16 else 4)
        offset = top[0] if at is None else at
        if at is None:
            top[0] += -(-size // 32) * 32
        return nc.alloc_sbuf_tensor_at(name, shape, dt, offset=offset)

    raw = place("raw", [P, 2, 2048])
    whi = place("whi", [P, 2, 2048], F32R)
    wlo = place("wlo", [P, 2, 2048], F32R)
    ACTS = top[0]
    acth = place("acth", [P, KC, SEQ], F32R)
    actl = place("actl", [P, KC, SEQ], F32R)
    h = place("h", [P, TB, D])
    ident = place("ident", [P, P])
    ident_b = place("ident_b", [P, P], BF16)
    strict_b = place("strict_b", [P, P], BF16)
    causal_b = place("causal_b", [P, P], BF16)
    neg_suffix = place("neg_suffix", [P, P])
    neg_ones = place("neg_ones", [P, P])
    causal6 = place("causal6", [P, 6 * P])
    cols = place("cols", [P, 4 * P])
    stats = place("stats", [P, TB, 2, 6])
    mean_var = place("mean_var", [P, TB, 2])
    rstd = place("rstd", [P, TB])
    small = place("small", [P, 64])
    neg_half = place("neg_half", [P, 16])
    ones_c = place("ones_c", [P, 1])
    c_silu = place("c_silu", [P, KC])
    modv = place("modv", [P, N_MOD])
    gains = place("gains", [P, 5, KC])
    WIDE = top[0]
    gb = place("gb", [P, 2, D])
    conv_t = place("conv_t", [P, 4, SEQ], at=WIDE)
    ARENA = top[0]
    arena_end = 229368
    assert ARENA + 2 * FC * SEQ * 4 <= arena_end, (ARENA, arena_end)

    hid_h = place("hid_h", [P, FC, SEQ], F32R, at=ARENA)
    hid_l = place("hid_l", [P, FC, SEQ], F32R, at=ARENA + FC * SEQ * 4)

    o = ARENA
    q_t = place("q_t", [P, KC, SEQ], at=o); o += 16384
    k_t = place("k_t", [P, KC, SEQ], at=o); o += 16384
    v_s = place("v_s", [P, TB, D], at=o); o += 16384
    qst = place("qst", [P, 2, SEQ], at=o); o += 4096
    kst = place("kst", [P, 2, SEQ], at=o); o += 4096
    vst = place("vst", [P, 2, TB, P], at=o); o += 4096
    CAUSAL = 1280
    sp_e = place("sp_e", [P, 2, CAUSAL], at=o); o += 2 * CAUSAL * 4
    sp = place("sp", [P, 2, CAUSAL], at=o); o += 2 * CAUSAL * 4
    wts = place("wts", [P, 2, CAUSAL], at=o); o += 2 * CAUSAL * 4
    assert o <= arena_end, (o, arena_end)
    x_in = place("x_in", [P, 4, P], at=ARENA)
    o = ARENA + 69632
    mraw = place("mraw", [P, 2, KC, 256], at=o); o += 16384
    macc = place("macc", [P, 6, 256], at=o); o += 6144
    assert o <= arena_end

    branch = place("branch", [P, TB, D], at=ACTS)
    branch_low = place("branch_low", [P, TB, D], at=ARENA)
    normed = place("normed", [P, TB, D], at=ARENA)
    modulated = place("modulated", [P, 2, SEQ], at=ARENA + 81920)
    gate_diag = place("gate_diag", [P, KC, P], at=ARENA + 20480)

    o = ARENA
    gate_z = place("gate_z", [P, TB, DI], at=o); o += 32768
    yh = place("yh", [P, DI // P, SEQ], F32R, at=o)
    yl = place("yl", [P, DI // P, SEQ], F32R, at=ACTS)
    tok = place("tok", [P, TB, DI + 512], at=o); o += 40960
    bct = place("bct", [P, 8, SEQ], at=o); o += 16384
    conv4 = place("conv4", [P, 4, SEQ], at=ARENA)
    state = place("state", [P, 512], at=o); o += 2048
    cbm = place("cbm", [P, 6 * P], at=o); o += 3072
    assert o <= arena_end, (o, arena_end)
    o = ACTS
    bst = place("bst", [P, SEQ], at=o); o += 2048
    cst = place("cst", [P, SEQ], at=o); o += 2048
    btk = place("btk", [P, 2, P], at=o); o += 1024
    xdt = place("xdt", [P, TB, 512], at=o); o += 8192
    xdt_tail = place("xdt_tail", [P, 2, 512], at=o); o += 4096
    decay = place("decay", [P, 2, 6 * P], at=o); o += 6144
    dx = place("dx", [P, TB, 512], at=o); o += 8192
    assert o <= ACTS + 32768
    wdt = place("wdt", [P, KC, SSM_H], at=WIDE + 8192 - 1024)
    o = WIDE
    dt = place("dt", [P, TB, SSM_H], at=o); o += 512
    dt_e = place("dt_e", [P, TB, SSM_H], at=o); o += 512
    dta = place("dta", [P, TB, SSM_H], at=o); o += 512
    acs = place("acs", [P, TB, SSM_H], at=o); o += 512
    eacs = place("eacs", [P, TB, SSM_H], at=o); o += 512
    tail = place("tail", [P, 2, SSM_H], at=o); o += 256
    heads = place("heads", [P, 3, SSM_H], at=o); o += 384
    dtag = place("dtag", [P, TB, HPG], at=o); o += 128
    acsg = place("acsg", [P, TB, HPG], at=o); o += 128
    gstats = place("gstats", [P, TB, SSM_G, 6], at=o); o += 384
    gmv = place("gmv", [P, TB * SSM_G, 2], at=o); o += 128
    ginv = place("ginv", [P, TB * SSM_G], at=o); o += 64
    assert o <= WIDE + 8192 - 1024

    o = ARENA
    mem_t = place("mem_t", [P, MB, D], at=o); o += 8192
    memh = place("memh", [P, KC, MEM], F32R, at=o); o += 8192
    meml = place("meml", [P, KC, MEM], F32R, at=o); o += 8192
    kx = place("kx", [P, KC, MEM], at=o); o += 8192
    vx = place("vx", [P, MB, D], at=o); o += 8192
    qx = place("qx", [P, KC, SEQ], at=o); o += 16384
    px = place("px", [P, 2, TB, MEM], at=o); o += 8192
    pxt = place("pxt", [P, MB, SEQ], at=o); o += 4096

    o = ARENA
    oacc = place("oacc", [P, TB, D], at=o); o += 16384
    kv8 = place("kv8", [P, 8, SEQ], at=o)
    q_r = place("q_r", [P, KC, SEQ], at=o); o += 16384
    kdup = place("kdup", [P, 2 * KV, SEQ], at=o); o += 16384
    v_sw = place("v_sw", [P, TB, 2 * KV * HD], at=o); o += 8192
    kcp = place("kcp", [P, 2, 16, KV * N_CMP], at=o)
    q_u = place("q_u", [P, KC, SEQ], at=o); o += 16384
    rot_t = place("rot_t", [P, 2, 2, SEQ], at=o)
    pc = place("pc", [P, TB, QG, CMP], at=o)
    pct = place("pct", [P, SEQ], at=o + 2048); o += 8192 + 4096
    select = place("select", [P, 5, P], at=o); o += 2560
    hid_k = place("hid_k", [P, 2, KV, CMP], at=o); o += 1024
    w2k = place("w2k", [P, 2, 2, HD], at=o); o += 1024
    w2v = place("w2v", [P, 2, HD], at=o); o += 512
    kcmp = place("kcmp", [P, KV, CMP], at=o); o += 512
    hid_v = place("hid_v", [P, 2, KV, QG, CMP], at=o)
    vbd = place("vbd", [P, KV, QG * HD], at=o); o += 4096
    gates = place("gates", [P, TB, 48], at=o); o += 768
    nst = place("nst", [P, 2, 4, TB], at=o); o += 128
    assert o <= arena_end, (o, arena_end)
    kcph = place("kcph", [P, 2, 16, KV * N_CMP], F32R, at=ACTS)
    kcpl = place("kcpl", [P, 2, 16, KV * N_CMP], F32R, at=ACTS + 16384)
    rotary = place("rotary", [P, 2, SEQ], at=WIDE)
    w_gate = place("w_gate", [P, KC, 48], at=WIDE + 4096)
    cmp_mask = place("cmp_mask", [P, TB * CMP + QG], at=WIDE + 6144)
    cst2 = place("cst2", [P, 4, TB * QG], at=WIDE + 7168)
    o = ACTS
    k_g = place("k_g", [P, 2, SEQ], at=o); o += 4096
    qr_g = place("qr_g", [P, 2, SEQ], at=o); o += 4096
    qu_g = place("qu_g", [P, 2, SEQ], at=o); o += 4096
    v_g = place("v_g", [P, 2, TB, HD], at=o); o += 2048
    kc_g = place("kc_g", [P, CMP], at=o); o += 128
    vb_g = place("vb_g", [P, QG * HD], at=o); o += 1024
    gate_g = place("gate_g", [P, TB, QG, 3], at=o); o += 192
    pn = place("pn", [P, 2, CAUSAL], at=o); o += 2 * CAUSAL * 4
    pnt = place("pnt", [P, CAUSAL], at=o); o += CAUSAL * 4
    assert o <= ACTS + 32768
    T_STRIPS = {3: (0, 0, 0), 2: (1, 0, 512), 0: (1, 384, 896), 1: (2, 0, 1024)}

    ps = ctx.enter_context(nc.psum_tensor("ps", [P, 8, 512], F32))

    raw_full = [sem("raw_full0"), sem("raw_full1")]
    hi_ready = sem("hi_ready")
    unit_ready = sem("unit_ready")
    marks = sem("marks")
    bank_free = sem("bank_free")
    params = sem("params")
    mem_in = sem("mem_in")
    x_loaded = sem("x_loaded")
    gb_in = sem("gb_in")
    turned = sem("turned")
    turned_hi = sem("turned_hi")
    turned_free = sem("turned_free")
    set_up = sem("set_up")
    dve_step = sem("dve_step")
    act_step = sem("act_step")
    h_sum = sem("h_sum")
    moments = sem("moments")
    rstd_ready = sem("rstd_ready")
    h_ready = sem("h_ready")
    evac_hi = sem("evac_hi")
    staged = sem("staged")
    z_ready = sem("z_ready")
    capped = sem("capped")
    log_ready = sem("log_ready")
    sp_ready = sem("sp_ready")
    logw_ready = sem("logw_ready")
    w_ready = sem("w_ready")
    o_ready = sem("o_ready")
    o_free = sem("o_free")
    mod_raw = [sem("mod_raw0"), sem("mod_raw1")]
    mod_acc = sem("mod_acc")
    mod_step = sem("mod_step")
    mod_cols = sem("mod_cols")
    mod_done = sem("mod_done")
    c_ready = sem("c_ready")
    diag_ready = sem("diag_ready")
    gate_rows = sem("gate_rows")
    gate_ready = sem("gate_ready")
    branch_out = sem("branch_out")
    normed_ready = sem("normed_ready")
    convolved = sem("convolved")
    tok_turned = sem("tok_turned")
    tok_free = sem("tok_free")
    bc_copied = sem("bc_copied")
    wdt_in = sem("wdt_in")
    dt_raw = sem("dt_raw")
    dt_cap = sem("dt_cap")
    dt_log = sem("dt_log")
    dta_ready = sem("dta_ready")
    acs_ready = sem("acs_ready")
    acs_out = sem("acs_out")
    tail_ready = sem("tail_ready")
    group_in = sem("group_in")
    xdt_ready = sem("xdt_ready")
    cb_ready = sem("cb_ready")
    cb_out = sem("cb_out")
    acs_rows = sem("acs_rows")
    decay_arg = sem("decay_arg")
    decay_exp = sem("decay_exp")
    mixed = sem("mixed")
    head_y = sem("head_y")
    group_y = sem("group_y")
    heads_in = sem("heads_in")
    a_ready = sem("a_ready")
    dx_ready = sem("dx_ready")
    pool_step = sem("pool_step")
    out_done = sem("out_done")

    nsa_in = sem("nsa_in")
    dup_ready = sem("dup_ready")
    dup_free = sem("dup_free")
    hid_padded = sem("hid_padded")
    blocks_hi = sem("blocks_hi")
    blocks_lo = sem("blocks_lo")
    rot_in = sem("rot_in")
    rot_ready = sem("rot_ready")
    rot_free = sem("rot_free")
    cmp_ready = sem("cmp_ready")
    cmp_kept = sem("cmp_kept")
    gates_raw = sem("gates_raw")
    gates_ready = sem("gates_ready")
    key_head_in = sem("key_head_in")
    c_scores = sem("c_scores")
    c_args = sem("c_args")
    c_exps = sem("c_exps")
    c_probs = sem("c_probs")
    c_turned = sem("c_turned")
    c_copied = sem("c_copied")
    c_outs = sem("c_outs")
    c_taken = sem("c_taken")
    n_scores = sem("n_scores")
    n_max = sem("n_max")
    n_exps = sem("n_exps")
    n_turned = sem("n_turned")
    n_copied_s = sem("n_copied_s")
    n_copied_v = sem("n_copied_v")
    n_outs = sem("n_outs")
    n_taken = sem("n_taken")

    scores = sem("scores")
    score_max = sem("score_max")
    probs = sem("probs")
    probs_normed = sem("probs_normed")
    probs_turned = sem("probs_turned")
    probs_copied = sem("probs_copied")
    heads_out = sem("heads_out")
    heads_free = sem("heads_free")
    taps = sem("taps")
    conv_done = sem("conv_done")
    gated = sem("gated")
    hid_value = sem("hid_value")
    hid_ready = sem("hid_ready")

    C_CW = 0
    C_PRE_MIX, C_PRE_FFN, C_KVN = 88, 104, 120
    C_CW2, C_CB = 128, 172
    C_SCB, C_SNORM = 216, 240
    C_SCW, C_C = 256, 352
    C_MODB = 384
    C_POS = (496, 360)

    def feature_units(w, c0):
        v = w.rearrange("(k p) c -> p k c", p=P)
        return lambda i: v[:, :, bass.ds(c0 + 256 * i, 256)]

    def token_units(w, c0, k0, nk):
        v = w.rearrange("(k p) c -> p k c", p=P)
        return lambda i: v[:, k0:k0 + nk, bass.ds(c0 + 512 * i, 512)]

    def strip(sb):
        bank, c0 = [(0, 0), (1, 0), (2, 0), (1, 384)][sb]
        return bank, c0, [0, 512, 896, 1152][sb], SEQ - P * sb

    engines = ExitStack()
    block = engines.enter_context(nc.Block())


    @block.sync
    def _(sp_q):
        turns = Turns()
        parity = [0]

        def load(source, n=2048):
            slot = parity[0] % 2
            parity[0] += 1
            sp_q.wait_ge(unit_ready, turns(unit_ready))
            k = source.shape[1]
            sp_q.dma_start(raw[:, slot, 0:n].rearrange("p (k c) -> p k c", k=k), source) \
                .then_inc(raw_full[slot], 16)

        def feature_loads(pairs, w, c0):
            with turns.loop(sp_q, pairs, {unit_ready: 2}) as i:
                for u in range(2):
                    load(feature_units(w, c0)(2 * i + u))

        def token_loads(halves, w, c0, kc=KC):
            units = -(-kc // 4)
            with turns.loop(sp_q, halves, {unit_ready: units}) as i:
                for u in range(units):
                    nk = min(4, kc - 4 * u)
                    load(token_units(w, c0, 4 * u, nk)(i), n=nk * 512)

        def ffn_loads(w_up, w_down):
            with turns.loop(sp_q, FC // 2, {unit_ready: 2}) as i:
                load(feature_units(w_up, 0)(i))
                load(feature_units(w_up, DFF)(i))
            token_loads(2, w_down, 0, FC)

        def ffn2_loads(layer):
            ffn_loads(a["ffn_w_in_2"][layer], a["ffn_w_out_2"][layer])

        def program():
            feature_loads(4, a["sb_win"][0], 0)
            token_loads(2, a["sb_win"][0], 2 * D)
            feature_loads(2, a["xa_wkv"][0], 0)
            token_loads(2, a["xa_wkv"][0], D)
            token_loads(2, a["mix_wo"][0], 0)
            feature_loads(2, a["xa_wq"][0], 0)
            token_loads(2, a["xa_wo"][0], 0)
            ffn_loads(a["ffn_up"][0], a["ffn_down"][0])
            ssm_w = a["ssm_w_in_2"][0]
            feature_loads(4, ssm_w, DI)
            feature_loads(1, ssm_w, 2 * DI)
            feature_loads(1, ssm_w, 2 * DI + 512)
            token_loads(4, ssm_w, 0)
            token_loads(2, a["ssm_w_out_2"][0], 0, DI // P)
            ffn2_loads(0)
            w_kv = a["w_kv_2"].rearrange("(k p) c -> p k c", p=P)
            with turns.loop(sp_q, 2, {unit_ready: 2}) as i:
                load(w_kv[:, :, bass.ds(512 * i, 256)])
                load(w_kv[:, :, bass.ds(768 * i + 256, 256)])
            load(w_kv[:, :, 768:1024])
            load(w_kv[:, :, 1280:1536])
            for w1 in (a["cmp_w1_k_2"], a["cmp_w1_v_2"]):
                for u in range(2):
                    load(w1.rearrange("(k p) c -> p k c", p=P)[:, KC * u:KC * u + KC, :])
            feature_loads(2, a["nsa_w_q_2"][0], 0)
            token_loads(2, a["nsa_w_o_2"][0], 0)
            ffn2_loads(1)
        program()
        sp_q.wait_ge(h_ready, 7 * TB)
        sp_q.dma_start(out.rearrange("a (t p) c -> p (a t) c", p=P), h[:]).then_inc(out_done, 16)
        sp_q.wait_ge(out_done, 16)

    @block.tensor
    def _(pe):
        turns = Turns()

        def product3(o, lh, ll, rh, rl, start, stop):
            nc.tensor.matmul(o, ll, rh, start=start, stop=False, skip_group_check=True)
            nc.tensor.matmul(o, lh, rl, start=False, stop=False, skip_group_check=True)
            return nc.tensor.matmul(o, lh, rh, start=False, stop=stop, skip_group_check=True)

        def banks_out(free=bank_free):
            pe.wait_ge(free, turns.seen.get(free.name, 0) + FREE0)

        mods_behind = [0]

        def turns_out():
            if mods_behind[0]:
                pe.wait_ge(mod_done, turns(mod_done, mods_behind[0]))
                mods_behind[0] = 0
            pe.wait_ge(turned_free, turns.seen.get("turned_free", 0) + 4)

        def feature_pairs(pairs, ah, al, n=SEQ, free=bank_free, mods=0, after=None, extra={}):
            banks_out()
            with turns.loop(pe, pairs, {unit_ready: 2, free: 4, mod_acc: mods} | extra):
                for u in range(2):
                    pe.wait_ge(unit_ready, SLOTS + turns(unit_ready))
                    wh = whi[:, u, :].rearrange("p (k c) -> p k c", k=KC)
                    wl = wlo[:, u, :].rearrange("p (k c) -> p k c", k=KC)
                    for j in range(2):
                        pe.wait_ge(free, turns(free))
                        for k in range(KC):
                            c = slice(P * j, P * j + P)
                            last = product3(ps[:, 2 * u + j, 0:n], wh[:, k, c], wl[:, k, c], ah[:, k, 0:n],
                                            al[:, k, 0:n], k == 0, k == KC - 1)
                        last.then_inc(marks, 1)
                if mods:
                    mod_columns(mods)
                if after:
                    after()
            mods_behind[0] += pairs if mods else 0
            if free is not bank_free:
                banks_out(free)

        def token_half(ah, al, kc, nt, free):
            units = -(-kc // 4)
            for u in range(units):
                pe.wait_ge(unit_ready, SLOTS + turns(unit_ready))
                wh = whi[:, u % 2, :].rearrange("p (k c) -> p k c", c=512)
                wl = wlo[:, u % 2, :].rearrange("p (k c) -> p k c", c=512)
                nk = min(4, kc - 4 * u)
                for t in range(nt):
                    if u == 0:
                        pe.wait_ge(free, turns(free) + FREE0 - nt)
                    c = slice(P * t, P * t + P)
                    for k in range(nk):
                        final = u == units - 1 and k == nk - 1
                        last = product3(ps[:, t, :], ah[:, 4 * u + k, c], al[:, 4 * u + k, c], wh[:, k, :],
                                        wl[:, k, :], u == 0 and k == 0, final)
                    if u == units - 1:
                        last.then_inc(marks, 1)
                if u < units - 1:
                    last.then_inc(marks, 1)

        def token_pairs(halves, ah, al, kc=KC, nt=TB, mods=0, free=bank_free):
            banks_out()
            with turns.loop(pe, halves, {unit_ready: -(-kc // 4), free: nt, mod_acc: mods}):
                token_half(ah, al, kc, nt, free)
                if mods:
                    mod_columns(mods)
            mods_behind[0] += halves if mods else 0
            if free is not bank_free:
                banks_out(free)

        def mod_columns(units):
            for u in range(units):
                pe.wait_ge(mod_acc, MODS + turns(mod_acc))
                for j in range(2):
                    last = nc.tensor.matmul(ps[:, 6, 2 * u + j:2 * u + j + 1], macc[:, u, P * j:P * j + P], ones_c[:],
                                            start=True, stop=True, skip_group_check=True)
            last.then_inc(mod_cols, 1)

        def to_features(src, blocks=TB, chunks=KC):
            for c in range(chunks):
                pe.wait_ge(turned_free, turns(turned_free))
                for t in range(blocks):
                    last = nc.tensor.transpose(ps[:, 4 + c % 4, P * t:P * t + P], src[:, t, P * c:P * c + P], ident[:])
                last.then_inc(turned, 1)

        def stick_breaking():
            banks_out()
            turns_out()
            with turns.loop(pe, 4, {staged: 6, w_ready: 12, sp_ready: 4, o_free: 2}):
                for pair in range(2):
                    pe.wait_ge(staged, turns(staged, 3))
                    for hd in range(2):
                        half = slice(64 * hd, 64 * hd + 64)
                        for sb in (0, 1, 3, 2):
                            bank, c0, _, n = strip(sb)
                            nc.tensor.matmul(ps[:, 3 * hd + bank, c0:c0 + n], kst[half, pair, P * sb:P * sb + P],
                                             qst[half, pair, P * sb:SEQ], start=sb != 3, stop=False,
                                             skip_group_check=True)
                            last = nc.tensor.matmul(ps[:, 3 * hd + bank, c0:c0 + P], ident_b[:], strict_b[:],
                                                    start=False, stop=False, skip_group_check=True)
                            if sb != 1:
                                last.then_inc(z_ready, 1)
                    for hd in range(2):
                        pe.wait_ge(sp_ready, turns(sp_ready))
                        for sb in (2, 3, 1, 0):
                            bank, c0, _, n = strip(sb)
                            for j in range(sb, TB):
                                _, _, offj, nj = strip(j)
                                last = nc.tensor.matmul(ps[:, 3 * hd + bank, c0 + n - nj:c0 + n],
                                                        (neg_suffix if j == sb else neg_ones)[:],
                                                        sp[:, hd, offj:offj + nj],
                                                        start=False, stop=j == TB - 1, skip_group_check=True)
                            if sb != 3:
                                last.then_inc(logw_ready, 1)
                    pe.wait_ge(o_free, turns(o_free))
                    for hd in range(2):
                        half = slice(64 * hd, 64 * hd + 64)
                        pe.wait_ge(w_ready, turns(w_ready, 3))
                        for sb in range(TB):
                            _, _, off, n = strip(sb)
                            last = nc.tensor.matmul(ps[half, 6 + pair, P * sb:SEQ], vst[:, pair, sb, half],
                                                    wts[:, hd, off:off + n], start=sb == 0, stop=sb == TB - 1,
                                                    skip_group_check=True)
                    last.then_inc(o_ready, 1)
            pe.wait_ge(o_free, turns.seen["o_free"] + 2)

        def cross_attention():
            banks_out()
            turns_out()

            def head_scores(hd):
                for t in range(TB):
                    bank = 2 * (hd % 2) + t // 2
                    if t % 2 == 0 and hd >= 2:
                        pe.wait_ge(probs, 4 * (hd - 1))
                    for c in range(2):
                        last = nc.tensor.matmul(ps[:, bank, MEM * (t % 2):MEM * (t % 2) + MEM],
                                                qx[:, 2 * hd + c, P * t:P * t + P], kx[:, 2 * hd + c, :],
                                                start=t % 2 == 0 and c == 0, stop=c == 1, skip_group_check=True)
                    if t % 2:
                        last.then_inc(scores, 1)

            head_scores(0)
            for hd in range(XA_HEADS):
                if hd + 1 < XA_HEADS:
                    head_scores(hd + 1)
                pe.wait_ge(probs_normed, hd + 1)
                if hd:
                    pe.wait_ge(probs_copied, 2 * hd)
                for m in range(MB):
                    for t in range(TB):
                        last = nc.tensor.transpose(ps[:, 4 + m, P * t:P * t + P], px[:, hd % 2, t, P * m:P * m + P],
                                                   ident[:])
                    last.then_inc(probs_turned, 1)
                for c in range(2):
                    pe.wait_ge(probs_copied, 2 * hd + 2)
                    if hd:
                        pe.wait_ge(heads_free, 2 * hd - 1 + c)
                    for m in range(MB):
                        last = nc.tensor.matmul(ps[:, 6 + c, :], vx[:, m, 256 * hd + P * c:256 * hd + P * c + P],
                                                pxt[:, m, :], start=m == 0, stop=m == MB - 1)
                    last.then_inc(heads_out, 1)
            pe.wait_ge(heads_free, 8)

        def gate_rows_of():
            pe.wait_ge(diag_ready, turns(diag_ready))
            for half in range(2):
                last = nc.tensor.matmul(ps[:, 4 + half, :], causal6[:, P:2 * P],
                                        gate_diag[:, 4 * half:4 * half + 4, :], start=True, stop=True)
            last.then_inc(gate_rows, 1)

        def normed_to_features():
            pe.wait_ge(normed_ready, turns(normed_ready, TB))
            turns_out()
            to_features(normed)
            turns_out()

        def gated_ffn():
            banks_out()
            with turns.loop(pe, FC // 2, {unit_ready: 2, hid_value: 2}):
                for u in range(2):
                    pe.wait_ge(unit_ready, SLOTS + turns(unit_ready))
                    wh = whi[:, u, :].rearrange("p (k c) -> p k c", k=KC)
                    wl = wlo[:, u, :].rearrange("p (k c) -> p k c", k=KC)
                    for j in range(2):
                        if u == 0:
                            pe.wait_ge(hid_value, turns(hid_value) - 2 + HID0)
                        for k in range(KC):
                            c = slice(P * j, P * j + P)
                            last = product3(ps[:, 2 * u + j, :], wh[:, k, c], wl[:, k, c], acth[:, k, :],
                                            actl[:, k, :], k == 0, k == KC - 1)
                        last.then_inc(marks, 1)
            pe.wait_ge(hid_ready, turns(hid_ready, FC))
            token_pairs(2, hid_h, hid_l, FC, free=branch_out)
            gate_rows_of()

        def value_units():
            for u in range(2):
                pe.wait_ge(unit_ready, SLOTS + turns(unit_ready))
                wh = whi[:, u, :].rearrange("p (k c) -> p k c", k=KC)
                wl = wlo[:, u, :].rearrange("p (k c) -> p k c", k=KC)
                for t in range(TB):
                    if u == 0:
                        pe.wait_ge(bank_free, turns(bank_free))
                    c = slice(P * t, P * t + P)
                    for k in range(KC):
                        last = product3(ps[:, t, 256 * u:256 * u + 256], acth[:, k, c], actl[:, k, c], wh[:, k, :],
                                        wl[:, k, :], u == 0 and k == 0, k == KC - 1)
                    if u == 1 or t == TB - 1:
                        last.then_inc(marks, 1)

        rotated = [0]

        def rotate(chunks, mats):
            for c in range(chunks):
                pe.wait_ge(rot_in, turns(rot_in, 2))
                for keep, move in mats:
                    if rotated[0] >= 4:
                        pe.wait_ge(rot_free, rotated[0] - 3)
                    o = ps[:, 4 + rotated[0] % 4, :]
                    nc.tensor.matmul(o, keep, rot_t[:, c % 2, 0, :], start=True, stop=False)
                    nc.tensor.matmul(o, move, rot_t[:, c % 2, 1, :], start=False, stop=True).then_inc(rot_ready, 1)
                    rotated[0] += 1

        def compression():
            for n in range(2 * KV):
                if n >= 4:
                    pe.wait_ge(dup_free, n - 3)
                nc.tensor.matmul(ps[:, 4 + n % 4, :], select[:, n % 2, :], kv8[:, n // 2, :], start=True, stop=True) \
                    .then_inc(dup_ready, 1)
            pe.wait_ge(dup_free, 2 * KV)
            rotate(4, [(select[:, half, :], select[:, 2 + half, :]) for half in range(2)])
            banks_out()
            for w in range(2):
                pe.wait_ge(blocks_lo, w + 1)
                for u in range(2):
                    pe.wait_ge(unit_ready, SLOTS + turns(unit_ready))
                    wh = whi[:, u, :].rearrange("p (k c) -> p k c", k=KC)
                    wl = wlo[:, u, :].rearrange("p (k c) -> p k c", k=KC)
                    for j in range(2):
                        for k in range(KC):
                            c = slice(P * j, P * j + P)
                            last = product3(ps[:, 2 * w + j, 0:KV * N_CMP], wh[:, k, c], wl[:, k, c],
                                            kcph[:, w, KC * u + k, :], kcpl[:, w, KC * u + k, :],
                                            u == 0 and k == 0, u == 1 and k == KC - 1)
                        if u == 1 or j == 1:
                            last.then_inc(marks, 1)
            turns(bank_free, 4)
            banks_out()
            pe.wait_ge(rot_free, rotated[0])
            for c in range(2):
                nc.tensor.matmul(ps[:, 4, 0:P], w2k[:, c, :, :], hid_k[:, c, :, :], start=c == 0, stop=c == 1)
            for g in range(KV):
                for c in range(2):
                    last = nc.tensor.matmul(ps[:, 5, HD * g:HD * g + HD],
                                            hid_v[:, c, g, :, :], w2v[:, c, :],
                                            start=g == 0 and c == 0, stop=c == 1, skip_group_check=True)
            last.then_inc(cmp_ready, 1)
            pe.wait_ge(cmp_kept, 1)

        def branch_gates():
            for t in range(TB):
                for k in range(KC):
                    for n, part in enumerate((acth, actl)):
                        last = nc.tensor.matmul(ps[:, 4, 48 * t:48 * t + 48],
                                                part[:, k, P * t:P * t + P].bitcast(F32), w_gate[:, k, :],
                                                start=k == 0 and n == 0, stop=k == KC - 1 and n == 1,
                                                skip_group_check=True)
            last.then_inc(gates_raw, 1)
            pe.wait_ge(gates_ready, 1)

        def nsa_attention():
            def job_scores(n):
                hd, w, slot = n // 2, n % 2, 3 * (n % 2)
                half = slice(HD * (hd % 2), HD * (hd % 2) + HD)
                for tb, (bank, c0, _) in T_STRIPS.items():
                    o = ps[:, slot + bank, c0:c0 + P * tb + P]
                    nc.tensor.matmul(o, qr_g[half, hd // 2, P * tb:P * tb + P], k_g[half, w, 0:P * tb + P],
                                     start=tb != 0, stop=False, skip_group_check=True)
                    last = nc.tensor.matmul(ps[:, slot + bank, c0 + P * tb:c0 + P * tb + P], ident_b[:], causal_b[:],
                                            start=False, stop=True, skip_group_check=True)
                    if tb != 2:
                        last.then_inc(n_scores, 1)

            with turns.loop(pe, KV, {key_head_in: 9, c_probs: 1, c_copied: 1, c_taken: 1, n_exps: 32, n_taken: 8,
                                     n_copied_s: 8, n_copied_v: 16}):
                pe.wait_ge(key_head_in, turns(key_head_in, 9))
                for side in range(2):
                    half = slice(HD * side, HD * side + HD)
                    for tb in range(TB):
                        for pair in range(2):
                            c0 = CMP * (2 * tb + pair)
                            last = nc.tensor.matmul(ps[:, 6 + side, c0:c0 + CMP],
                                                    qu_g[half, pair, P * tb:P * tb + P], kc_g[half, :],
                                                    start=tb == 0 and pair == 0, stop=True, skip_group_check=True)
                    last.then_inc(c_scores, 1)
                job_scores(0)
                pe.wait_ge(c_probs, turns(c_probs))
                for tb in range(TB):
                    last = nc.tensor.transpose(ps[:, 6, P * tb:P * tb + P], pc[:, tb, :, :], ident[:])
                last.then_inc(c_turned, 1)
                pe.wait_ge(c_copied, turns(c_copied))
                for tb in range(TB):
                    last = nc.tensor.matmul(ps[:, 3 + tb // 2, 256 * (tb % 2):256 * (tb % 2) + 256],
                                            pct[:, P * tb:P * tb + P], vb_g[:], start=tb % 2 == 0, stop=True,
                                            skip_group_check=True)
                last.then_inc(c_outs, 1)
                pe.wait_ge(c_taken, turns(c_taken))
                for n in range(2 * QG):
                    if n + 1 < 2 * QG:
                        if n:
                            pe.wait_ge(n_taken, DONE0 + turns(n_taken))
                        job_scores(n + 1)
                    for r, blocks in enumerate(((0, 1, 2, 3), (4, 5, 6, 7), (8, 9))):
                        pe.wait_ge(n_exps, turns(n_exps, (1, 2, 1)[r]))
                        if r == 2:
                            pe.wait_ge(n_copied_s, turns(n_copied_s))
                        for b, block in enumerate(blocks):
                            last = nc.tensor.transpose(ps[:, 6 + (3 * n + r) % 2, P * b:P * b + P],
                                                       pn[:, n % 2, P * block:P * block + P], ident[:])
                        last.then_inc(n_turned, 1)
                    pe.wait_ge(n_copied_v, turns(n_copied_v, 2))
                    for tb in range(TB):
                        off = T_STRIPS[tb][2]
                        for sb in range(tb + 1):
                            last = nc.tensor.matmul(ps[:, 3 * (n % 2) + 2, 256 + HD * tb:256 + HD * tb + HD],
                                                    pnt[:, off + P * sb:off + P * sb + P], v_g[:, n % 2, sb, :],
                                                    start=tb == 0 and sb == 0, stop=sb == tb, skip_group_check=True)
                    last.then_inc(n_outs, 1)
                turns(n_taken, 2)
            pe.wait_ge(n_taken, DONE0 + turns.seen["n_taken"])

        def turn_chunks():
            for j in range(4):
                pe.wait_ge(convolved, turns(convolved))
                pe.wait_ge(tok_free, turns(tok_free))
                for t in range(TB):
                    last = nc.tensor.transpose(ps[:, 4 + j, P * t:P * t + P], conv4[:, j, P * t:P * t + P], ident[:])
                last.then_inc(tok_turned, 1)

        def dt_and_sums():
            pe.wait_ge(wdt_in, 16)
            pe.wait_ge(tok_free, turns.seen["tok_free"] + 4)
            for t in range(TB):
                for k in range(KC):
                    for n, part in enumerate((acth, actl)):
                        last = nc.tensor.matmul(ps[:, 4, SSM_H * t:SSM_H * t + SSM_H],
                                                part[:, k, P * t:P * t + P].bitcast(F32), wdt[:, k, :],
                                                start=k == 0 and n == 0, stop=k == KC - 1 and n == 1,
                                                skip_group_check=True)
            last.then_inc(dt_raw, 1)
            pe.wait_ge(dta_ready, 1)
            upper, ones = causal6[:, 0:P], causal6[:, P:2 * P]
            for t in range(TB):
                o = ps[:, 5, SSM_H * t:SSM_H * t + SSM_H]
                if t % 2:
                    nc.tensor.matmul(o, ones, dta[:, t - 1, :], start=True, stop=False, skip_group_check=True)
                nc.tensor.matmul(o, upper, dta[:, t, :], start=t % 2 == 0, stop=True, skip_group_check=True)
            for t in range(2):
                last = nc.tensor.matmul(ps[:, 5, P:P + SSM_H], ones, dta[:, t, :], start=t == 0, stop=t == 1,
                                        skip_group_check=True)
            last.then_inc(acs_ready, 1)

        def scan():
            segs = [(0, 0, 256), (1, 256, 128), (2, 384, 256), (3, 640, 128)]

            def sum_rows(hd):
                bank = 6 + hd % 2
                for ch in range(2):
                    for b in range(2):
                        last = nc.tensor.matmul(ps[:, bank, 256 * ch + P * b:256 * ch + 256],
                                                dtag[:, 2 * ch + b, hd:hd + 1].to_broadcast([P, P]),
                                                causal6[:, 0:256 - P * b], start=ch == 0 and b == 0, stop=b == 1,
                                                skip_group_check=True)
                last.then_inc(acs_rows, 1)

            pe.wait_ge(acs_out, 1)
            with turns.loop(pe, SSM_G, {group_in: 5, xdt_ready: 1, cb_out: 1, decay_arg: 8, mixed: 8, group_y: 1}):
                pe.wait_ge(group_in, turns(group_in, 5))
                pe.wait_ge(group_y, turns(group_y) - 1 + DONE0)
                for ch in range(2):
                    for b in range(2):
                        nc.tensor.matmul(ps[:, 6 + ch, 256 * b:256 * b + 256 - P * b],
                                         bst[:, 256 * ch + P * b:256 * ch + P * b + P],
                                         cst[:, 256 * ch + P * b:256 * ch + 256], start=b == 0, stop=True,
                                         skip_group_check=True)
                pe.wait_ge(xdt_ready, turns(xdt_ready))
                for t in range(2):
                    last = nc.tensor.matmul(ps[:, 5, :], btk[:, t, :], xdt_tail[:, t, :], start=t == 0, stop=t == 1)
                last.then_inc(cb_ready, 1)
                pe.wait_ge(cb_out, turns(cb_out))
                for t in range(2):
                    nc.tensor.matmul(ps[:, 4 + t, :], cst[:, 256 + P * t:384 + P * t], state[:], start=True, stop=True)
                sum_rows(0)
                sum_rows(1)
                for hd in range(HPG):
                    pe.wait_ge(mixed, turns(mixed))
                    w = decay[:, hd % 2, :]
                    for t in range(TB):
                        for b in range(t % 2 + 1):
                            key, off, _ = segs[t - t % 2 + b]
                            q0 = off + (P * (t % 2) if b == 0 else 0)
                            last = nc.tensor.matmul(ps[:, t, 64 * hd:64 * hd + 64], w[:, q0:q0 + P],
                                                    xdt[:, key, 64 * hd:64 * hd + 64],
                                                    start=hd == 0 and b == 0, stop=b == t % 2,
                                                    skip_group_check=True)
                    last.then_inc(head_y, 1)
                    if hd + 2 < HPG:
                        pe.wait_ge(decay_arg, turns(decay_arg))
                        sum_rows(hd + 2)
                turns(decay_arg, 2)

        pe.wait_ge(x_loaded, 16)
        pe.wait_ge(params, 16 * N_PARAMS)
        to_features(h)
        pe.wait_ge(turned_free, turns(turned_free))
        for t in range(4):
            last = nc.tensor.transpose(ps[:, 4, P * t:P * t + P], x_in[:, t, :], ident[:])
        last.then_inc(turned, 1)
        turns_out()
        pe.wait_ge(set_up, SET_UP)
        feature_pairs(4, acth, actl, mods=6)
        token_pairs(2, acth, actl, mods=4)
        turns_out()
        stick_breaking()
        pe.wait_ge(mem_in, 16)
        to_features(mem_t, MB)
        turns_out()
        feature_pairs(2, memh, meml, MEM, mods=2)
        token_pairs(2, memh, meml, nt=MB, mods=2)
        token_pairs(2, acth, actl, mods=4)
        turns_out()
        pe.wait_ge(h_ready, turns(h_ready, TB))
        to_features(h)
        turns_out()
        feature_pairs(2, acth, actl, mods=4)
        cross_attention()
        token_pairs(2, acth, actl)
        pe.wait_ge(h_ready, turns(h_ready, TB))
        to_features(h)
        turns_out()
        feature_pairs(FC // 2, acth, actl, free=conv_done)
        pe.wait_ge(hid_ready, turns(hid_ready, FC))
        token_pairs(2, hid_h, hid_l, FC)
        pe.wait_ge(h_ready, turns(h_ready, TB))
        normed_to_features()
        tok_steps = {convolved: 4, tok_free: 4}
        feature_pairs(4, acth, actl, free=conv_done, after=turn_chunks, extra=tok_steps)
        feature_pairs(1, acth, actl, free=conv_done, after=turn_chunks, extra=tok_steps)
        feature_pairs(1, acth, actl, free=conv_done)
        token_pairs(4, acth, actl)
        dt_and_sums()
        banks_out()
        scan()
        pe.wait_ge(normed_ready, turns(normed_ready))
        to_features(gate_z, chunks=DI // P)
        turns_out()
        token_pairs(2, yh, yl, DI // P, free=branch_out)
        gate_rows_of()
        normed_to_features()
        gated_ffn()
        normed_to_features()
        feature_pairs(2, acth, actl)
        value_units()
        banks_out()
        pe.wait_ge(nsa_in, 16 * NSA_PARAMS)
        compression()
        to_features(normed)
        turns_out()
        feature_pairs(2, acth, actl)
        branch_gates()
        rotate(KC, [(ident[:], select[:, 4, :])])
        pe.wait_ge(rot_free, rotated[0])
        banks_out()
        nsa_attention()
        to_features(oacc)
        turns_out()
        token_pairs(2, acth, actl, free=branch_out)
        gate_rows_of()
        normed_to_features()
        gated_ffn()

    @block.scalar
    def _(act):
        turns = Turns()

        def split(slot):
            act.wait_ge(raw_full[slot], turns(raw_full[slot], 16))
            nc.scalar.activation(whi[:, slot, :], raw[:, slot, :], ACT.Copy).then_inc(hi_ready, 1)

        PAIR = {marks: 4, raw_full[0]: 16, raw_full[1]: 16}

        def feature_copies(pairs, dst, scale=1.0, n=SEQ):
            with turns.loop(act, pairs, PAIR) as i:
                for u in range(2):
                    for j in range(2):
                        act.wait_ge(marks, turns(marks))
                        nc.scalar.activation(dst[:, 4 * i + 2 * u + j, 0:n], ps[:, 2 * u + j, 0:n], ACT.Copy,
                                             scale=scale).then_inc(bank_free, 1)
                    split(u)

        def token_splits(halves, kc=KC, nt=TB):
            units = -(-kc // 4)
            with turns.loop(act, halves, {marks: units - 1 + nt, raw_full[0]: 8 * units, raw_full[1]: 8 * units}):
                for u in range(units):
                    act.wait_ge(marks, turns(marks, 1 if u < units - 1 else nt))
                    split(u % 2)

        def turned_his(dst, n=SEQ):
            for c in range(KC):
                act.wait_ge(turned, turns(turned))
                nc.scalar.activation(dst[:, c, 0:n], ps[:, 4 + c % 4, 0:n], ACT.Copy).then_inc(turned_hi, 1)
            turns(turned_free, KC)

        def modulated_his(hi, gain, shift, chunks=KC):
            for c in range(chunks):
                act.wait_ge(turned, turns(turned))
                act.wait_ge(turned_free, TURNED0 + turns(turned_free) - 2)
                nc.scalar.activation(modulated[:, c % 2, :], ps[:, 4 + c % 4, :], ACT.Identity, scale=gain(c),
                                     bias=shift(c) if shift else 0.0).then_inc(act_step, 1)
                act.wait_ge(act_step, turns(act_step))
                nc.scalar.activation(hi[:, c, :], modulated[:, c % 2, :], ACT.Copy).then_inc(turned_hi, 1)

        def load_gb(n):
            act.dma_start(gb[:, 0, :], a["ln_g"][0:1, n, :].to_broadcast([P, D])).then_inc(gb_in, 16)
            act.dma_start(gb[:, 1, :], a["ln_b"][0:1, n, :].to_broadcast([P, D])).then_inc(gb_in, 16)

        def stick_breaking():
            with turns.loop(act, 4, {capped: 4, act_step: 4, logw_ready: 12, o_ready: 2}) as i:
                for pair in range(2):
                    for hd in range(2):
                        act.wait_ge(capped, turns(capped))
                        nc.scalar.activation(sp_e[:, hd, :], sp_e[:, hd, :], ACT.Exp) \
                            .then_inc(act_step, 1)
                        act.wait_ge(act_step, turns(act_step))
                        nc.scalar.activation(sp_e[:, hd, :], sp_e[:, hd, :], ACT.Ln, bias=1.0) \
                            .then_inc(log_ready, 1)
                    for hd in range(2):
                        for strips in ((2,), (3, 1), (0,)):
                            act.wait_ge(logw_ready, turns(logw_ready))
                            for sb in strips:
                                bank, c0, off, n = strip(sb)
                                last = nc.scalar.activation(wts[:, hd, off:off + n],
                                                            ps[:, 3 * hd + bank, c0:c0 + n], ACT.Exp)
                            last.then_inc(w_ready, 1)
                    act.wait_ge(o_ready, turns(o_ready))
                    nc.scalar.activation(acth[:, 2 * i + pair, :], ps[:, 6 + pair, :], ACT.Copy).then_inc(evac_hi, 1)

        def cross_attention():
            def exps(hd):
                act.wait_ge(score_max, hd + 1)
                for t in range(TB):
                    nc.scalar.activation(px[:, hd % 2, t, :],
                                         ps[:, 2 * (hd % 2) + t // 2, MEM * (t % 2):MEM * (t % 2) + MEM], ACT.Exp,
                                         bias=small[:, 4 * (hd % 2) + t:4 * (hd % 2) + t + 1],
                                         accum_out=small[:, 8 + 4 * (hd % 2) + t:9 + 4 * (hd % 2) + t]) \
                        .then_inc(probs, 1)

            exps(0)
            for hd in range(XA_HEADS):
                if hd + 1 < XA_HEADS:
                    exps(hd + 1)
                for m in range(MB):
                    act.wait_ge(probs_turned, 2 * hd + m + 1)
                    nc.scalar.activation(pxt[:, m, :], ps[:, 4 + m, :], ACT.Copy).then_inc(probs_copied, 1)
                for c in range(2):
                    act.wait_ge(heads_out, 2 * hd + c + 1)
                    nc.scalar.activation(acth[:, 2 * hd + c, :], ps[:, 6 + c, :], ACT.Copy).then_inc(evac_hi, 1)

        def conv_ffn():
            with turns.loop(act, FC // 2, PAIR | {hid_ready: 2, conv_done: 4, hid_value: 2}) as i:
                for u in range(2):
                    for j in range(2):
                        act.wait_ge(marks, turns(marks))
                        c = FC * u + 2 * i + j
                        nc.scalar.activation(conv_t[:, 2 * u + j, :], ps[:, 2 * u + j, :], ACT.Identity,
                                             scale=cols[:, bass.ds(C_CW2 + c, 1)], bias=cols[:, bass.ds(C_CB + c, 1)]) \
                            .then_inc(taps, 1)
                    if u == 0:
                        split(0)
                for j in range(2):
                    act.wait_ge(conv_done, FREE0 + turns(conv_done))
                    nc.scalar.activation(conv_t[:, j, :], conv_t[:, j, :], ACT.Gelu_apprx_tanh).then_inc(gated, 1)
                turns(conv_done, 2)
                split(1)
                for j in range(2):
                    act.wait_ge(hid_value, HID0 + turns(hid_value))
                    nc.scalar.activation(hid_h[:, 2 * i + j, :], conv_t[:, j, :], ACT.Copy).then_inc(evac_hi, 1)
                act.wait_ge(hid_ready, turns(hid_ready, 2))

        def branch_copies(kc, last=False, branch=branch):
            units = -(-kc // 4)

            def half(i, splits=units - 1):
                for u in range(units - 1):
                    act.wait_ge(marks, turns(marks))
                    if u < splits:
                        split(u % 2)
                for t in range(TB):
                    act.wait_ge(marks, turns(marks))
                    nc.scalar.activation(branch[:, t, bass.ds(512 * i, 512)], ps[:, t, :], ACT.Copy) \
                        .then_inc(branch_out, 1)

            if not last:
                with turns.loop(act, 2, {marks: units + 3, raw_full[0]: 8 * units, raw_full[1]: 8 * units}) as i:
                    half(i)
                    split(1)
            else:
                half(0)
                split(1)
                half(1, units - 2)

        def load_gain(name, layer):
            act.dma_start(gb[:, 1, :], a[name][layer:layer + 1, :].to_broadcast([P, D])).then_inc(gb_in, 16)

        def modulation(gain, shift):
            return (lambda c: gains[:, gain, c:c + 1]), (lambda c: modv[:, shift + c:shift + c + 1])

        def gated_ffn(layer, last=False):
            with turns.loop(act, FC // 2, PAIR | {hid_ready: 2, hid_value: 2}) as i:
                for j in range(2):
                    act.wait_ge(marks, turns(marks))
                    nc.scalar.activation(conv_t[:, j, :], ps[:, j, :], ACT.Silu).then_inc(gated, 1)
                split(0)
                act.wait_ge(marks, turns(marks, 2))
                split(1)
                for j in range(2):
                    act.wait_ge(hid_value, HID0 + turns(hid_value))
                    nc.scalar.activation(hid_h[:, 2 * i + j, :], conv_t[:, j, :], ACT.Copy).then_inc(evac_hi, 1)
                act.wait_ge(hid_ready, turns(hid_ready, 2))
            load_gain("norm_post_ffn_2", layer)
            branch_copies(FC, last)

        def conv_pairs(pairs, first, to_tokens):
            with turns.loop(act, pairs, PAIR | {conv_done: 4, tok_turned: 4 * to_tokens}) as i:
                for u in range(2):
                    for j in range(2):
                        b = 2 * u + j
                        act.wait_ge(marks, turns(marks))
                        c = 4 * i + (first + b)
                        nc.scalar.activation(conv4[:, b, :], ps[:, b, :], ACT.Identity,
                                             scale=cols[:, bass.ds(C_SCW + 72 + c, 1)],
                                             bias=cols[:, bass.ds(C_SCB + c, 1)]).then_inc(taps, 1)
                    if u == 0:
                        split(0)
                for b in range(4):
                    act.wait_ge(conv_done, FREE0 + turns(conv_done))
                    nc.scalar.activation(conv4[:, b, :], conv4[:, b, :], ACT.Silu).then_inc(convolved, 1)
                split(1)
                if to_tokens:
                    for b in range(4):
                        act.wait_ge(tok_turned, turns(tok_turned))
                        c = 4 * i + (first + b)
                        nc.scalar.activation(tok[:, :, bass.ds(P * c, P)],
                                             ps[:, 4 + b, :].rearrange("p (t f) -> p t f", t=TB), ACT.Copy) \
                            .then_inc(tok_free, 1)

        def mamba():
            act.wait_ge(h_ready, 3 * TB)
            act.dma_start(wdt[:], a["ssm_w_in_2"][0].rearrange("(k p) c -> p k c", p=P)[:, :, 2 * DI + 1024:]) \
                .then_inc(wdt_in, 16)
            for n, name in enumerate(("ssm_dt_bias_2", "ssm_a_log_2", "ssm_d_2")):
                act.dma_start(heads[:, n, :], a[name].to_broadcast([P, SSM_H])).then_inc(heads_in, 16)
            modulated_his(acth, *modulation(0, 0))
            conv_pairs(4, 0, True)
            conv_pairs(1, 16, True)
            act.wait_ge(bc_copied, 4)
            conv_pairs(1, 20, False)
            act.wait_ge(bc_copied, 8)
            with turns.loop(act, 4, {marks: 5, raw_full[0]: 16, raw_full[1]: 16}) as i:
                act.wait_ge(marks, turns(marks))
                split(0)
                for t in range(TB):
                    act.wait_ge(marks, turns(marks))
                    nc.scalar.activation(gate_z[:, t, bass.ds(512 * i, 512)], ps[:, t, :], ACT.Silu) \
                        .then_inc(bank_free, 1)
                split(1)
            act.wait_ge(heads_in, 48)
            nc.scalar.activation(heads[:, 1, :], heads[:, 1, :], ACT.Exp).then_inc(a_ready, 1)
            act.wait_ge(dt_cap, 1)
            nc.scalar.activation(dt_e[:], dt_e[:], ACT.Exp).then_inc(act_step, 1)
            act.wait_ge(act_step, turns(act_step))
            nc.scalar.activation(dt_e[:], dt_e[:], ACT.Ln, bias=1.0).then_inc(dt_log, 1)
            act.wait_ge(acs_out, 1)
            nc.scalar.activation(eacs[:], acs[:], ACT.Exp)
            nc.scalar.activation(tail[:], tail[:], ACT.Exp).then_inc(tail_ready, 1)

        def scan():
            with turns.loop(act, SSM_G, {decay_arg: 8}):
                for hd in range(HPG):
                    act.wait_ge(decay_arg, turns(decay_arg))
                    nc.scalar.activation(decay[:, hd % 2, :], decay[:, hd % 2, :], ACT.Exp).then_inc(decay_exp, 1)

        def rotated_out(dst, banks):
            for b in range(banks):
                act.wait_ge(rot_ready, turns(rot_ready))
                n = turns.seen["rot_ready"] - 1
                nc.scalar.activation(dst[:, b, :], ps[:, 4 + n % 4, :], ACT.Copy).then_inc(rot_free, 1)

        def compression():
            rotated_out(kdup, 2 * KV)
            for w in range(2):
                act.wait_ge(dup_free, KV * w + KV)
                nc.scalar.activation(kcph[:, w, :, :], kcp[:, w, :, :], ACT.Copy).then_inc(blocks_hi, 1)
            act.wait_ge(hid_padded, 2)
            for w in range(2):
                act.wait_ge(marks, turns(marks))
                split(0)
                for j in range(2):
                    act.wait_ge(marks, turns(marks))
                    x = ps[:, 2 * w + j, 0:KV * N_CMP].rearrange("p (g c) -> p g c", g=KV)
                    if w:
                        x = x.unsqueeze(2).to_broadcast([P, KV, QG, N_CMP])
                    nc.scalar.activation(hid_v[:, j, :, :, 0:N_CMP] if w else hid_k[:, j, :, 0:N_CMP], x, ACT.Silu) \
                        .then_inc(bank_free, 1)
                split(1)

        def nsa_attention():
            def job_exps(n):
                act.wait_ge(n_max, turns(n_max))
                for tb, (bank, c0, off) in T_STRIPS.items():
                    w = P * tb + P
                    nc.scalar.activation(pn[:, n % 2, off:off + w], ps[:, 3 * (n % 2) + bank, c0:c0 + w], ACT.Exp,
                                         bias=nst[:, n % 2, 1, tb:tb + 1],
                                         accum_out=nst[:, n % 2, 2, tb:tb + 1]).then_inc(n_exps, 1)

            with turns.loop(act, KV, {c_args: 1, n_max: 8, c_turned: 1, n_turned: 24}):
                act.wait_ge(c_args, turns(c_args))
                nc.scalar.activation(pc[:], pc[:], ACT.Exp).then_inc(c_exps, 1)
                job_exps(0)
                act.wait_ge(c_turned, turns(c_turned))
                nc.scalar.activation(pct[:], ps[:, 6, :], ACT.Copy).then_inc(c_copied, 1)
                for n in range(2 * QG):
                    if n + 1 < 2 * QG:
                        job_exps(n + 1)
                    act.wait_ge(n_turned, turns(n_turned))
                    nc.scalar.activation(pnt[:, 0:512], ps[:, 6 + (3 * n) % 2, :], ACT.Copy).then_inc(n_copied_s, 1)
                    turns(n_turned, 2)

        act.dma_start(h[:], a["x"].rearrange("a (t p) c -> p (a t) c", p=P)).then_inc(x_loaded, 16)
        act.dma_start(ident[:], a["c_ident"]).then_inc(params, 16)
        act.dma_start(neg_suffix[:], a["c_neg_suffix"]).then_inc(params, 16)
        act.dma_start(causal6[:], a["c_causal6"]).then_inc(params, 16)
        act.wait_ge(pool_step, 1)
        for tile, row, name, src in param_rows(a):
            n = src.shape[0]
            act.dma_start(x_in[row:row + n, tile, :], src).then_inc(params, 16)
        split(0)
        split(1)
        turned_his(acth)
        act.wait_ge(turned, turns(turned))
        nc.scalar.activation(cols[:], ps[:, 4, :], ACT.Copy).then_inc(turned_hi, 1)
        turns(turned_free)
        act.wait_ge(turned_hi, KC + 1)
        nc.scalar.activation(c_silu[:], cols[:, C_C:C_C + KC], ACT.Silu).then_inc(c_ready, 1)
        feature_copies(2, q_t, 0.125)
        feature_copies(2, k_t)
        token_splits(2)
        stick_breaking()
        act.wait_ge(o_free, 2 + KC)
        act.dma_start(mem_t[:], a["mem"].rearrange("a (t p) c -> p (a t) c", p=P)).then_inc(mem_in, 16)
        load_gb(0)
        turned_his(memh, MEM)
        feature_copies(1, kx, n=MEM)
        feature_copies(1, kx[:, 4:8, :], n=MEM)
        token_splits(2, nt=MB)
        token_splits(2)
        turned_his(acth)
        load_gb(1)
        feature_copies(2, qx, 1.0 / 16)
        cross_attention()
        token_splits(2)
        turned_his(acth)
        conv_ffn()
        load_gb(2)
        token_splits(2, FC)
        mamba()
        scan()
        modulated_his(yh, lambda c: cols[:, C_SNORM + c:C_SNORM + c + 1], None, DI // P)
        load_gain("norm_post_mix_2", 0)
        branch_copies(DI // P, branch=branch_low)
        modulated_his(acth, *modulation(2, 24))
        gated_ffn(0)
        act.wait_ge(h_ready, 5 * TB)
        act.dma_start(select[:], a["c_select"].rearrange("p (n c) -> p n c", n=5)).then_inc(nsa_in, 16)
        act.dma_start(rotary[:], a["c_rotary"].rearrange("p (n c) -> p n c", n=2)).then_inc(nsa_in, 16)
        act.dma_start(cmp_mask[:], a["c_compressed"]).then_inc(nsa_in, 16)
        for twice in range(2):
            act.dma_start(w2k[:, :, twice, :], a["cmp_w2_k_2"].rearrange("(k p) c -> p k c", p=P)).then_inc(nsa_in, 16)
        act.dma_start(w2v[:], a["cmp_w2_v_2"].rearrange("(k p) c -> p k c", p=P)).then_inc(nsa_in, 16)
        act.dma_start(w_gate[:], a["nsa_w_q_2"][0].rearrange("(k p) c -> p k c", p=P)[:, :, D:]).then_inc(nsa_in, 16)
        modulated_his(acth, *modulation(4, 96))
        feature_copies(2, kv8)
        token_splits(1)
        compression()
        modulated_his(acth, *modulation(1, 48))
        feature_copies(2, q_u, 0.125)
        act.wait_ge(gates_raw, 1)
        nc.scalar.activation(gates[:], ps[:, 4, 0:48 * TB].rearrange("p (t c) -> p t c", t=TB), ACT.Sigmoid) \
            .then_inc(gates_ready, 1)
        rotated_out(q_r, KC)
        nsa_attention()
        turned_his(acth)
        load_gain("norm_post_mix_2", 1)
        branch_copies(KC, branch=branch_low)
        modulated_his(acth, *modulation(3, 72))
        gated_ffn(1, last=True)

    @block.vector
    def _(dve):
        turns = Turns()

        def split(slot):
            dve.wait_ge(hi_ready, turns(hi_ready))
            nc.vector.tensor_tensor(wlo[:, slot, :], raw[:, slot, :], whi[:, slot, :].bitcast(F32), ALU.subtract) \
                .then_inc(unit_ready, 1)

        def lo_part(dst, src, hi):
            return nc.vector.tensor_tensor(dst, src, hi.bitcast(F32), ALU.subtract)

        def mod_couples(first, count):
            for b in range(first, first + count):
                for s in range(2):
                    dve.wait_ge(mod_raw[s], turns(mod_raw[s], 16))
                for k in range(KC):
                    for s in range(2):
                        o, w, c = macc[:, 2 * b + s, :], mraw[:, s, k, :], c_silu[:, k:k + 1]
                        if k:
                            dve.wait_ge(mod_step, turns(mod_step))
                            last = nc.vector.scalar_tensor_tensor(out=o, in0=w, scalar=c, in1=o, op0=ALU.mult,
                                                                  op1=ALU.add)
                        else:
                            last = nc.vector.tensor_scalar(o, w, c, None, ALU.mult)
                        last.then_inc(mod_acc if k == KC - 1 else mod_step, 1)

        def mod_store(units, col):
            dve.wait_ge(mod_cols, turns(mod_cols))
            nc.vector.tensor_tensor(modv[:, bass.ds(col, 2 * units)], ps[:, 6, 0:2 * units],
                                    cols[:, bass.ds(C_MODB + col, 2 * units)], ALU.add).then_inc(mod_done, 1)

        def mod_steps(units):
            return {mod_raw[0]: 8 * units, mod_raw[1]: 8 * units, mod_step: 7 * units, mod_cols: int(units > 0)}

        def splits(pairs, mods=0, col=0):
            with turns.loop(dve, pairs, {hi_ready: 2, marks: 4} | mod_steps(mods)) as i:
                early = -(-mods // 4)
                mod_couples(0, early)
                split(0)
                mod_couples(early, mods // 2 - early)
                split(1)
                turns(marks, 4)
                if mods:
                    mod_store(mods, 2 * mods * i + col)

        def token_banks(halves, take, kc=KC, nt=TB, mods=0, col=0):
            units = -(-kc // 4)
            with turns.loop(dve, halves, {marks: units - 1 + nt, hi_ready: units} | mod_steps(mods)) as i:
                early = -(-mods // 4)
                mod_couples(0, early)
                for u in range(units - 1):
                    split(u % 2)
                mod_couples(early, mods // 2 - early)
                turns(marks, units - 1)
                for t in range(nt):
                    dve.wait_ge(marks, turns(marks))
                    take(i, t).then_inc(bank_free, 1)
                split(1)
                if mods:
                    mod_store(mods, 2 * mods * i + col)

        def turned_los(dst, hi, n=SEQ):
            for c in range(KC):
                dve.wait_ge(turned_hi, turns(turned_hi))
                lo_part(dst[:, c, 0:n], ps[:, 4 + c % 4, 0:n], hi[:, c, 0:n]).then_inc(turned_free, 1)

        def residual_sum(i, t):
            c = bass.ds(512 * i, 512)
            return nc.vector.scalar_tensor_tensor(out=h[:, t, c], in0=h[:, t, c], scalar=ALPHA, in1=ps[:, t, :],
                                                  op0=ALU.mult, op1=ALU.add)

        def layer_norm():
            dve.drain()
            for t in range(TB):
                for half in range(2):
                    last = nc.vector.bn_stats(stats[:, t, half, :], h[:, t, 512 * half:512 * half + 512])
            last.then_inc(dve_step, 1)
            dve.wait_ge(dve_step, turns(dve_step))
            for t in range(TB):
                last = nc.vector.bn_aggr(mean_var[:, t, :], stats[:, t, :, :])
            last.then_inc(moments, 1)
            dve.wait_ge(rstd_ready, turns(rstd_ready))
            dve.wait_ge(gb_in, turns(gb_in, 32))
            for t in range(TB):
                last = nc.vector.tensor_scalar(h[:, t, :], h[:, t, :], mean_var[:, t, 0:1], rstd[:, t:t + 1],
                                               ALU.subtract, ALU.mult)
            last.then_inc(dve_step, 1)
            dve.wait_ge(dve_step, turns(dve_step))
            for t in range(TB):
                last = nc.vector.tensor_tensor(h[:, t, :], h[:, t, :], gb[:, 0, :], ALU.mult)
            last.then_inc(dve_step, 1)
            dve.wait_ge(dve_step, turns(dve_step))
            for t in range(TB):
                nc.vector.tensor_tensor(h[:, t, :], h[:, t, :], gb[:, 1, :], ALU.add).then_inc(h_ready, 1)

        def stick_breaking():
            with turns.loop(dve, 4, {z_ready: 12, log_ready: 4, evac_hi: 2}) as i:
                for pair in range(2):
                    for hd in range(2):
                        for strips in ((0,), (1, 3), (2,)):
                            dve.wait_ge(z_ready, turns(z_ready))
                            for sb in strips:
                                bank, c0, off, n = strip(sb)
                                last = nc.vector.tensor_scalar(sp_e[:, hd, off:off + n],
                                                               ps[:, 3 * hd + bank, c0:c0 + n], SOFTPLUS_MAX, None,
                                                               ALU.min)
                        last.then_inc(capped, 1)
                    for hd in range(2):
                        dve.wait_ge(log_ready, turns(log_ready))
                        for sb in range(TB):
                            bank, c0, off, n = strip(sb)
                            last = nc.vector.scalar_tensor_tensor(
                                out=sp[:, hd, off:off + n], in0=ps[:, 3 * hd + bank, c0:c0 + n], scalar=1.0,
                                in1=sp_e[:, hd, off:off + n], op0=ALU.mult, op1=ALU.max)
                        last.then_inc(sp_ready, 1)
                    dve.wait_ge(evac_hi, turns(evac_hi))
                    lo_part(actl[:, 2 * i + pair, :], ps[:, 6 + pair, :], acth[:, 2 * i + pair, :]) \
                        .then_inc(o_free, 1)

        def cross_attention():
            def maxima(hd):
                b = 4 * (hd % 2)
                for k in range(2):
                    dve.wait_ge(scores, 2 * hd + k + 1)
                    last = nc.vector.tensor_reduce(small[:, 16 + b + 2 * k:18 + b + 2 * k],
                                                   ps[:, 2 * (hd % 2) + k, :].rearrange("p (t m) -> p t m", t=2),
                                                   AX.X, ALU.max)
                last.then_inc(dve_step, 1)
                dve.wait_ge(dve_step, turns(dve_step))
                nc.vector.tensor_scalar(small[:, b:b + 4], small[:, 16 + b:20 + b], -1.0, None, ALU.mult) \
                    .then_inc(score_max, 1)

            def normalise(hd):
                b = 4 * (hd % 2)
                dve.wait_ge(probs, 4 * hd + 4)
                nc.vector.reciprocal(small[:, 24 + b:28 + b], small[:, 8 + b:12 + b]).then_inc(dve_step, 1)
                dve.wait_ge(dve_step, turns(dve_step))
                nc.vector.tensor_tensor(px[:, hd % 2, :, :], px[:, hd % 2, :, :],
                                        small[:, 24 + b:28 + b].unsqueeze(2).to_broadcast([P, TB, MEM]),
                                        ALU.mult).then_inc(probs_normed, 1)

            maxima(0)
            for hd in range(XA_HEADS):
                if hd + 1 < XA_HEADS:
                    maxima(hd + 1)
                normalise(hd)
                for c in range(2):
                    dve.wait_ge(evac_hi, turns(evac_hi))
                    lo_part(actl[:, 2 * hd + c, :], ps[:, 6 + c, :], acth[:, 2 * hd + c, :]).then_inc(heads_free, 1)

        def conv_ffn():
            with turns.loop(dve, FC // 2, {hi_ready: 2, taps: 4, dve_step: 4, gated: 2, evac_hi: 2,
                                           conv_done: 4, marks: 4}) as i:
                turns(marks, 4)
                for u in range(2):
                    for tap, shift in ((1, 1), (0, 2)):
                        for j in range(2):
                            if tap:
                                dve.wait_ge(taps, turns(taps))
                            w = cols[:, bass.ds(C_CW + 2 * FC * tap + FC * u + 2 * i + j, 1)]
                            x = conv_t[:, 2 * u + j, shift:]
                            last = nc.vector.scalar_tensor_tensor(out=x, in0=ps[:, 2 * u + j, 0:SEQ - shift],
                                                                  scalar=w, in1=x, op0=ALU.mult, op1=ALU.add)
                            last.then_inc(dve_step if tap else conv_done, 1)
                        if tap:
                            dve.wait_ge(dve_step, turns(dve_step, 2))
                    if u == 0:
                        split(0)
                dve.wait_ge(conv_done, FREE0 + turns(conv_done, 4))
                for j in range(2):
                    dve.wait_ge(gated, turns(gated))
                    nc.vector.tensor_tensor(conv_t[:, j, :], conv_t[:, j, :], conv_t[:, 2 + j, :], ALU.mult) \
                        .then_inc(hid_value, 1)
                split(1)
                for j in range(2):
                    dve.wait_ge(evac_hi, turns(evac_hi))
                    lo_part(hid_l[:, 2 * i + j, :], conv_t[:, j, :], hid_h[:, 2 * i + j, :]).then_inc(hid_ready, 1)

        def stored(ins):
            ins.then_inc(dve_step, 1)
            dve.wait_ge(dve_step, turns(dve_step))

        def row_moments(src):
            dve.drain()
            for t in range(TB):
                for half in range(2):
                    last = nc.vector.bn_stats(stats[:, t, half, :], src[:, t, 512 * half:512 * half + 512])
            stored(last)
            for t in range(TB):
                last = nc.vector.bn_aggr(mean_var[:, t, :], stats[:, t, :, :])
            stored(last)
            stored(nc.vector.tensor_tensor(mean_var[:, :, 0], mean_var[:, :, 0], mean_var[:, :, 0], ALU.mult))
            nc.vector.tensor_tensor(mean_var[:, :, 1], mean_var[:, :, 1], mean_var[:, :, 0], ALU.add) \
                .then_inc(moments, 1)
            dve.wait_ge(rstd_ready, turns(rstd_ready))

        def normed_rows():
            row_moments(h)
            for t in range(TB):
                nc.vector.tensor_scalar(normed[:, t, :], h[:, t, :], rstd[:, t:t + 1], None, ALU.mult) \
                    .then_inc(normed_ready, 1)

        def modulated_los(lo, hi, chunks=KC):
            for c in range(chunks):
                dve.wait_ge(turned_hi, turns(turned_hi))
                lo_part(lo[:, c, :], modulated[:, c % 2, :], hi[:, c, :]).then_inc(turned_free, 1)

        def branch_splits(kc, last=False):
            units = -(-kc // 4)
            with turns.loop(dve, 1 if last else 2, {hi_ready: units}):
                for u in range(units):
                    split(u % 2)
            if last:
                for u in range(units - 2):
                    split(u % 2)

        def add_branch(gate, branch=branch):
            dve.wait_ge(branch_out, FREE0 + turns(branch_out, 8))
            make_diag(gate)
            row_moments(branch)
            dve.wait_ge(gate_rows, turns(gate_rows))
            dve.wait_ge(gb_in, turns(gb_in, 16))
            stored(nc.vector.tensor_tensor(gb[:, 0, :].rearrange("p (b c) -> p b c", b=2), ps[:, 4:6, :],
                                           gb[:, 1, :].rearrange("p (b c) -> p b c", b=2), ALU.mult))
            for t in range(TB):
                last = nc.vector.scalar_tensor_tensor(out=branch[:, t, :], in0=branch[:, t, :],
                                                      scalar=rstd[:, t:t + 1], in1=gb[:, 0, :], op0=ALU.mult,
                                                      op1=ALU.mult)
            stored(last)
            for t in range(TB):
                nc.vector.tensor_tensor(h[:, t, :], h[:, t, :], branch[:, t, :], ALU.add).then_inc(h_ready, 1)

        def gated_ffn(gate, last=False):
            with turns.loop(dve, FC // 2, {hi_ready: 2, gated: 2, evac_hi: 2, marks: 4}) as i:
                split(0)
                turns(marks, 2)
                for j in range(2):
                    dve.wait_ge(marks, turns(marks))
                    dve.wait_ge(gated, turns(gated))
                    nc.vector.tensor_tensor(conv_t[:, j, :], conv_t[:, j, :], ps[:, 2 + j, :], ALU.mult) \
                        .then_inc(hid_value, 1)
                split(1)
                for j in range(2):
                    dve.wait_ge(evac_hi, turns(evac_hi))
                    lo_part(hid_l[:, 2 * i + j, :], conv_t[:, j, :], hid_h[:, 2 * i + j, :]).then_inc(hid_ready, 1)
            branch_splits(FC, last)
            add_branch(gate)

        def conv_pairs(pairs, first):
            with turns.loop(dve, pairs, {hi_ready: 2, taps: 4, dve_step: 8, marks: 4}) as i:
                turns(marks, 4)
                for u in range(2):
                    for tap, shift in ((2, 1), (1, 2), (0, 3)):
                        for j in range(2):
                            b = 2 * u + j
                            if tap == 2:
                                dve.wait_ge(taps, turns(taps))
                            x = conv4[:, b, shift:]
                            last = nc.vector.scalar_tensor_tensor(
                                out=x, in0=ps[:, b, 0:SEQ - shift],
                                scalar=cols[:, bass.ds(C_SCW + 24 * tap + 4 * i + (first + b), 1)], in1=x,
                                op0=ALU.mult, op1=ALU.add)
                            last.then_inc(dve_step if tap else conv_done, 1)
                        if tap:
                            dve.wait_ge(dve_step, turns(dve_step, 2))
                    if u == 0:
                        split(0)
                split(1)

        def per_head(x):
            return x.unsqueeze(2).to_broadcast([P, HPG, 64])

        def by_head(x):
            return x.rearrange("p (h d) -> p h d", h=HPG)

        def dt_and_sums():
            dve.wait_ge(a_ready, 1)
            nc.vector.tensor_scalar(heads[:, 1, :], heads[:, 1, :], -1.0, None, ALU.mult)
            dve.wait_ge(dt_raw, 1)
            stored(nc.vector.tensor_tensor(dt[:], ps[:, 4, 0:P].rearrange("p (t h) -> p t h", t=TB),
                                           heads[:, 0:1, :].to_broadcast([P, TB, SSM_H]), ALU.add))
            nc.vector.tensor_scalar(dt_e[:], dt[:], SOFTPLUS_MAX, None, ALU.min).then_inc(dt_cap, 1)
            dve.wait_ge(dt_log, 1)
            stored(nc.vector.tensor_tensor(dt[:], dt[:], dt_e[:], ALU.max))
            nc.vector.tensor_tensor(dta[:], dt[:], heads[:, 1:2, :].to_broadcast([P, TB, SSM_H]), ALU.mult) \
                .then_inc(dta_ready, 1)
            dve.wait_ge(acs_ready, 1)
            stored(nc.vector.tensor_copy(acs[:], ps[:, 5, 0:P].rearrange("p (t h) -> p t h", t=TB)))
            nc.vector.tensor_tensor(tail[:], ps[:, 5:6, P:P + SSM_H].to_broadcast([P, 2, SSM_H]), acs[:, 0:2, :],
                                    ALU.subtract).then_inc(acs_out, 1)

        def scan():
            dve.wait_ge(tail_ready, 1)
            with turns.loop(dve, SSM_G, {group_in: 5, dve_step: 16, cb_ready: 1, acs_rows: 8, head_y: 8,
                                         dx_ready: 4}) as g:
                dve.wait_ge(group_in, turns(group_in, 5))
                cols_g, heads_g = bass.ds(512 * g, 512), bass.ds(HPG * g, HPG)
                for t in range(TB):
                    last = nc.vector.tensor_tensor(by_head(xdt[:, t, :]), by_head(tok[:, t, cols_g]),
                                                   per_head(dt[:, t, heads_g]), ALU.mult)
                stored(last)
                for t in range(2):
                    last = nc.vector.tensor_tensor(by_head(xdt_tail[:, t, :]), by_head(xdt[:, t, :]),
                                                   per_head(tail[:, t, heads_g]), ALU.mult)
                last.then_inc(xdt_ready, 1)
                dve.wait_ge(cb_ready, turns(cb_ready))
                for ch in range(2):
                    c = slice(3 * P * ch, 3 * P * ch + 3 * P)
                    nc.vector.tensor_tensor(cbm[:, c], ps[:, 6 + ch, 0:3 * P], causal6[:, c], ALU.mult)
                nc.vector.tensor_copy(state[:], ps[:, 5, :]).then_inc(cb_out, 1)
                for hd in range(HPG):
                    dve.wait_ge(acs_rows, turns(acs_rows))
                    if hd >= 2:
                        dve.wait_ge(head_y, turns(head_y))
                    for t in range(TB):
                        ch, b = t // 2, t % 2
                        off, n = 384 * ch + 256 * b, 256 - P * b
                        last = nc.vector.tensor_scalar(decay[:, hd % 2, off:off + n],
                                                       ps[:, 6 + hd % 2, 256 * ch + P * b:256 * ch + 256],
                                                       acsg[:, t, hd:hd + 1], 0.0, ALU.subtract, ALU.min)
                    last.then_inc(decay_arg, 1)
                dve.wait_ge(head_y, turns(head_y, 2))
                for t in range(TB):
                    dve.wait_ge(dx_ready, turns(dx_ready))
                    stored(nc.vector.tensor_tensor(dx[:, t, :], dx[:, t, :], ps[:, t, :], ALU.add))
                    if t >= 2:
                        stored(nc.vector.tensor_tensor(by_head(xdt[:, t, :]), by_head(ps[:, 2 + t, :]),
                                                       per_head(eacs[:, t, heads_g]), ALU.mult))
                        stored(nc.vector.tensor_tensor(dx[:, t, :], dx[:, t, :], xdt[:, t, :], ALU.add))
                    stored(nc.vector.tensor_tensor(gate_z[:, t, cols_g], gate_z[:, t, cols_g], dx[:, t, :],
                                                   ALU.mult))
                    last = nc.vector.bn_stats(gstats[:, t, g, :], gate_z[:, t, cols_g])
                    if t < TB - 1:
                        stored(last)
                last.then_inc(group_y, 1)

        def group_norm():
            dve.wait_ge(group_y, DONE0 + SSM_G)
            for n in range(TB * SSM_G):
                last = nc.vector.bn_aggr(gmv[:, n, :], gstats[:, n // SSM_G, n % SSM_G, :])
            stored(last)
            stored(nc.vector.tensor_tensor(gmv[:, :, 0], gmv[:, :, 0], gmv[:, :, 0], ALU.mult))
            nc.vector.tensor_tensor(ginv[:], gmv[:, :, 1], gmv[:, :, 0], ALU.add).then_inc(moments, 1)
            dve.wait_ge(rstd_ready, turns(rstd_ready))
            for n in range(TB * SSM_G):
                x = gate_z[:, n // SSM_G, 512 * (n % SSM_G):512 * (n % SSM_G) + 512]
                last = nc.vector.tensor_scalar(x, x, ginv[:, n:n + 1], None, ALU.mult)
            last.then_inc(normed_ready, 1)

        def rotate(src, chunks, first=0):
            for c in range(chunks):
                if c >= 2:
                    dve.wait_ge(rot_ready, turns(rot_ready, first))
                for n in range(2):
                    nc.vector.tensor_tensor(rot_t[:, c % 2, n, :], src[:, c, :], rotary[:, n, :], ALU.mult) \
                        .then_inc(rot_in, 1)
            turns(rot_ready, 2 * first)

        def compression():
            dve.wait_ge(nsa_in, 16 * NSA_PARAMS)
            for n in range(2 * KV):
                w, g = n // KV, n % KV
                dve.wait_ge(dup_ready, n + 1)
                for half in range(2):
                    rows = slice(HD * half, HD * half + HD)
                    x = ps[rows, 4 + n % 4, :].rearrange("p (n b two) -> p two b n", b=8, two=2)
                    for e in range(2):
                        pos = cols[rows, C_POS[w] + 8 * e:C_POS[w] + 8 * e + 8]
                        last = nc.vector.tensor_tensor(kcp[rows, w, 8 * e:8 * e + 8, N_CMP * g:N_CMP * g + N_CMP],
                                                       x[:, half, :, e:e + N_CMP],
                                                       pos.unsqueeze(2).to_broadcast([HD, 8, N_CMP]), ALU.add)
                last.then_inc(dup_free, 1)
            rotate(kv8[:, 4:8, :], 4, 2)
            for w in range(2):
                dve.wait_ge(blocks_hi, w + 1)
                lo_part(kcpl[:, w, :, :], kcp[:, w, :, :], kcph[:, w, :, :]).then_inc(blocks_lo, 1)
            for w in range(2):
                split(0)
                split(1)
            turns(marks, 6)
            dve.wait_ge(cmp_ready, 1)
            nc.vector.tensor_copy(kcmp[:], ps[:, 4, 0:P].rearrange("p (g c) -> p g c", g=KV))
            same = cmp_mask[:, TB * CMP:].unsqueeze(2).to_broadcast([P, QG, HD])
            for g in range(KV):
                last = nc.vector.tensor_tensor(vbd[:, g, :].rearrange("p (h d) -> p h d", h=QG),
                                               ps[:, 5:6, HD * g:HD * g + HD].to_broadcast([P, QG, HD]), same, ALU.mult)
            last.then_inc(cmp_kept, 1)

        def nsa_attention():
            heads16 = lambda n: cst2[:, n, :]
            wide = lambda n: cst2[:, n, :].rearrange("p (t h) -> p t h", t=TB).unsqueeze(3).to_broadcast([P, TB, QG, CMP])

            def maxima(n):
                s = n % 2
                for tb, (bank, c0, _) in T_STRIPS.items():
                    if tb != 0:
                        dve.wait_ge(n_scores, turns(n_scores))
                    last = nc.vector.tensor_reduce(nst[:, s, 0, tb:tb + 1], ps[:, 3 * s + bank, c0:c0 + P * tb + P],
                                                   AX.X, ALU.max)
                stored(last)
                nc.vector.tensor_scalar(nst[:, s, 1, :], nst[:, s, 0, :], -1.0, None, ALU.mult).then_inc(n_max, 1)

            with turns.loop(dve, KV, {c_scores: 2, dve_step: 7 + 8 * 3, n_scores: 24, c_exps: 1, c_outs: 1, n_turned: 24,
                                      n_exps: 32, n_outs: 8}) as g:
                mask = cmp_mask[:, 0:TB * CMP].rearrange("p (t c) -> p t c", t=TB).unsqueeze(2)
                for side in range(2):
                    dve.wait_ge(c_scores, turns(c_scores))
                    last = nc.vector.tensor_tensor(
                        pc[:].rearrange("p t (pair side) c -> p side t pair c", side=2)[:, side],
                        ps[:, 6 + side, 0:256].rearrange("p (t pair c) -> p t pair c", t=TB, pair=2),
                        mask.to_broadcast([P, TB, 2, CMP]), ALU.add)
                stored(last)
                stored(nc.vector.tensor_reduce(heads16(0), pc[:].rearrange("p t h c -> p (t h) c"), AX.X, ALU.max))
                stored(nc.vector.tensor_scalar(heads16(0), heads16(0), -1.0e20, None, ALU.max))
                nc.vector.tensor_tensor(pc[:], pc[:], wide(0), ALU.subtract).then_inc(c_args, 1)
                maxima(0)
                dve.wait_ge(c_exps, turns(c_exps))
                stored(nc.vector.tensor_reduce(heads16(1), pc[:].rearrange("p t h c -> p (t h) c"), AX.X, ALU.add))
                stored(nc.vector.tensor_scalar(heads16(1), heads16(1), 0.5, None, ALU.max))
                stored(nc.vector.reciprocal(heads16(2), heads16(1)))
                stored(nc.vector.tensor_tensor(heads16(3).rearrange("p (t h) -> p t h", t=TB),
                                               heads16(2).rearrange("p (t h) -> p t h", t=TB), gate_g[:, :, :, 0],
                                               ALU.mult))
                nc.vector.tensor_tensor(pc[:], pc[:], wide(3), ALU.mult).then_inc(c_probs, 1)
                dve.wait_ge(c_outs, turns(c_outs))
                for b in range(2):
                    last = nc.vector.tensor_copy(oacc[:, 2 * b:2 * b + 2, bass.ds(256 * g, 256)],
                                                 ps[:, 3 + b, :].rearrange("p (t c) -> p t c", t=2))
                last.then_inc(c_taken, 1)
                for n in range(2 * QG):
                    s = n % 2
                    if n + 1 < 2 * QG:
                        maxima(n + 1)
                    turns(n_turned)
                    for r in (1, 2):
                        dve.wait_ge(n_turned, turns(n_turned))
                        w = 512 if r == 1 else 256
                        nc.vector.tensor_copy(pnt[:, 512 * r:512 * r + w], ps[:, 6 + (3 * n + r) % 2, 0:w]) \
                            .then_inc(n_copied_v, 1)
                    dve.wait_ge(n_exps, turns(n_exps, 4))
                    stored(nc.vector.reciprocal(nst[:, s, 3, :], nst[:, s, 2, :]))
                    stored(nc.vector.tensor_tensor(nst[:, s, 3, :], nst[:, s, 3, :], gate_g[:, :, n // 2, 1 + n % 2],
                                                   ALU.mult))
                    dve.wait_ge(n_outs, turns(n_outs))
                    for tb in range(TB):
                        c = bass.ds(256 * g + HD * (n // 2), HD)
                        last = nc.vector.scalar_tensor_tensor(
                            out=oacc[:, tb, c], in0=ps[:, 3 * s + 2, 256 + HD * tb:256 + HD * tb + HD],
                            scalar=nst[:, s, 3, tb:tb + 1], in1=oacc[:, tb, c], op0=ALU.mult, op1=ALU.add)
                    last.then_inc(n_taken, 1)

        def make_diag(gate):
            last = nc.vector.tensor_tensor(gate_diag[:], ident[:].unsqueeze(1).to_broadcast([P, KC, P]),
                                           modv[:, gate:gate + KC].unsqueeze(2).to_broadcast([P, KC, P]), ALU.mult)
            return last.then_inc(diag_ready, 1)

        dve.sem_inc(bank_free, FREE0)
        dve.sem_inc(conv_done, FREE0)
        dve.sem_inc(branch_out, FREE0)
        dve.sem_inc(tok_free, 4)
        dve.sem_inc(hid_value, HID0)
        dve.sem_inc(group_y, DONE0)
        dve.sem_inc(n_taken, DONE0)
        dve.sem_inc(mod_acc, MODS)
        dve.sem_inc(turned_free, 4)
        dve.sem_inc(o_free, 2)
        dve.sem_inc(unit_ready, SLOTS)
        nc.vector.memset(neg_ones[:], -1.0).then_inc(set_up, 1)
        nc.vector.memset(ones_c[:], 1.0).then_inc(set_up, 1)
        dve.wait_ge(params, 16 * N_PARAMS)
        nc.vector.tensor_copy(ident_b[:], ident[:]).then_inc(set_up, 1)
        split(0)
        split(1)
        turned_los(actl, acth)
        dve.wait_ge(turned_hi, turns(turned_hi))
        nc.vector.tensor_copy(small[:, 0:1], cols[:, 0:1]).then_inc(turned_free, 1)
        dve.wait_ge(c_ready, 1)
        splits(4, mods=6, col=0)
        token_banks(2, lambda i, t: nc.vector.tensor_copy(v_s[:, t, bass.ds(512 * i, 512)], ps[:, t, :]),
                    mods=4, col=48)
        stick_breaking()
        turned_los(meml, memh, MEM)
        splits(2, mods=2, col=64)
        token_banks(2, lambda i, t: nc.vector.tensor_copy(vx[:, t, bass.ds(512 * i, 512)], ps[:, t, :]), nt=MB,
                    mods=2, col=72)
        token_banks(2, residual_sum, mods=4, col=80)
        layer_norm()
        turned_los(actl, acth)
        splits(2, mods=4, col=96)
        dve.wait_ge(mod_done, 14)
        for n, (scale, g) in enumerate(((8, C_PRE_MIX), (56, C_PRE_MIX + KC), (32, C_PRE_FFN), (80, C_PRE_FFN + KC),
                                        (104, C_KVN))):
            nc.vector.scalar_tensor_tensor(out=gains[:, n, :], in0=modv[:, scale:scale + KC], scalar=1.0,
                                           in1=cols[:, g:g + KC], op0=ALU.add, op1=ALU.mult)
        cross_attention()
        token_banks(2, residual_sum)
        layer_norm()
        turned_los(actl, acth)
        conv_ffn()
        token_banks(2, residual_sum, FC)
        layer_norm()
        normed_rows()
        modulated_los(actl, acth)
        conv_pairs(4, 0)
        conv_pairs(1, 16)
        conv_pairs(1, 20)
        with turns.loop(dve, 4, {hi_ready: 2}):
            split(0)
            split(1)
        turns(marks, 20)
        dt_and_sums()
        scan()
        group_norm()
        modulated_los(yl, yh, DI // P)
        branch_splits(DI // P)
        add_branch(16, branch_low)
        normed_rows()
        modulated_los(actl, acth)
        turns(marks, 8 + 6)
        gated_ffn(40)
        turns(marks, 18)
        normed_rows()
        modulated_los(actl, acth)
        splits(2)
        token_banks(1, lambda i, t: nc.vector.tensor_copy(v_sw[:, t, :], ps[:, t, :]))
        compression()
        modulated_los(actl, acth)
        splits(2)
        dve.wait_ge(gates_ready, 1)
        rotate(q_u, KC, 1)
        nsa_attention()
        turned_los(actl, acth)
        branch_splits(KC)
        add_branch(64, branch_low)
        normed_rows()
        modulated_los(actl, acth)
        turns(marks, 10)
        gated_ffn(88, last=True)

    @block.gpsimd
    def _(pool):
        turns = Turns()

        def inverse_roots(eps, src=mean_var[:, :, 1], dst=rstd[:], n=TB):
            pool.wait_ge(moments, turns(moments))
            nc.gpsimd.tensor_scalar(dst, src, eps, None, ALU.add).then_inc(pool_step, 1)
            pool.wait_ge(pool_step, turns(pool_step))
            nc.gpsimd.tensor_tensor(dst, dst, neg_half[:, 0:n], ALU.pow).then_inc(rstd_ready, 1)
            pool.wait_ge(rstd_ready, turns(rstd_ready))

        def mod_loads(turns_, units, w, first):
            v = w.rearrange("(k p) c -> p k c", p=P)
            with turns.loop(pool, turns_, {mod_acc: units}) as i:
                for u in range(units):
                    pool.wait_ge(mod_acc, turns(mod_acc))
                    pool.dma_start(mraw[:, u % 2, :, :], v[:, :, bass.ds(256 * units * i + 256 * (first + u), 256)]) \
                        .then_inc(mod_raw[u % 2], 16)

        def scan():
            pool.wait_ge(acs_out, 1)
            pool.wait_ge(tok_free, 4 + 20)
            with turns.loop(pool, SSM_G, {group_y: 1, group_in: 5, decay_exp: 8, cb_out: 1, mixed: 8,
                                          dx_ready: 4}) as g:
                pool.wait_ge(group_y, turns(group_y) - 1 + DONE0)
                for dst, src in ((bst[:], bct[:, g, :]), (cst[:], bct[:, 4 + g, :]),
                                 (btk[:], tok[:, 0:2, bass.ds(P * g + DI, P)]),
                                 (dtag[:], dta[:, :, bass.ds(HPG * g, HPG)]),
                                 (acsg[:], acs[:, :, bass.ds(HPG * g, HPG)])):
                    nc.gpsimd.tensor_copy(dst, src).then_inc(group_in, 1)
                    pool.wait_ge(group_in, turns(group_in))
                pool.wait_ge(cb_out, turns(cb_out))
                for hd in range(HPG):
                    pool.wait_ge(decay_exp, turns(decay_exp))
                    nc.gpsimd.tensor_tensor(decay[:, hd % 2, :], decay[:, hd % 2, :], cbm[:], ALU.mult) \
                        .then_inc(mixed, 1)
                    pool.wait_ge(mixed, turns(mixed))
                    if hd < TB:
                        nc.gpsimd.tensor_tensor(
                            dx[:, hd, :].rearrange("p (h d) -> p h d", h=HPG),
                            tok[:, hd, bass.ds(512 * g, 512)].rearrange("p (h d) -> p h d", h=HPG),
                            heads[:, 2, bass.ds(HPG * g, HPG)].unsqueeze(2).to_broadcast([P, HPG, 64]), ALU.mult) \
                            .then_inc(dx_ready, 1)
                        pool.wait_ge(dx_ready, turns(dx_ready))

        nc.gpsimd.memset(x_in[96:P, 2:4, :], 0.0).then_inc(pool_step, 1)
        pool.wait_ge(pool_step, turns(pool_step))
        nc.gpsimd.memset(neg_half[:], -0.5).then_inc(pool_step, 1)
        pool.wait_ge(pool_step, turns(pool_step))
        nc.gpsimd.memset(strict_b[:], 0.0).then_inc(pool_step, 1)
        pool.wait_ge(pool_step, turns(pool_step))
        nc.gpsimd.affine_select(out=strict_b[:], in_=strict_b[:], pattern=[[1, P]], compare_op=ALU.is_gt, fill=NEG,
                                base=0, channel_multiplier=-1).then_inc(set_up, 1)
        nc.gpsimd.memset(causal_b[:], 0.0).then_inc(pool_step, 1)
        pool.wait_ge(pool_step, turns(pool_step))
        nc.gpsimd.affine_select(out=causal_b[:], in_=causal_b[:], pattern=[[-1, P]], compare_op=ALU.is_ge, fill=NEG,
                                base=0, channel_multiplier=1).then_inc(set_up, 1)
        mod_loads(4, 6, a["mod_w_2"][0], 0)
        mod_loads(2, 4, a["mod_w_2"][1], 0)
        pool.wait_ge(bank_free, 4 + 24)
        with turns.loop(pool, 4, {o_free: 2, staged: 6}) as i:
            for pair in range(2):
                pool.wait_ge(o_free, turns(o_free))
                c = 2 * i + pair
                nc.gpsimd.tensor_copy(qst[:, pair, :], q_t[:, c, :]).then_inc(staged, 1)
                pool.wait_ge(staged, turns(staged))
                nc.gpsimd.tensor_copy(kst[:, pair, :], k_t[:, c, :]).then_inc(staged, 1)
                pool.wait_ge(staged, turns(staged))
                nc.gpsimd.tensor_copy(vst[:, pair, :, :], v_s[:, :, bass.ds(P * c, P)]).then_inc(staged, 1)
                pool.wait_ge(staged, turns(staged))
        pool.wait_ge(o_free, 2 + KC)
        mod_loads(2, 2, a["mod_w_2"][1], 8)
        mod_loads(2, 2, a["mod_w_2"][1], 12)
        mod_loads(2, 4, a["mod_w_2"][1], 16)
        inverse_roots(LN_EPS)
        mod_loads(2, 4, a["kv_mod_w_2"], 0)
        inverse_roots(LN_EPS)
        inverse_roots(LN_EPS)
        inverse_roots(RMS_EPS)
        for kind in range(2):
            for j in range(4):
                pool.wait_ge(convolved, 16 + 4 * kind + j + 1)
                nc.gpsimd.tensor_copy(bct[:, 4 * kind + j, :], conv4[:, j, :]).then_inc(bc_copied, 1)
                pool.wait_ge(bc_copied, turns(bc_copied))
        scan()
        inverse_roots(RMS_EPS, ginv[:], ginv[:], TB * SSM_G)
        inverse_roots(RMS_EPS)
        inverse_roots(RMS_EPS)
        inverse_roots(RMS_EPS)
        inverse_roots(RMS_EPS)
        for x in (hid_k, hid_v):
            nc.gpsimd.memset(x[:], 0.0).then_inc(hid_padded, 1)
            pool.wait_ge(hid_padded, turns(hid_padded))
        pool.wait_ge(cmp_kept, 1)
        pool.wait_ge(rot_free, 2 * KV + KC)
        with turns.loop(pool, KV, {n_taken: 8, key_head_in: 9}) as g:
            pool.wait_ge(n_taken, turns(n_taken, 8) - 8 + DONE0)
            for dst, src in ((kc_g[:], kcmp[:, g, :]), (qu_g[:], q_u[:, bass.ds(2 * g, 2), :]),
                             (k_g[:, 0, :], kdup[:, g, :]), (qr_g[:], q_r[:, bass.ds(2 * g, 2), :]),
                             (k_g[:, 1, :], kdup[:, KV + g, :]), (gate_g[:].rearrange("p t h c -> p t (h c)"), gates[:, :, bass.ds(12 * g, 12)]),
                             (vb_g[:], vbd[:, g, :]), (v_g[:, 0, :, :], v_sw[:, :, bass.ds(HD * g, HD)]),
                             (v_g[:, 1, :, :], v_sw[:, :, bass.ds(HD * g + 256, HD)])):
                nc.gpsimd.tensor_copy(dst, src).then_inc(key_head_in, 1)
                pool.wait_ge(key_head_in, turns(key_head_in))
        inverse_roots(RMS_EPS)
        inverse_roots(RMS_EPS)
        inverse_roots(RMS_EPS)

    engines.close()
    ctx.close()


_INS = (
    "x mem ln_g ln_b mix_wo sb_win xa_wq xa_wkv xa_wo ffn_up ffn_conv ffn_conv_b ffn_down c_2 mod_w_2 mod_b_2 "
    "norm_pre_mix_2 norm_post_mix_2 norm_pre_ffn_2 norm_post_ffn_2 ffn_w_in_2 ffn_w_out_2 ssm_w_in_2 "
    "ssm_conv_w_2 ssm_conv_b_2 ssm_dt_bias_2 ssm_a_log_2 ssm_d_2 ssm_norm_2 ssm_w_out_2 kv_norm_2 kv_mod_w_2 "
    "kv_mod_b_2 w_kv_2 cmp_pos_k_2 cmp_w1_k_2 cmp_w2_k_2 cmp_pos_v_2 cmp_w1_v_2 cmp_w2_v_2 nsa_w_q_2 nsa_w_o_2"
).split()


def kernel(**inputs):
    import concourse.bacc as _bacc
    from concourse.bass_utils import run_bass_kernel_spmd as _run

    nc = _bacc.Bacc("TRN2", target_bir_lowering=False, num_devices=1)
    arrays, dram = {}, {}
    given = {name: np.ascontiguousarray(inputs[name]) for name in _INS}
    given.update(shape_constants())
    for name, array in given.items():
        arrays[f"in_{name}"] = array
        dram[name] = nc.dram_tensor(f"in_{name}", array.shape, mybir.dt.from_np(array.dtype),
                                    kind="ExternalInput").ap()
    out = nc.dram_tensor("out", (1, SEQ, D), F32, kind="ExternalOutput").ap()
    build(nc, dram, out)
    r = _run(nc, [arrays], core_ids=[0])
    return r.results[0]["out"]
```

```python
from contextlib import ExitStack, contextmanager

import numpy as np
import concourse.bass as bass
from concourse import mybir

F32 = mybir.dt.float32
F32R = mybir.dt.float32r
BF16 = mybir.dt.bfloat16
ALU = mybir.AluOpType
ACT = mybir.ActivationFunctionType
AX = mybir.AxisListType

P = 128
SEQ, D = 512, 1024
TB = SEQ // P
KC = D // P
MEM = 256
MB = MEM // P
DFF = 2816
FC = DFF // P
XA_HEADS = 4
DI = 2048
SSM_H, SSM_G, HPG = 32, 4, 8
HD, ROT = 64, 16
KV, QG = 4, 4
N_CMP, CMP = 31, 32
ALPHA = 2.0 ** 0.25
NEG = -1.0e30
LN_EPS = 1e-5
SOFTPLUS_MAX = 40.0


class Turns:

    def __init__(self):
        self.seen, self.turn, self.step = {}, None, {}

    def __call__(self, sem, n=1):
        self.seen[sem.name] = self.seen.get(sem.name, 0) + n
        value = self.seen[sem.name]
        if self.turn is not None:
            if sem.name not in self.step:
                raise ValueError(f"{sem.name}: no step per turn given")
            value = self.turn * self.step[sem.name] + value
        return value

    @contextmanager
    def loop(self, eng, count, steps):
        before = dict(self.seen)
        self.step = {s.name: n for s, n in steps.items()}
        with eng.Fori(0, count) as turn:
            self.turn = turn
            yield turn
            self.turn = None
        grown = {k: v - before.get(k, 0) for k, v in self.seen.items() if v != before.get(k, 0)}
        assert grown == {k: v for k, v in self.step.items() if v}, f"a turn waits for {grown}, given {self.step}"
        for k, v in grown.items():
            self.seen[k] = before.get(k, 0) + v * count
        self.step = {}


def shape_constants():
    p = np.arange(P)[:, None]
    f = np.arange(P)[None, :]
    upper = (p <= f).astype(np.float32)
    ones = np.ones((P, P), np.float32)
    return {
        "c_ident": np.eye(P, dtype=np.float32),
        "c_neg_suffix": -(p >= f).astype(np.float32),
        "c_causal6": np.concatenate([upper, ones, upper, upper, ones, upper], axis=1),
        "c_select": head_selections(),
        "c_rotary": rotary_tables(),
        "c_compressed": compressed_masks(),
    }


def swap(d):
    return d + ROT // 2 if d < ROT // 2 else d - ROT // 2


def head_selections():
    m = np.zeros((P, 5, P), np.float32)
    for half in range(2):
        for out_half in range(2):
            for d in range(HD):
                m[HD * half + d, half, HD * out_half + d] = 1
                if d < ROT:
                    m[HD * half + swap(d), 2 + half, HD * out_half + d] = 1
        for d in range(ROT):
            m[HD * half + swap(d), 4, HD * half + d] = 1
    return m.reshape(P, 5 * P)


def rotary_tables():
    half = ROT // 2
    inv = np.float32(500000.0) ** (-np.arange(half, dtype=np.float32) / np.float32(half))
    angle = np.arange(SEQ, dtype=np.float32)[:, None] * inv[None, :]
    cos, sin = np.cos(angle).T, np.sin(angle).T
    table = np.zeros((P, 2, SEQ), np.float32)
    table[:, 0] = 1
    for head in range(2):
        r = HD * head
        table[r:r + half, 0], table[r + half:r + ROT, 0] = cos, cos
        table[r:r + half, 1], table[r + half:r + ROT, 1] = sin, -sin
    return table.reshape(P, 2 * SEQ)


def compressed_masks():
    t = np.arange(SEQ).reshape(TB, P).T[:, :, None]
    c = np.arange(CMP)[None, None, :]
    mask = np.where((16 * c + 31 <= t) & (c < N_CMP), 0.0, NEG).astype(np.float32)
    same = (np.arange(P)[:, None] // CMP == np.arange(4)[None, :]).astype(np.float32)
    return np.concatenate([mask.reshape(P, TB * CMP), same], axis=1)


def param_rows(a):
    rows = lambda x: x.rearrange("(r c) -> r c", c=P)
    plan = [
        [("tap0", rows(a["ffn_conv"][0, 0, 0])), ("tap1", rows(a["ffn_conv"][0, 1, 0])),
         ("pre_mix", a["norm_pre_mix_2"].rearrange("l (r c) -> (l r) c", c=P)),
         ("pre_ffn", a["norm_pre_ffn_2"].rearrange("l (r c) -> (l r) c", c=P)), ("kv_norm", rows(a["kv_norm_2"]))],
        [("tap2", rows(a["ffn_conv"][0, 2, 0])), ("conv_b", rows(a["ffn_conv_b"][0])),
         ("ssm_conv_b", rows(a["ssm_conv_b_2"][0])), ("ssm_norm", rows(a["ssm_norm_2"][0]))],
        [("ssm_taps", a["ssm_conv_w_2"][0].rearrange("w (r c) -> (w r) c", c=P)), ("c", rows(a["c_2"][0])),
         ("cmp_pos_v", a["cmp_pos_v_2"].rearrange("(r two) d -> r (two d)", two=2))],
        [("mod_b", a["mod_b_2"].rearrange("l (r c) -> (l r) c", c=P)), ("kv_mod_b", rows(a["kv_mod_b_2"])),
         ("cmp_pos_k", a["cmp_pos_k_2"].rearrange("(r two) d -> r (two d)", two=2))],
    ]
    for tile, entries in enumerate(plan):
        row = 0
        for name, src in entries:
            yield tile, row, name, src
            row += src.shape[0]


N_PARAMS = 2 + 15
N_MOD = 2 * 48 + 16
NSA_PARAMS = 6
SET_UP = 5
FREE0 = 4
SLOTS = 2
HID0 = 2
DONE0 = 1
PAIRS0 = 2
TURNED0 = 4
QK_MODS = 4
MODS = 2
RMS_EPS = 1e-6


def build(nc, a, out):
    ctx = ExitStack()

    def sem(name):
        return ctx.enter_context(nc.semaphore(name))

    top = [16512]

    def place(name, shape, dt=F32, at=None):
        size = int(np.prod(shape[1:])) * (2 if dt == BF16 else 4)
        offset = top[0] if at is None else at
        if at is None:
            top[0] += -(-size // 32) * 32
        return nc.alloc_sbuf_tensor_at(name, shape, dt, offset=offset)

    raw = place("raw", [P, 2, 2048])
    whi = place("whi", [P, 2, 2048], F32R)
    wlo = place("wlo", [P, 2, 2048], F32R)
    ACTS = top[0]
    acth = place("acth", [P, KC, SEQ], F32R)
    actl = place("actl", [P, KC, SEQ], F32R)
    h = place("h", [P, TB, D])
    ident = place("ident", [P, P])
    ident_b = place("ident_b", [P, P], BF16)
    strict_b = place("strict_b", [P, P], BF16)
    causal_b = place("causal_b", [P, P], BF16)
    SUFFIX = top[0]
    neg_suffix = place("neg_suffix", [P, P])
    ONES = top[0]
    neg_ones = place("neg_ones", [P, P])
    norm_stats = place("norm_stats", [P, TB, 2, 6], at=ONES)
    norm_mv = place("norm_mv", [P, TB, 2], at=ONES + 192)
    norm_rstd = place("norm_rstd", [P, TB], at=ONES + 224)
    causal6 = place("causal6", [P, 6 * P])
    cols = place("cols", [P, 4 * P])
    stats = place("stats", [P, TB, 2, 6])
    mean_var = place("mean_var", [P, TB, 2])
    rstd = place("rstd", [P, TB])
    small = place("small", [P, 64])
    neg_half = place("neg_half", [P, 16])
    ones_c = place("ones_c", [P, 1])
    c_silu = place("c_silu", [P, KC])
    modv = place("modv", [P, N_MOD])
    gains = place("gains", [P, 5, KC])
    WIDE = top[0]
    gb = place("gb", [P, 2, D])
    conv_t = place("conv_t", [P, 4, SEQ], at=WIDE)
    ARENA = top[0]
    arena_end = 229368
    assert ARENA + 2 * FC * SEQ * 4 <= arena_end, (ARENA, arena_end)

    hid_h = place("hid_h", [P, FC, SEQ], F32R, at=ARENA)
    hid_l = place("hid_l", [P, FC, SEQ], F32R, at=ARENA + FC * SEQ * 4)

    o = ARENA
    q_t = place("q_t", [P, KC, SEQ], at=o); o += 16384
    k_t = place("k_t", [P, KC, SEQ], at=o); o += 16384
    v_s = place("v_s", [P, TB, D], at=o); o += 16384
    qst = place("qst", [P, 2, SEQ], at=o); o += 4096
    kst = place("kst", [P, 2, SEQ], at=o); o += 4096
    vst = place("vst", [P, 2, TB, P], at=o); o += 4096
    CAUSAL = 1280
    sp_e = place("sp_e", [P, 2, CAUSAL], at=o); o += 2 * CAUSAL * 4
    sp = place("sp", [P, 2, CAUSAL], at=o); o += 2 * CAUSAL * 4
    wts = place("wts", [P, 2, CAUSAL], at=o); o += 2 * CAUSAL * 4
    assert o <= arena_end, (o, arena_end)
    x_in = place("x_in", [P, 4, P], at=ARENA)
    o = ARENA + 69632
    mraw = place("mraw", [P, 2, KC, 256], at=o); o += 16384
    macc = place("macc", [P, 6, 256], at=o); o += 6144
    macc2 = place("macc2", [P, 2, 256], at=o); o += 2048
    assert o <= arena_end

    branch = place("branch", [P, TB, D], at=ACTS + 16384)
    branch_low = place("branch_low", [P, TB, D], at=ARENA)
    normed = place("normed", [P, TB, D], at=ARENA)
    modulated = place("modulated", [P, 2, SEQ], at=ARENA + 81920)
    gate_diag = place("gate_diag", [P, KC, P], at=WIDE)

    o = ARENA
    gate_z = place("gate_z", [P, TB, DI], at=o); o += 32768
    yh = place("yh", [P, DI // P, SEQ], F32R, at=o)
    yl = place("yl", [P, DI // P, SEQ], F32R, at=ACTS)
    tok = place("tok", [P, TB, DI + 512], at=o); o += 40960
    bct = place("bct", [P, 8, SEQ], at=o); o += 16384
    conv4 = place("conv4", [P, 4, SEQ], at=ARENA)
    state = place("state", [P, 512], at=o); o += 2048
    cbm = place("cbm", [P, 6 * P], at=o); o += 3072
    assert o <= arena_end, (o, arena_end)
    o = ACTS
    bst = place("bst", [P, SEQ], at=o); o += 2048
    cst = place("cst", [P, SEQ], at=o); o += 2048
    btk = place("btk", [P, 2, P], at=o); o += 1024
    xdt = place("xdt", [P, TB, 512], at=o); o += 8192
    xdt_tail = place("xdt_tail", [P, 2, 512], at=o); o += 4096
    decay = place("decay", [P, 2, 6 * P], at=o); o += 6144
    dx = place("dx", [P, TB, 512], at=o); o += 8192
    assert o <= ACTS + 32768
    wdt = place("wdt", [P, KC, SSM_H], at=WIDE + 8192 - 1024)
    o = WIDE
    dt = place("dt", [P, TB, SSM_H], at=o); o += 512
    dt_e = place("dt_e", [P, TB, SSM_H], at=o); o += 512
    dta = place("dta", [P, TB, SSM_H], at=o); o += 512
    acs = place("acs", [P, TB, SSM_H], at=o); o += 512
    eacs = place("eacs", [P, TB, SSM_H], at=o); o += 512
    tail = place("tail", [P, 2, SSM_H], at=o); o += 256
    heads = place("heads", [P, 3, SSM_H], at=o); o += 384
    dtag = place("dtag", [P, TB, HPG], at=o); o += 128
    acsg = place("acsg", [P, TB, HPG], at=o); o += 128
    gstats = place("gstats", [P, TB, SSM_G, 6], at=o); o += 384
    gmv = place("gmv", [P, TB * SSM_G, 2], at=o); o += 128
    ginv = place("ginv", [P, TB * SSM_G], at=o); o += 64
    assert o <= WIDE + 4096
    wdt_h = place("wdt_h", [P, KC, SSM_H], F32R, at=WIDE + 4096)
    wdt_l = place("wdt_l", [P, KC, SSM_H], F32R, at=WIDE + 5120)
    dt_t = place("dt_t", [P, SEQ], at=WIDE + 6144)

    o = ARENA
    mem_t = place("mem_t", [P, MB, D], at=o); o += 8192
    memh = place("memh", [P, KC, MEM], F32R, at=o); o += 8192
    meml = place("meml", [P, KC, MEM], F32R, at=o); o += 8192
    kx = place("kx", [P, KC, MEM], at=o); o += 8192
    vx = place("vx", [P, MB, D], at=o); o += 8192
    qx = place("qx", [P, KC, SEQ], at=o); o += 16384
    px = place("px", [P, 2, TB, MEM], at=o); o += 8192
    pxt = place("pxt", [P, MB, SEQ], at=o); o += 4096

    o = ARENA
    pn = place("pn", [P, 2, CAUSAL], at=o)
    pnt_h = place("pnt_h", [P, CAUSAL], F32R, at=o + 2 * CAUSAL * 4); o += 16384
    kv8 = place("kv8", [P, 8, SEQ], at=o)
    q_u = place("q_u", [P, KC, SEQ], at=o)
    q_st = place("q_st", [P, QG, SEQ], F32R, at=o)
    v_st = place("v_st", [P, 2, TB, 2, 2, HD], F32R, at=o + 8192); o += 16384
    kdup_h = place("kdup_h", [P, 2 * KV, SEQ], F32R, at=o); o += 16384
    kcp = place("kcp", [P, 2, 16, KV * N_CMP], at=o)
    kdup_l = place("kdup_l", [P, 2 * KV, SEQ], F32R, at=o); o += 16384
    v_hl = place("v_hl", [P, 2, TB, 2 * KV * HD], F32R, at=o)
    v_h, v_l = v_hl[:, 0], v_hl[:, 1]
    o += 16384
    rot_t = place("rot_t", [P, 2, 2, SEQ], at=o)
    pc = place("pc", [P, TB, 4 * QG, CMP], at=o)
    diag = place("diag", [P, 2, TB, P], at=o)
    vb_g = place("vb_g", [P, QG * HD], at=o + 4096); o += 8192
    pnt_l = place("pnt_l", [P, CAUSAL], F32R, at=o - 3072)
    select = place("select", [P, 5, P], at=o); o += 2560
    hid_v = place("hid_v", [P, 2, KV, QG, CMP], at=o)
    vbd = place("vbd", [P, KV, QG * HD], at=o); o += 4096
    gates = place("gates", [P, TB, 48], at=o); o += 768
    nst = place("nst", [P, 2, 4, TB], at=o); o += 128
    assert o <= arena_end, (o, arena_end)
    kcph = place("kcph", [P, 2, 16, KV * N_CMP], F32R, at=ACTS)
    kcpl = place("kcpl", [P, 2, 16, KV * N_CMP], F32R, at=ACTS + 16384)
    rotary = place("rotary", [P, 2, SEQ], at=WIDE)
    rotary_q = place("rotary_q", [P, 2, SEQ], at=ARENA)
    w_gate_h = place("w_gate_h", [P, KC, 48], F32R, at=WIDE)
    w_gate_l = place("w_gate_l", [P, KC, 48], F32R, at=WIDE + 1536)
    gates_t = place("gates_t", [P, SEQ], at=WIDE + 3072)
    pct = place("pct", [P, KV, SEQ], at=WIDE)
    hid_k = place("hid_k", [P, 2, KV, CMP], at=WIDE + 4096)
    w2v = place("w2v", [P, 2, HD], at=WIDE + 5120)
    w_gate = place("w_gate", [P, KC, 48], at=WIDE + 4096)
    cmp_mask = place("cmp_mask", [P, TB * CMP + QG], at=WIDE + 6144)
    w2k = place("w2k", [P, 2, 2, HD], at=WIDE + 7168)
    cst2 = place("cst2", [P, 4, TB * 4 * QG], at=WIDE + 7168)
    kcmp = place("kcmp", [P, KV, CMP], at=SUFFIX)
    T_STRIPS = {3: 0, 2: 512, 0: 896, 1: 1024}

    def query_head(n):
        return (n // 2) ^ 1

    ROUNDS = ([(0, t) for t in range(4)], [(1, 1), (1, 2), (1, 3), (3, 3)], [(2, 2), (2, 3)])
    S_STRIPS = {0: 0, 1: 512, 3: 896, 2: 1024}

    ps = ctx.enter_context(nc.psum_tensor("ps", [P, 8, 512], F32))

    raw_full = [sem("raw_full0"), sem("raw_full1")]
    hi_ready = sem("hi_ready")
    unit_ready = sem("unit_ready")
    marks = sem("marks")
    bank_free = sem("bank_free")
    params = sem("params")
    mem_in = sem("mem_in")
    ident_in = sem("ident_in")
    x_loaded = [sem(f"x_loaded{t}") for t in range(TB)]
    gb_in = sem("gb_in")
    turned = sem("turned")
    shaped = sem("shaped")
    turned_hi = sem("turned_hi")
    turned_free = sem("turned_free")
    set_up = sem("set_up")
    dve_step = sem("dve_step")
    act_step = sem("act_step")
    h_sum = sem("h_sum")
    norm_moments = sem("norm_moments")
    norm_root = sem("norm_root")
    moments = sem("moments")
    rstd_ready = sem("rstd_ready")
    h_ready = sem("h_ready")
    evac_hi = sem("evac_hi")
    staged = sem("staged")
    z_ready = sem("z_ready")
    capped = sem("capped")
    log_ready = sem("log_ready")
    sp_ready = sem("sp_ready")
    logw_ready = sem("logw_ready")
    w_ready = sem("w_ready")
    o_ready = sem("o_ready")
    o_free = sem("o_free")
    mod_raw = [sem("mod_raw0"), sem("mod_raw1")]
    mod_acc = sem("mod_acc")
    mod_step = sem("mod_step")
    mod_cols = sem("mod_cols")
    mod_done = sem("mod_done")
    c_ready = sem("c_ready")
    diag_ready = sem("diag_ready")
    gate_rows = sem("gate_rows")
    branch_out = sem("branch_out")
    normed_ready = sem("normed_ready")
    
    convolved = sem("convolved")
    tok_turned = sem("tok_turned")
    tok_free = sem("tok_free")
    bc_copied = sem("bc_copied")
    wdt_in = sem("wdt_in")
    wdt_hi = sem("wdt_hi")
    wdt_lo = sem("wdt_lo")
    dt_raw = sem("dt_raw")
    dt_kept = sem("dt_kept")
    dt_turned = sem("dt_turned")
    dt_cap = sem("dt_cap")
    dt_log = sem("dt_log")
    dta_ready = sem("dta_ready")
    acs_ready = sem("acs_ready")
    acs_out = sem("acs_out")
    tail_ready = sem("tail_ready")
    group_in = sem("group_in")
    heads_staged = sem("heads_staged")
    xdt_ready = sem("xdt_ready")
    cb_ready = sem("cb_ready")
    cb_out = sem("cb_out")
    acs_rows = sem("acs_rows")
    decay_arg = sem("decay_arg")
    decay_exp = sem("decay_exp")
    mixed = sem("mixed")
    head_y = sem("head_y")
    group_y = sem("group_y")
    heads_in = sem("heads_in")
    a_ready = sem("a_ready")
    dx_ready = sem("dx_ready")
    pool_step = sem("pool_step")
    out_done = sem("out_done")

    nsa_in = sem("nsa_in")
    dup_ready = sem("dup_ready")
    dup_free = sem("dup_free")
    hid_padded = sem("hid_padded")
    blocks_hi = sem("blocks_hi")
    blocks_lo = sem("blocks_lo")
    rot_in = sem("rot_in")
    rot_ready = sem("rot_ready")
    rot_free = sem("rot_free")
    cmp_ready = sem("cmp_ready")
    cmp_kept = sem("cmp_kept")
    gates_raw = sem("gates_raw")
    gates_ready = sem("gates_ready")
    v_hi = sem("v_hi")
    rot_hi = sem("rot_hi")
    gate_w = sem("gate_w")
    rotary_in = sem("rotary_in")
    gate_hi = sem("gate_hi")
    gate_lo = sem("gate_lo")
    gates_kept = sem("gates_kept")
    gates_turned = sem("gates_turned")
    c_scores = sem("c_scores")
    c_args = sem("c_args")
    c_exps = sem("c_exps")
    c_probs = sem("c_probs")
    c_turned = sem("c_turned")
    c_copied = sem("c_copied")
    q_in = [sem("q_in0"), sem("q_in1")]
    v_in = sem("v_in")
    n_scores = sem("n_scores")
    n_max = sem("n_max")
    n_exps = sem("n_exps")
    n_fac = sem("n_fac")
    n_diag = sem("n_diag")
    n_turned = sem("n_turned")
    n_hi = sem("n_hi")
    n_lo = sem("n_lo")
    n_outs = sem("n_outs")
    n_out_hi = sem("n_out_hi")
    n_taken = sem("n_taken")

    scores = sem("scores")
    score_max = sem("score_max")
    probs = sem("probs")
    probs_normed = sem("probs_normed")
    probs_turned = sem("probs_turned")
    probs_copied = sem("probs_copied")
    heads_out = sem("heads_out")
    heads_free = sem("heads_free")
    taps = sem("taps")
    conv_done = sem("conv_done")
    gated = sem("gated")
    hid_value = sem("hid_value")
    hid_ready = sem("hid_ready")

    C_CW = 0
    C_PRE_MIX, C_PRE_FFN, C_KVN = 88, 104, 120
    C_CW2, C_CB = 128, 172
    C_SCB, C_SNORM = 216, 240
    C_SCW, C_C = 256, 352
    C_MODB = 384
    C_POS = (496, 360)

    def feature_units(w, c0):
        v = w.rearrange("(k p) c -> p k c", p=P)
        return lambda i: v[:, :, bass.ds(c0 + 256 * i, 256)]

    def token_units(w, c0, k0, nk):
        v = w.rearrange("(k p) c -> p k c", p=P)
        return lambda i: v[:, k0:k0 + nk, bass.ds(c0 + 512 * i, 512)]

    def strip(sb):
        bank, c0 = [(0, 0), (1, 0), (2, 0), (1, 384)][sb]
        return bank, c0, [0, 512, 896, 1152][sb], SEQ - P * sb

    engines = ExitStack()
    block = engines.enter_context(nc.Block())

    @block.sync
    def _(sp_q):
        turns = Turns()
        parity = [0]

        def load(source, n=2048):
            slot = parity[0] % 2
            parity[0] += 1
            sp_q.wait_ge(unit_ready, turns(unit_ready))
            k = source.shape[1]
            sp_q.dma_start(raw[:, slot, 0:n].rearrange("p (k c) -> p k c", k=k), source) \
                .then_inc(raw_full[slot], 16)

        def feature_loads(pairs, w, c0):
            with turns.loop(sp_q, pairs, {unit_ready: 2}) as i:
                for u in range(2):
                    load(feature_units(w, c0)(2 * i + u))

        def token_loads(halves, w, c0, kc=KC):
            units = -(-kc // 4)
            with turns.loop(sp_q, halves, {unit_ready: units}) as i:
                for u in range(units):
                    nk = min(4, kc - 4 * u)
                    load(token_units(w, c0, 4 * u, nk)(i), n=nk * 512)

        def ffn_loads(w_up, w_down):
            with turns.loop(sp_q, FC // 2, {unit_ready: 2}) as i:
                load(feature_units(w_up, 0)(i))
                load(feature_units(w_up, DFF)(i))
            token_loads(2, w_down, 0, FC)

        def ffn2_loads(layer):
            ffn_loads(a["ffn_w_in_2"][layer], a["ffn_w_out_2"][layer])

        def program():
            feature_loads(4, a["sb_win"][0], 0)
            token_loads(2, a["sb_win"][0], 2 * D)
            feature_loads(2, a["xa_wkv"][0], 0)
            token_loads(2, a["xa_wkv"][0], D)
            token_loads(2, a["mix_wo"][0], 0)
            feature_loads(2, a["xa_wq"][0], 0)
            token_loads(2, a["xa_wo"][0], 0)
            ffn_loads(a["ffn_up"][0], a["ffn_down"][0])
            ssm_w = a["ssm_w_in_2"][0]
            feature_loads(4, ssm_w, DI)
            feature_loads(1, ssm_w, 2 * DI)
            feature_loads(1, ssm_w, 2 * DI + 512)
            token_loads(4, ssm_w, 0)
            token_loads(2, a["ssm_w_out_2"][0], 0, DI // P)
            ffn2_loads(0)
            w_kv = a["w_kv_2"].rearrange("(k p) c -> p k c", p=P)
            with turns.loop(sp_q, 2, {unit_ready: 2}) as i:
                load(w_kv[:, :, bass.ds(512 * i, 256)])
                load(w_kv[:, :, bass.ds(768 * i + 256, 256)])
            load(w_kv[:, :, 768:1024])
            load(w_kv[:, :, 1280:1536])
            for w1 in (a["cmp_w1_k_2"], a["cmp_w1_v_2"]):
                for u in range(2):
                    load(w1.rearrange("(k p) c -> p k c", p=P)[:, KC * u:KC * u + KC, :])
            feature_loads(2, a["nsa_w_q_2"][0], 0)
            token_loads(2, a["nsa_w_o_2"][0], 0)
            sp_q.wait_ge(rot_free, 2 * KV + KC)
            with turns.loop(sp_q, KV, {n_taken: 2}) as g:
                for pair in range(2):
                    sp_q.wait_ge(n_taken, turns(n_taken))
                    for side in range(2):
                        for part, x in enumerate((acth, actl)):
                            sp_q.dma_start(q_st[HD * part:HD * part + HD, 2 * pair + side, :].bitcast(F32),
                                           x[HD * side:HD * side + HD, 2 * g + pair, :].bitcast(F32)) \
                                .then_inc(q_in[pair], 16)
            ffn2_loads(1)
        x_blocks = a["x"].rearrange("a (t p) c -> p (a t) c", p=P)
        for t in range(TB):
            sp_q.dma_start(h[:, t, :], x_blocks[:, t, :]).then_inc(x_loaded[t], 16)
        program()
        for t in range(TB):
            sp_q.wait_ge(h_ready, 6 * TB + t + 1)
            sp_q.dma_start(out.rearrange("a (t p) c -> p (a t) c", p=P)[:, t, :], h[:, t, :]).then_inc(out_done, 16)
        sp_q.wait_ge(out_done, 16 * TB)

    @block.tensor
    def _(pe):
        turns = Turns()

        def product3(o, lh, ll, rh, rl, start, stop):
            nc.tensor.matmul(o, ll, rh, start=start, stop=False, skip_group_check=True)
            nc.tensor.matmul(o, lh, rl, start=False, stop=False, skip_group_check=True)
            return nc.tensor.matmul(o, lh, rh, start=False, stop=stop, skip_group_check=True)

        def banks_out(free=bank_free):
            pe.wait_ge(free, turns.seen.get(free.name, 0) + FREE0)

        mods_behind = [0]

        def turns_out():
            if mods_behind[0]:
                pe.wait_ge(mod_done, turns(mod_done, mods_behind[0]))
                mods_behind[0] = 0
            pe.wait_ge(turned_free, turns.seen.get("turned_free", 0) + 4)

        def feature_pairs(pairs, ah, al, n=SEQ, free=bank_free, mods=0, after=None, extra={}):
            banks_out()
            with turns.loop(pe, pairs, {unit_ready: 2, free: 4, mod_acc: mods} | extra):
                for u in range(2):
                    pe.wait_ge(unit_ready, SLOTS + turns(unit_ready))
                    wh = whi[:, u, :].rearrange("p (k c) -> p k c", k=KC)
                    wl = wlo[:, u, :].rearrange("p (k c) -> p k c", k=KC)
                    for j in range(2):
                        pe.wait_ge(free, turns(free))
                        for k in range(KC):
                            c = slice(P * j, P * j + P)
                            last = product3(ps[:, 2 * u + j, 0:n], wh[:, k, c], wl[:, k, c], ah[:, k, 0:n],
                                            al[:, k, 0:n], k == 0, k == KC - 1)
                        last.then_inc(marks, 1)
                if mods:
                    mod_columns(mods)
                if after:
                    after()
            mods_behind[0] += pairs if mods else 0
            if free is not bank_free:
                banks_out(free)

        def token_half(ah, al, kc, nt, free):
            units = -(-kc // 4)
            for u in range(units):
                pe.wait_ge(unit_ready, SLOTS + turns(unit_ready))
                wh = whi[:, u % 2, :].rearrange("p (k c) -> p k c", c=512)
                wl = wlo[:, u % 2, :].rearrange("p (k c) -> p k c", c=512)
                nk = min(4, kc - 4 * u)
                for t in range(nt):
                    if u == 0:
                        pe.wait_ge(free, turns(free) + FREE0 - nt)
                    c = slice(P * t, P * t + P)
                    for k in range(nk):
                        final = u == units - 1 and k == nk - 1
                        last = product3(ps[:, t, :], ah[:, 4 * u + k, c], al[:, 4 * u + k, c], wh[:, k, :],
                                        wl[:, k, :], u == 0 and k == 0, final)
                    if u == units - 1:
                        last.then_inc(marks, 1)
                if u < units - 1:
                    last.then_inc(marks, 1)

        def token_pairs(halves, ah, al, kc=KC, nt=TB, mods=0, free=bank_free):
            banks_out()
            with turns.loop(pe, halves, {unit_ready: -(-kc // 4), free: nt, mod_acc: mods}):
                token_half(ah, al, kc, nt, free)
                if mods:
                    mod_columns(mods)
            mods_behind[0] += halves if mods else 0
            if free is not bank_free:
                banks_out(free)

        def mod_columns(units):
            for u in range(units):
                pe.wait_ge(mod_acc, MODS + turns(mod_acc))
                for j in range(2):
                    last = nc.tensor.matmul(ps[:, 6, 2 * u + j:2 * u + j + 1], macc[:, u, P * j:P * j + P], ones_c[:],
                                            start=True, stop=True, skip_group_check=True)
            last.then_inc(mod_cols, 1)

        def to_features(src, blocks=TB, chunks=KC, ready=None):
            for t in range(blocks):
                if ready is not None:
                    if isinstance(ready, list):
                        pe.wait_ge(ready[t], 16)
                    else:
                        pe.wait_ge(ready, turns(ready))
                for j in range(chunks // 4):
                    pe.wait_ge(turned_free, turns(turned_free))
                    bank = 4 + (t * (chunks // 4) + j) % 4
                    for c in range(4):
                        last = nc.tensor.transpose(ps[:, bank, P * c:P * c + P],
                                                   src[:, t, P * (4 * j + c):P * (4 * j + c) + P], ident[:])
                    last.then_inc(turned, 1)

        def stick_breaking():
            banks_out()
            turns_out()
            with turns.loop(pe, 4, {staged: 6, w_ready: 12, sp_ready: 4, o_free: 2}):
                for pair in range(2):
                    pe.wait_ge(staged, turns(staged, 3))
                    for hd in range(2):
                        half = slice(64 * hd, 64 * hd + 64)
                        for sb in (0, 1, 3, 2):
                            bank, c0, _, n = strip(sb)
                            nc.tensor.matmul(ps[:, 3 * hd + bank, c0:c0 + n], kst[half, pair, P * sb:P * sb + P],
                                             qst[half, pair, P * sb:SEQ], start=sb != 3, stop=False,
                                             skip_group_check=True)
                            last = nc.tensor.matmul(ps[:, 3 * hd + bank, c0:c0 + P], ident_b[:], strict_b[:],
                                                    start=False, stop=False, skip_group_check=True)
                            if sb != 1:
                                last.then_inc(z_ready, 1)
                    for hd in range(2):
                        pe.wait_ge(sp_ready, turns(sp_ready))
                        for sb in (2, 3, 1, 0):
                            bank, c0, _, n = strip(sb)
                            for j in range(sb, TB):
                                _, _, offj, nj = strip(j)
                                last = nc.tensor.matmul(ps[:, 3 * hd + bank, c0 + n - nj:c0 + n],
                                                        (neg_suffix if j == sb else neg_ones)[:],
                                                        sp[:, hd, offj:offj + nj],
                                                        start=False, stop=j == TB - 1, skip_group_check=True)
                            if sb != 3:
                                last.then_inc(logw_ready, 1)
                    pe.wait_ge(o_free, turns(o_free))
                    for hd in range(2):
                        half = slice(64 * hd, 64 * hd + 64)
                        pe.wait_ge(w_ready, turns(w_ready, 3))
                        for sb in range(TB):
                            _, _, off, n = strip(sb)
                            last = nc.tensor.matmul(ps[half, 6 + pair, P * sb:SEQ], vst[:, pair, sb, half],
                                                    wts[:, hd, off:off + n], start=sb == 0, stop=sb == TB - 1,
                                                    skip_group_check=True)
                    last.then_inc(o_ready, 1)
            pe.wait_ge(o_free, turns.seen["o_free"] + 2)

        def cross_attention():
            banks_out()
            turns_out()

            def head_scores(hd):
                for t in range(TB):
                    bank = 2 * (hd % 2) + t // 2
                    if t % 2 == 0 and hd >= 2:
                        pe.wait_ge(probs, 4 * (hd - 1))
                    for c in range(2):
                        last = nc.tensor.matmul(ps[:, bank, MEM * (t % 2):MEM * (t % 2) + MEM],
                                                qx[:, 2 * hd + c, P * t:P * t + P], kx[:, 2 * hd + c, :],
                                                start=t % 2 == 0 and c == 0, stop=c == 1, skip_group_check=True)
                    if t % 2:
                        last.then_inc(scores, 1)

            head_scores(0)
            for hd in range(XA_HEADS):
                if hd + 1 < XA_HEADS:
                    head_scores(hd + 1)
                pe.wait_ge(probs_normed, hd + 1)
                if hd:
                    pe.wait_ge(probs_copied, 2 * hd)
                for m in range(MB):
                    for t in range(TB):
                        last = nc.tensor.transpose(ps[:, 4 + m, P * t:P * t + P], px[:, hd % 2, t, P * m:P * m + P],
                                                   ident[:])
                    last.then_inc(probs_turned, 1)
                for c in range(2):
                    pe.wait_ge(probs_copied, 2 * hd + 2)
                    if hd:
                        pe.wait_ge(heads_free, 2 * hd - 1 + c)
                    for m in range(MB):
                        last = nc.tensor.matmul(ps[:, 6 + c, :], vx[:, m, 256 * hd + P * c:256 * hd + P * c + P],
                                                pxt[:, m, :], start=m == 0, stop=m == MB - 1)
                    last.then_inc(heads_out, 1)
            pe.wait_ge(heads_free, 8)

        def gate_rows_of():
            turns_out()
            pe.wait_ge(diag_ready, turns(diag_ready))
            for half in range(2):
                last = nc.tensor.matmul(ps[:, 4 + half, :], causal6[:, P:2 * P],
                                        gate_diag[:, 4 * half:4 * half + 4, :], start=True, stop=True)
            last.then_inc(gate_rows, 1)

        def normed_to_features():
            turns_out()
            to_features(normed, ready=normed_ready)
            turns_out()

        def gated_ffn():
            banks_out()
            with turns.loop(pe, FC // 2, {unit_ready: 2, hid_value: 2}):
                for u in range(2):
                    pe.wait_ge(unit_ready, SLOTS + turns(unit_ready))
                    wh = whi[:, u, :].rearrange("p (k c) -> p k c", k=KC)
                    wl = wlo[:, u, :].rearrange("p (k c) -> p k c", k=KC)
                    for j in range(2):
                        if u == 0:
                            pe.wait_ge(hid_value, turns(hid_value) - 2 + HID0)
                        for k in range(KC):
                            c = slice(P * j, P * j + P)
                            last = product3(ps[:, 2 * u + j, :], wh[:, k, c], wl[:, k, c], acth[:, k, :],
                                            actl[:, k, :], k == 0, k == KC - 1)
                        last.then_inc(marks, 1)
            gate_rows_of()
            pe.wait_ge(hid_ready, turns(hid_ready, FC))
            token_pairs(2, hid_h, hid_l, FC, free=branch_out)

        def value_units():
            for u in range(2):
                pe.wait_ge(unit_ready, SLOTS + turns(unit_ready))
                wh = whi[:, u, :].rearrange("p (k c) -> p k c", k=KC)
                wl = wlo[:, u, :].rearrange("p (k c) -> p k c", k=KC)
                for t in range(TB):
                    if u == 0:
                        pe.wait_ge(bank_free, turns(bank_free))
                    c = slice(P * t, P * t + P)
                    for k in range(KC):
                        last = product3(ps[:, t, 256 * u:256 * u + 256], acth[:, k, c], actl[:, k, c], wh[:, k, :],
                                        wl[:, k, :], u == 0 and k == 0, k == KC - 1)
                    if u == 1 or t == TB - 1:
                        last.then_inc(marks, 1)

        rotated = [0]

        def rotate(chunks, mats):
            for c in range(chunks):
                pe.wait_ge(rot_in, turns(rot_in, 2))
                for keep, move in mats:
                    if rotated[0] >= 4:
                        pe.wait_ge(rot_free, rotated[0] - 3)
                    o = ps[:, 4 + rotated[0] % 4, :]
                    nc.tensor.matmul(o, keep, rot_t[:, c % 2, 0, :], start=True, stop=False)
                    nc.tensor.matmul(o, move, rot_t[:, c % 2, 1, :], start=False, stop=True).then_inc(rot_ready, 1)
                    rotated[0] += 1

        def compression():
            for n in range(2 * KV):
                if n >= 4:
                    pe.wait_ge(dup_free, n - 3)
                nc.tensor.matmul(ps[:, 4 + n % 4, :], select[:, n % 2, :], kv8[:, n // 2, :], start=True, stop=True) \
                    .then_inc(dup_ready, 1)
            pe.wait_ge(dup_free, 2 * KV)
            rotate(4, [(select[:, half, :], select[:, 2 + half, :]) for half in range(2)])
            banks_out()
            for w in range(2):
                pe.wait_ge(blocks_lo, w + 1)
                for u in range(2):
                    pe.wait_ge(unit_ready, SLOTS + turns(unit_ready))
                    wh = whi[:, u, :].rearrange("p (k c) -> p k c", k=KC)
                    wl = wlo[:, u, :].rearrange("p (k c) -> p k c", k=KC)
                    for j in range(2):
                        for k in range(KC):
                            c = slice(P * j, P * j + P)
                            last = product3(ps[:, 2 * w + j, 0:KV * N_CMP], wh[:, k, c], wl[:, k, c],
                                            kcph[:, w, KC * u + k, :], kcpl[:, w, KC * u + k, :],
                                            u == 0 and k == 0, u == 1 and k == KC - 1)
                        if u == 1 or j == 1:
                            last.then_inc(marks, 1)
            turns(bank_free, 4)
            banks_out()
            pe.wait_ge(rot_free, rotated[0])
            for c in range(2):
                nc.tensor.matmul(ps[:, 4, 0:P], w2k[:, c, :, :], hid_k[:, c, :, :], start=c == 0, stop=c == 1)
            for g in range(KV):
                for c in range(2):
                    last = nc.tensor.matmul(ps[:, 5, HD * g:HD * g + HD],
                                            hid_v[:, c, g, :, :], w2v[:, c, :],
                                            start=g == 0 and c == 0, stop=c == 1, skip_group_check=True)
            last.then_inc(cmp_ready, 1)
            pe.wait_ge(cmp_kept, 1)

        def branch_gates():
            pe.wait_ge(gate_lo, 1)
            for k in range(KC):
                last = product3(ps[0:48, 4, :], w_gate_h[:, k, :], w_gate_l[:, k, :], acth[:, k, :], actl[:, k, :],
                                k == 0, k == KC - 1)
            last.then_inc(gates_raw, 1)
            pe.wait_ge(gates_kept, 1)
            for t in range(TB):
                last = nc.tensor.transpose(ps[:, 5, 48 * t:48 * t + 48], gates_t[0:48, P * t:P * t + P],
                                           ident[0:48, 0:48])
            last.then_inc(gates_turned, 1)

        def compressed_weights():
            for side in range(2):
                half = slice(HD * side, HD * side + HD)
                for tb in range(TB):
                    for c in range(KC):
                        c0 = CMP * (KC * (tb % 2) + c)
                        last = nc.tensor.matmul(ps[:, 2 * side + tb // 2, c0:c0 + CMP],
                                                q_u[half, c, P * tb:P * tb + P], kcmp[half, c // 2, :],
                                                start=tb % 2 == 0 and c == 0, stop=True, skip_group_check=True)
            last.then_inc(c_scores, 1)

        def turn_compressed():
            pe.wait_ge(c_probs, 1)
            for g in range(KV):
                for tb in range(TB):
                    last = nc.tensor.transpose(ps[:, 4 + g, P * tb:P * tb + P], pc[:, tb, QG * g:QG * g + QG, :],
                                               ident[:])
                last.then_inc(c_turned, 1)
            pe.wait_ge(c_copied, KV)

        def nsa_attention():
            def job_scores(n, g):
                hd, w = query_head(n), n % 2
                for tb in T_STRIPS:
                    if n:
                        pe.wait_ge(n_exps, turns(n_exps))
                    for part, k in enumerate((kdup_l, kdup_h)):
                        nc.tensor.matmul(ps[:, tb, 0:P * tb + P], q_st[:, hd, P * tb:P * tb + P],
                                         k[:, KV * w + g, 0:P * tb + P], start=part == 0, stop=False,
                                         skip_group_check=True)
                    nc.tensor.matmul(ps[:, tb, P * tb:P * tb + P], ident_b[:], causal_b[:], start=False, stop=True,
                                     skip_group_check=True).then_inc(n_scores, 1)

            def job_outputs(n):
                hd, w, pair = query_head(n), n % 2, n // 4
                pe.wait_ge(n_lo, turns(n_lo, 3))
                rows = HD * (1 + hd % 2)
                for sb, off in S_STRIPS.items():
                    m = SEQ - P * sb
                    v = [v_st[:, part, sb, w, :, :].rearrange("p z c -> p (z c)")[:, 2 * HD - rows:]
                         for part in range(2)]
                    product3(ps[0:rows, 6 + pair, P * sb:SEQ], *v, pnt_h[:, off:off + m], pnt_l[:, off:off + m],
                             n % 4 == 0 and sb == 0, False)

            def pair_outputs(pair, g):
                nc.tensor.matmul(ps[:, 6 + pair, :], vb_g[:, P * pair:P * pair + P], pct[:, g, :], start=False,
                                 stop=True, skip_group_check=True).then_inc(n_outs, 1)

            with turns.loop(pe, KV, {q_in[0]: 64, q_in[1]: 64, v_in: 2, n_exps: 32, n_diag: 8, n_lo: 24,
                                     n_taken: 2}) as g:
                pe.wait_ge(q_in[0], turns(q_in[0], 64))
                job_scores(0, g)
                for n in range(2 * QG):
                    if n + 1 == QG:
                        pe.wait_ge(q_in[1], turns(q_in[1], 64))
                    if n + 1 < 2 * QG:
                        job_scores(n + 1, g)
                    else:
                        pe.wait_ge(n_exps, turns(n_exps, 4))
                    if n == 1:
                        pe.wait_ge(v_in, turns(v_in, 2))
                        pe.wait_ge(n_taken, turns(n_taken))
                    if n == QG + 1:
                        pe.wait_ge(n_taken, turns(n_taken))
                    if n:
                        job_outputs(n - 1)
                    if n == QG:
                        pair_outputs(0, g)
                    pe.wait_ge(n_diag, turns(n_diag))
                    for r, blocks in enumerate(ROUNDS):
                        if r == 2:
                            pe.wait_ge(n_lo, turns.turn * 24 + turns.seen.get("n_lo", 0) + 1)
                        for b, (sb, tb) in enumerate(blocks):
                            off = T_STRIPS[tb] + P * sb
                            last = nc.tensor.matmul(ps[:, 4 + (3 * n + r) % 2, P * b:P * b + P],
                                                    pn[:, n % 2, off:off + P], diag[:, n % 2, tb, :], start=b == 0,
                                                    stop=True, skip_group_check=True)
                        last.then_inc(n_turned, 1)
                job_outputs(2 * QG - 1)
                pair_outputs(1, g)
            pe.wait_ge(n_taken, PAIRS0 + 2 * KV)

        def turn_chunks():
            for j in range(4):
                pe.wait_ge(convolved, turns(convolved))
                pe.wait_ge(tok_free, turns(tok_free))
                for t in range(TB):
                    last = nc.tensor.transpose(ps[:, 4 + j, P * t:P * t + P], conv4[:, j, P * t:P * t + P], ident[:])
                last.then_inc(tok_turned, 1)

        def dt_and_sums():
            pe.wait_ge(wdt_lo, 1)
            pe.wait_ge(tok_free, turns.seen["tok_free"] + 4)
            for k in range(KC):
                last = product3(ps[0:SSM_H, 4, :], wdt_h[:, k, :], wdt_l[:, k, :], acth[:, k, :], actl[:, k, :],
                                k == 0, k == KC - 1)
            last.then_inc(dt_raw, 1)
            pe.wait_ge(dt_kept, 1)
            for t in range(TB):
                last = nc.tensor.transpose(ps[:, 6, SSM_H * t:SSM_H * t + SSM_H], dt_t[0:SSM_H, P * t:P * t + P],
                                           ident[0:SSM_H, 0:SSM_H])
            last.then_inc(dt_turned, 1)
            pe.wait_ge(dta_ready, 1)
            upper, ones = causal6[:, 0:P], causal6[:, P:2 * P]
            for t in range(TB):
                o = ps[:, 5, SSM_H * t:SSM_H * t + SSM_H]
                if t % 2:
                    nc.tensor.matmul(o, ones, dta[:, t - 1, :], start=True, stop=False, skip_group_check=True)
                nc.tensor.matmul(o, upper, dta[:, t, :], start=t % 2 == 0, stop=True, skip_group_check=True)
            for t in range(2):
                last = nc.tensor.matmul(ps[:, 5, P:P + SSM_H], ones, dta[:, t, :], start=t == 0, stop=t == 1,
                                        skip_group_check=True)
            last.then_inc(acs_ready, 1)

        def scan():
            segs = [(0, 0, 256), (1, 256, 128), (2, 384, 256), (3, 640, 128)]

            def sum_rows(hd):
                bank = 6 + hd % 2
                for ch in range(2):
                    for b in range(2):
                        last = nc.tensor.matmul(ps[:, bank, 256 * ch + P * b:256 * ch + 256],
                                                dtag[:, 2 * ch + b, hd:hd + 1].to_broadcast([P, P]),
                                                causal6[:, 0:256 - P * b], start=ch == 0 and b == 0, stop=b == 1,
                                                skip_group_check=True)
                last.then_inc(acs_rows, 1)

            pe.wait_ge(acs_out, 1)
            with turns.loop(pe, SSM_G, {group_in: 3, heads_staged: 2, xdt_ready: 1, cb_out: 1, decay_arg: 8, mixed: 8,
                                        group_y: 1}):
                pe.wait_ge(group_in, turns(group_in, 3))
                pe.wait_ge(group_y, turns(group_y) - 1 + DONE0)
                for ch in range(2):
                    for b in range(2):
                        nc.tensor.matmul(ps[:, 6 + ch, 256 * b:256 * b + 256 - P * b],
                                         bst[:, 256 * ch + P * b:256 * ch + P * b + P],
                                         cst[:, 256 * ch + P * b:256 * ch + 256], start=b == 0, stop=True,
                                         skip_group_check=True)
                pe.wait_ge(xdt_ready, turns(xdt_ready))
                for t in range(2):
                    last = nc.tensor.matmul(ps[:, 5, :], btk[:, t, :], xdt_tail[:, t, :], start=t == 0, stop=t == 1)
                last.then_inc(cb_ready, 1)
                pe.wait_ge(cb_out, turns(cb_out))
                for t in range(2):
                    nc.tensor.matmul(ps[:, 4 + t, :], cst[:, 256 + P * t:384 + P * t], state[:], start=True, stop=True)
                pe.wait_ge(heads_staged, turns(heads_staged, 2))
                sum_rows(0)
                sum_rows(1)
                for hd in range(HPG):
                    pe.wait_ge(mixed, turns(mixed))
                    w = decay[:, hd % 2, :]
                    for t in range(TB):
                        for b in range(t % 2 + 1):
                            key, off, _ = segs[t - t % 2 + b]
                            q0 = off + (P * (t % 2) if b == 0 else 0)
                            last = nc.tensor.matmul(ps[:, t, 64 * hd:64 * hd + 64], w[:, q0:q0 + P],
                                                    xdt[:, key, 64 * hd:64 * hd + 64],
                                                    start=hd == 0 and b == 0, stop=b == t % 2,
                                                    skip_group_check=True)
                    last.then_inc(head_y, 1)
                    if hd + 2 < HPG:
                        pe.wait_ge(decay_arg, turns(decay_arg))
                        sum_rows(hd + 2)
                turns(decay_arg, 2)

        pe.wait_ge(ident_in, 16)
        to_features(h, ready=x_loaded)
        pe.wait_ge(params, 16 * N_PARAMS)
        pe.wait_ge(turned_free, turns(turned_free))
        for t in range(4):
            last = nc.tensor.transpose(ps[:, 4, P * t:P * t + P], x_in[:, t, :], ident[:])
        last.then_inc(turned, 1)
        turns_out()
        pe.wait_ge(set_up, SET_UP)
        feature_pairs(4, acth, actl, mods=QK_MODS)
        token_pairs(2, acth, actl, mods=4)
        turns_out()
        stick_breaking()
        pe.wait_ge(mem_in, 16)
        to_features(mem_t, MB)
        turns_out()
        feature_pairs(2, memh, meml, MEM, mods=2)
        token_pairs(2, memh, meml, nt=MB, mods=2)
        token_pairs(2, acth, actl, mods=4, free=h_sum)
        turns_out()
        to_features(h, ready=h_ready)
        turns_out()
        feature_pairs(2, acth, actl, mods=4)
        cross_attention()
        token_pairs(2, acth, actl, mods=4, free=h_sum)
        turns_out()
        to_features(h, ready=h_ready)
        turns_out()
        feature_pairs(FC // 2, acth, actl, free=conv_done)
        pe.wait_ge(hid_ready, turns(hid_ready, FC))
        token_pairs(2, hid_h, hid_l, FC, free=h_sum)
        normed_to_features()
        tok_steps = {convolved: 4, tok_free: 4}
        feature_pairs(4, acth, actl, free=conv_done, after=turn_chunks, extra=tok_steps)
        feature_pairs(1, acth, actl, free=conv_done, after=turn_chunks, extra=tok_steps)
        feature_pairs(1, acth, actl, free=conv_done)
        token_pairs(4, acth, actl)
        dt_and_sums()
        banks_out()
        scan()
        to_features(gate_z, chunks=DI // P, ready=normed_ready)
        gate_rows_of()
        turns_out()
        token_pairs(2, yh, yl, DI // P, free=branch_out)
        normed_to_features()
        gated_ffn()
        normed_to_features()
        feature_pairs(2, acth, actl)
        value_units()
        banks_out()
        pe.wait_ge(nsa_in, 16 * NSA_PARAMS)
        compression()
        to_features(normed)
        turns_out()
        feature_pairs(2, acth, actl)
        banks_out()
        compressed_weights()
        branch_gates()
        turn_compressed()
        rotate(KC, [(ident[:], select[:, 4, :])])
        pe.wait_ge(rot_free, rotated[0])
        nsa_attention()
        gate_rows_of()
        token_pairs(2, acth, actl, free=branch_out)
        normed_to_features()
        gated_ffn()

    @block.scalar
    def _(act):
        turns = Turns()

        def split(slot):
            act.wait_ge(raw_full[slot], turns(raw_full[slot], 16))
            nc.scalar.activation(whi[:, slot, :], raw[:, slot, :], ACT.Copy).then_inc(hi_ready, 1)

        PAIR = {marks: 4, raw_full[0]: 16, raw_full[1]: 16}

        def feature_copies(pairs, dst, scale=1.0, n=SEQ):
            with turns.loop(act, pairs, PAIR) as i:
                for u in range(2):
                    for j in range(2):
                        act.wait_ge(marks, turns(marks))
                        nc.scalar.activation(dst[:, 4 * i + 2 * u + j, 0:n], ps[:, 2 * u + j, 0:n], ACT.Copy,
                                             scale=scale).then_inc(bank_free, 1)
                    split(u)

        def token_splits(halves, kc=KC, nt=TB):
            units = -(-kc // 4)
            with turns.loop(act, halves, {marks: units - 1 + nt, raw_full[0]: 8 * units, raw_full[1]: 8 * units}):
                for u in range(units):
                    act.wait_ge(marks, turns(marks, 1 if u < units - 1 else nt))
                    split(u % 2)

        def turned_his(dst, blocks=TB, chunks=KC):
            for r in range(blocks * chunks // 4):
                t, j = divmod(r, chunks // 4)
                act.wait_ge(turned, turns(turned))
                nc.scalar.activation(dst[:, 4 * j:4 * j + 4, P * t:P * t + P],
                                     ps[:, 4 + r % 4, :].rearrange("p (c q) -> p c q", c=4), ACT.Copy) \
                    .then_inc(turned_hi, 1)
            turns(turned_free, blocks * chunks // 4)

        def modulated_block(hi, t, gain, shift, chunks=KC):
            for j in range(chunks // 4):
                r = t * (chunks // 4) + j
                temporary = modulated[:, r % 2, :]
                act.wait_ge(turned, turns(turned))
                if shift and j:
                    turns(turned_free)
                    act.wait_ge(shaped, turns(shaped))
                else:
                    act.wait_ge(turned_free, TURNED0 + turns(turned_free) - 2)
                    for c in range(4):
                        cc = 4 * j + c
                        last = nc.scalar.activation(temporary[:, P * c:P * c + P],
                                                    ps[:, 4 + r % 4, P * c:P * c + P], ACT.Identity,
                                                    scale=gain(cc), bias=shift(cc) if shift else 0.0)
                    last.then_inc(act_step, 1)
                    act.wait_ge(act_step, turns(act_step))
                nc.scalar.activation(hi[:, 4 * j:4 * j + 4, P * t:P * t + P],
                                     temporary.rearrange("p (c q) -> p c q", c=4), ACT.Copy).then_inc(turned_hi, 1)

        def modulated_his(hi, gain, shift, chunks=KC):
            for t in range(TB):
                modulated_block(hi, t, gain, shift, chunks)

        def norm_rows(t):
            act.wait_ge(norm_root, turns(norm_root))
            nc.scalar.activation(normed[:, t, :], h[:, t, :], ACT.Copy, scale=norm_rstd[:, t:t + 1]) \
                .then_inc(normed_ready, 1)

        def norm_and_modulate(hi, gain, shift):
            for t in range(TB):
                norm_rows(t)
                if t:
                    modulated_block(hi, t - 1, gain, shift)
            modulated_block(hi, TB - 1, gain, shift)

        def load_gb(n):
            act.dma_start(gb[:, 0, :], a["ln_g"][0:1, n, :].to_broadcast([P, D])).then_inc(gb_in, 16)
            act.dma_start(gb[:, 1, :], a["ln_b"][0:1, n, :].to_broadcast([P, D])).then_inc(gb_in, 16)

        def stick_breaking():
            with turns.loop(act, 4, {capped: 4, act_step: 4, logw_ready: 12, o_ready: 2}) as i:
                for pair in range(2):
                    for hd in range(2):
                        act.wait_ge(capped, turns(capped))
                        nc.scalar.activation(sp_e[:, hd, :], sp_e[:, hd, :], ACT.Exp) \
                            .then_inc(act_step, 1)
                        act.wait_ge(act_step, turns(act_step))
                        nc.scalar.activation(sp_e[:, hd, :], sp_e[:, hd, :], ACT.Ln, bias=1.0) \
                            .then_inc(log_ready, 1)
                    for hd in range(2):
                        for strips in ((2,), (3, 1), (0,)):
                            act.wait_ge(logw_ready, turns(logw_ready))
                            for sb in strips:
                                bank, c0, off, n = strip(sb)
                                last = nc.scalar.activation(wts[:, hd, off:off + n],
                                                            ps[:, 3 * hd + bank, c0:c0 + n], ACT.Exp)
                            last.then_inc(w_ready, 1)
                    act.wait_ge(o_ready, turns(o_ready))
                    nc.scalar.activation(acth[:, 2 * i + pair, :], ps[:, 6 + pair, :], ACT.Copy).then_inc(evac_hi, 1)

        def cross_attention():
            def exps(hd):
                act.wait_ge(score_max, hd + 1)
                for t in range(TB):
                    nc.scalar.activation(px[:, hd % 2, t, :],
                                         ps[:, 2 * (hd % 2) + t // 2, MEM * (t % 2):MEM * (t % 2) + MEM], ACT.Exp,
                                         bias=small[:, 4 * (hd % 2) + t:4 * (hd % 2) + t + 1],
                                         accum_out=small[:, 8 + 4 * (hd % 2) + t:9 + 4 * (hd % 2) + t]) \
                        .then_inc(probs, 1)

            exps(0)
            for hd in range(XA_HEADS):
                if hd + 1 < XA_HEADS:
                    exps(hd + 1)
                for m in range(MB):
                    act.wait_ge(probs_turned, 2 * hd + m + 1)
                    nc.scalar.activation(pxt[:, m, :], ps[:, 4 + m, :], ACT.Copy).then_inc(probs_copied, 1)
                for c in range(2):
                    act.wait_ge(heads_out, 2 * hd + c + 1)
                    nc.scalar.activation(acth[:, 2 * hd + c, :], ps[:, 6 + c, :], ACT.Copy).then_inc(evac_hi, 1)

        def conv_ffn():
            with turns.loop(act, FC // 2, PAIR | {hid_ready: 2, conv_done: 4, hid_value: 2}) as i:
                for u in range(2):
                    for j in range(2):
                        act.wait_ge(marks, turns(marks))
                        c = FC * u + 2 * i + j
                        nc.scalar.activation(conv_t[:, 2 * u + j, :], ps[:, 2 * u + j, :], ACT.Identity,
                                             scale=cols[:, bass.ds(C_CW2 + c, 1)], bias=cols[:, bass.ds(C_CB + c, 1)]) \
                            .then_inc(taps, 1)
                    if u == 0:
                        split(0)
                for j in range(2):
                    act.wait_ge(conv_done, FREE0 + turns(conv_done))
                    nc.scalar.activation(conv_t[:, j, :], conv_t[:, j, :], ACT.Gelu_apprx_tanh).then_inc(gated, 1)
                turns(conv_done, 2)
                split(1)
                for j in range(2):
                    act.wait_ge(hid_value, HID0 + turns(hid_value))
                    nc.scalar.activation(hid_h[:, 2 * i + j, :], conv_t[:, j, :], ACT.Copy).then_inc(evac_hi, 1)
                act.wait_ge(hid_ready, turns(hid_ready, 2))

        def branch_copies(kc, last=False, branch=branch, following=None):
            units = -(-kc // 4)
            for i in range(2):
                for u in range(units - 1):
                    act.wait_ge(marks, turns(marks))
                    if not (last and i == 1 and u >= units - 2):
                        split(u % 2)
                for t in range(TB):
                    act.wait_ge(marks, turns(marks))
                    nc.scalar.activation(branch[:, t, 512 * i:512 * i + 512], ps[:, t, :], ACT.Copy) \
                        .then_inc(branch_out, 1)
                if i == 0:
                    split(1)
            if following:
                norm_and_modulate(*following)
                split(1)

        def load_gain(name, layer):
            act.dma_start(gb[:, 1, :], a[name][layer:layer + 1, :].to_broadcast([P, D])).then_inc(gb_in, 16)

        def modulation(gain, shift):
            return (lambda c: gains[:, gain, c:c + 1]), (lambda c: modv[:, shift + c:shift + c + 1])

        def gated_ffn(layer, last=False, following=None):
            with turns.loop(act, FC // 2, PAIR | {hid_ready: 2, hid_value: 2}) as i:
                for j in range(2):
                    act.wait_ge(marks, turns(marks))
                    nc.scalar.activation(conv_t[:, j, :], ps[:, j, :], ACT.Silu).then_inc(gated, 1)
                split(0)
                act.wait_ge(marks, turns(marks, 2))
                split(1)
                for j in range(2):
                    act.wait_ge(hid_value, HID0 + turns(hid_value))
                    nc.scalar.activation(hid_h[:, 2 * i + j, :], conv_t[:, j, :], ACT.Copy).then_inc(evac_hi, 1)
                act.wait_ge(hid_ready, turns(hid_ready, 2))
            load_gain("norm_post_ffn_2", layer)
            branch_copies(FC, last, following=following)

        def conv_pairs(pairs, first, to_tokens):
            with turns.loop(act, pairs, PAIR | {conv_done: 4, tok_turned: 4 * to_tokens}) as i:
                for u in range(2):
                    for j in range(2):
                        b = 2 * u + j
                        act.wait_ge(marks, turns(marks))
                        c = 4 * i + (first + b)
                        nc.scalar.activation(conv4[:, b, :], ps[:, b, :], ACT.Identity,
                                             scale=cols[:, bass.ds(C_SCW + 72 + c, 1)],
                                             bias=cols[:, bass.ds(C_SCB + c, 1)]).then_inc(taps, 1)
                    if u == 0:
                        split(0)
                for b in range(4):
                    act.wait_ge(conv_done, FREE0 + turns(conv_done))
                    nc.scalar.activation(conv4[:, b, :], conv4[:, b, :], ACT.Silu).then_inc(convolved, 1)
                split(1)
                if to_tokens:
                    for b in range(4):
                        act.wait_ge(tok_turned, turns(tok_turned))
                        c = 4 * i + (first + b)
                        nc.scalar.activation(tok[:, :, bass.ds(P * c, P)],
                                             ps[:, 4 + b, :].rearrange("p (t f) -> p t f", t=TB), ACT.Copy) \
                            .then_inc(tok_free, 1)

        def mamba():
            act.wait_ge(h_ready, 3 * TB)
            act.dma_start(wdt[:], a["ssm_w_in_2"][0].rearrange("(k p) c -> p k c", p=P)[:, :, 2 * DI + 1024:]) \
                .then_inc(wdt_in, 16)
            for n, name in enumerate(("ssm_dt_bias_2", "ssm_a_log_2", "ssm_d_2")):
                act.dma_start(heads[:, n, :], a[name].to_broadcast([P, SSM_H])).then_inc(heads_in, 16)
            conv_pairs(4, 0, True)
            conv_pairs(1, 16, True)
            act.wait_ge(bc_copied, 4)
            conv_pairs(1, 20, False)
            act.wait_ge(wdt_in, 16)
            nc.scalar.activation(wdt_h[:], wdt[:], ACT.Copy).then_inc(wdt_hi, 1)
            act.wait_ge(bc_copied, 8)
            with turns.loop(act, 4, {marks: 5, raw_full[0]: 16, raw_full[1]: 16}) as i:
                act.wait_ge(marks, turns(marks))
                split(0)
                for t in range(TB):
                    act.wait_ge(marks, turns(marks))
                    nc.scalar.activation(gate_z[:, t, bass.ds(512 * i, 512)], ps[:, t, :], ACT.Silu) \
                        .then_inc(bank_free, 1)
                split(1)
            act.wait_ge(heads_in, 48)
            nc.scalar.activation(heads[:, 1, :], heads[:, 1, :], ACT.Exp).then_inc(a_ready, 1)
            act.wait_ge(dt_raw, 1)
            act.wait_ge(wdt_lo, 1)
            nc.scalar.activation(dt_t[0:SSM_H, :], ps[0:SSM_H, 4, :], ACT.Copy).then_inc(dt_kept, 1)
            act.wait_ge(dt_cap, 1)
            nc.scalar.activation(dt_e[:], dt_e[:], ACT.Exp).then_inc(act_step, 1)
            act.wait_ge(act_step, turns(act_step))
            nc.scalar.activation(dt_e[:], dt_e[:], ACT.Ln, bias=1.0).then_inc(dt_log, 1)
            act.wait_ge(acs_out, 1)
            nc.scalar.activation(eacs[:], acs[:], ACT.Exp)
            nc.scalar.activation(tail[:], tail[:], ACT.Exp).then_inc(tail_ready, 1)

        def scan():
            act.wait_ge(tok_free, 4 + 20)
            with turns.loop(act, SSM_G, {decay_arg: 8, group_y: 1}) as g:
                act.wait_ge(group_y, turns(group_y) - 1 + DONE0)
                for dst, src in ((bst[:], bct[:, g, :]), (cst[:], bct[:, 4 + g, :]),
                                 (btk[:], tok[:, 0:2, bass.ds(P * g + DI, P)])):
                    nc.scalar.activation(dst, src, ACT.Copy).then_inc(group_in, 1)
                for hd in range(HPG):
                    act.wait_ge(decay_arg, turns(decay_arg))
                    nc.scalar.activation(decay[:, hd % 2, :], decay[:, hd % 2, :], ACT.Exp).then_inc(decay_exp, 1)

        def rotated_out(dst, banks):
            for b in range(banks):
                act.wait_ge(rot_ready, turns(rot_ready))
                n = turns.seen["rot_ready"] - 1
                nc.scalar.activation(dst[:, b, :], ps[:, 4 + n % 4, :], ACT.Copy).then_inc(rot_hi, 1)

        def compression():
            for w in range(2):
                act.wait_ge(dup_free, KV * w + KV)
                nc.scalar.activation(kcph[:, w, :, :], kcp[:, w, :, :], ACT.Copy).then_inc(blocks_hi, 1)
            rotated_out(kdup_h, 2 * KV)
            act.wait_ge(hid_padded, 2)
            for w in range(2):
                act.wait_ge(marks, turns(marks))
                split(0)
                for j in range(2):
                    act.wait_ge(marks, turns(marks))
                    x = ps[:, 2 * w + j, 0:KV * N_CMP].rearrange("p (g c) -> p g c", g=KV)
                    if w:
                        x = x.unsqueeze(2).to_broadcast([P, KV, QG, N_CMP])
                    nc.scalar.activation(hid_v[:, j, :, :, 0:N_CMP] if w else hid_k[:, j, :, 0:N_CMP], x, ACT.Silu) \
                        .then_inc(bank_free, 1)
                split(1)

        def nsa_attention():
            def job_exps(n):
                for tb, off in T_STRIPS.items():
                    act.wait_ge(n_max, turns(n_max))
                    w = P * tb + P
                    nc.scalar.activation(pn[:, n % 2, off:off + w], ps[:, tb, 0:w], ACT.Exp,
                                         bias=nst[:, n % 2, 0, tb:tb + 1],
                                         accum_out=nst[:, n % 2, 1, tb:tb + 1]).then_inc(n_exps, 1)

            with turns.loop(act, KV, {n_max: 32, n_turned: 24, n_outs: 2}) as g:
                job_exps(0)
                for n in range(2 * QG):
                    if n + 1 < 2 * QG:
                        job_exps(n + 1)
                    for r, blocks in enumerate(ROUNDS):
                        act.wait_ge(n_turned, turns(n_turned))
                        w = P * len(blocks)
                        nc.scalar.activation(pnt_h[:, 512 * r:512 * r + w], ps[:, 4 + (3 * n + r) % 2, 0:w],
                                             ACT.Copy).then_inc(n_hi, 1)
                    if n in (QG, 2 * QG - 1):
                        act.wait_ge(n_outs, turns(n_outs))
                        pair = int(n > QG)
                        nc.scalar.activation(acth[:, 2 * g + pair, :], ps[:, 6 + pair, :], ACT.Copy) \
                            .then_inc(n_out_hi, 1)

        act.dma_start(ident[:], a["c_ident"]).then_inc(ident_in, 16)
        act.dma_start(neg_suffix[:], a["c_neg_suffix"]).then_inc(params, 16)
        act.dma_start(causal6[:], a["c_causal6"]).then_inc(params, 16)
        act.wait_ge(pool_step, 1)
        for tile, row, name, src in param_rows(a):
            n = src.shape[0]
            act.dma_start(x_in[row:row + n, tile, :], src).then_inc(params, 16)
        turned_his(acth)
        split(0)
        split(1)
        act.wait_ge(turned, turns(turned))
        nc.scalar.activation(cols[:], ps[:, 4, :], ACT.Copy).then_inc(turned_hi, 1)
        turns(turned_free)
        act.wait_ge(turned_hi, KC + 1)
        nc.scalar.activation(c_silu[:], cols[:, C_C:C_C + KC], ACT.Silu).then_inc(c_ready, 1)
        feature_copies(2, q_t, 0.125)
        feature_copies(2, k_t)
        token_splits(2)
        stick_breaking()
        act.wait_ge(o_free, 2 + KC)
        act.dma_start(mem_t[:], a["mem"].rearrange("a (t p) c -> p (a t) c", p=P)).then_inc(mem_in, 16)
        load_gb(0)
        turned_his(memh, MB)
        feature_copies(1, kx, n=MEM)
        feature_copies(1, kx[:, 4:8, :], n=MEM)
        token_splits(2, nt=MB)
        token_splits(2)
        turned_his(acth)
        load_gb(1)
        feature_copies(2, qx, 1.0 / 16)
        cross_attention()
        token_splits(2)
        turned_his(acth)
        conv_ffn()
        load_gb(2)
        token_splits(2, FC)
        norm_and_modulate(acth, *modulation(0, 0))
        mamba()
        scan()
        modulated_his(yh, lambda c: cols[:, C_SNORM + c:C_SNORM + c + 1], None, DI // P)
        load_gain("norm_post_mix_2", 0)
        branch_copies(DI // P, branch=branch_low, following=(acth, *modulation(2, 24)))
        gated_ffn(0, following=(acth, *modulation(4, 96)))
        act.wait_ge(h_ready, 5 * TB)
        act.dma_start(select[:], a["c_select"].rearrange("p (n c) -> p n c", n=5)).then_inc(nsa_in, 16)
        act.dma_start(rotary[:], a["c_rotary"].rearrange("p (n c) -> p n c", n=2)).then_inc(nsa_in, 16)
        act.dma_start(cmp_mask[:], a["c_compressed"]).then_inc(nsa_in, 16)
        for twice in range(2):
            act.dma_start(w2k[:, :, twice, :], a["cmp_w2_k_2"].rearrange("(k p) c -> p k c", p=P)).then_inc(nsa_in, 16)
        act.dma_start(w2v[:], a["cmp_w2_v_2"].rearrange("(k p) c -> p k c", p=P)).then_inc(nsa_in, 16)
        feature_copies(2, kv8)
        act.wait_ge(marks, turns(marks))
        split(0)
        for t in range(TB):
            act.wait_ge(marks, turns(marks))
            nc.scalar.activation(v_h[:, t, :], ps[:, t, :], ACT.Copy).then_inc(v_hi, 1)
        split(1)
        compression()
        act.wait_ge(cmp_kept, 1)
        act.dma_start(w_gate[:], a["nsa_w_q_2"][0].rearrange("(k p) c -> p k c", p=P)[:, :, D:]).then_inc(gate_w, 16)
        act.wait_ge(gate_w, 16)
        nc.scalar.activation(w_gate_h[:], w_gate[:], ACT.Copy).then_inc(gate_hi, 1)
        modulated_his(acth, *modulation(1, 48))
        act.dma_start(rotary_q[:], a["c_rotary"].rearrange("p (n c) -> p n c", n=2)).then_inc(rotary_in, 16)
        feature_copies(2, q_u, 0.125)
        act.wait_ge(c_args, 1)
        nc.scalar.activation(pc[:], pc[:], ACT.Exp).then_inc(c_exps, 1)
        act.wait_ge(gates_raw, 1)
        act.wait_ge(gate_lo, 1)
        nc.scalar.activation(gates_t[0:48, :], ps[0:48, 4, :], ACT.Copy).then_inc(gates_kept, 1)
        act.wait_ge(gates_turned, 1)
        nc.scalar.activation(gates[:], ps[:, 5, 0:48 * TB].rearrange("p (t c) -> p t c", t=TB), ACT.Sigmoid) \
            .then_inc(gates_ready, 1)
        for g in range(KV):
            act.wait_ge(c_turned, g + 1)
            nc.scalar.activation(pct[:, g, :], ps[:, 4 + g, :], ACT.Copy).then_inc(c_copied, 1)
        rotated_out(acth, KC)
        nsa_attention()
        load_gain("norm_post_mix_2", 1)
        branch_copies(KC, branch=branch_low, following=(acth, *modulation(3, 72)))
        gated_ffn(1, last=True)

    @block.vector
    def _(dve):
        turns = Turns()

        def split(slot):
            dve.wait_ge(hi_ready, turns(hi_ready))
            nc.vector.tensor_tensor(wlo[:, slot, :], raw[:, slot, :], whi[:, slot, :].bitcast(F32), ALU.subtract) \
                .then_inc(unit_ready, 1)

        def lo_part(dst, src, hi):
            return nc.vector.tensor_tensor(dst, src, hi.bitcast(F32), ALU.subtract)

        def mod_units(first, count):
            for b in range(first, first + count):
                dve.wait_ge(mod_raw[b % 2], turns(mod_raw[b % 2], 16))
                for k in range(KC // 2):
                    for chain, o in enumerate((macc[:, b, :], macc2[:, b % 2, :])):
                        kk = k + KC // 2 * chain
                        w, c = mraw[:, b % 2, kk, :], c_silu[:, kk:kk + 1]
                        if k:
                            dve.wait_ge(mod_step, turns(mod_step))
                            last = nc.vector.scalar_tensor_tensor(out=o, in0=w, scalar=c, in1=o, op0=ALU.mult,
                                                                  op1=ALU.add)
                        else:
                            last = nc.vector.tensor_scalar(o, w, c, None, ALU.mult)
                        last.then_inc(mod_step, 1)
                dve.wait_ge(mod_step, turns(mod_step, 2))
                nc.vector.tensor_tensor(macc[:, b, :], macc[:, b, :], macc2[:, b % 2, :], ALU.add).then_inc(mod_acc, 1)

        def mod_store(units, col):
            dve.wait_ge(mod_cols, turns(mod_cols))
            nc.vector.tensor_tensor(modv[:, bass.ds(col, 2 * units)], ps[:, 6, 0:2 * units],
                                    cols[:, bass.ds(C_MODB + col, 2 * units)], ALU.add).then_inc(mod_done, 1)

        def mod_steps(units):
            return {mod_raw[0]: 8 * units, mod_raw[1]: 8 * units, mod_step: 8 * units, mod_cols: int(units > 0)}

        def splits(pairs, mods=0, col=0):
            with turns.loop(dve, pairs, {hi_ready: 2, marks: 4} | mod_steps(mods)) as i:
                early = -(-mods // 2)
                mod_units(0, early)
                split(0)
                mod_units(early, mods - early)
                split(1)
                turns(marks, 4)
                if mods:
                    mod_store(mods, 2 * mods * i + col)

        def token_banks(halves, take, kc=KC, nt=TB, mods=0, col=0):
            units = -(-kc // 4)
            with turns.loop(dve, halves, {marks: units - 1 + nt, hi_ready: units} | mod_steps(mods)) as i:
                early = -(-mods // 2)
                mod_units(0, early)
                for u in range(units - 1):
                    split(u % 2)
                mod_units(early, mods - early)
                turns(marks, units - 1)
                for t in range(nt):
                    dve.wait_ge(marks, turns(marks))
                    take(i, t).then_inc(bank_free, 1)
                split(1)
                if mods:
                    mod_store(mods, 2 * mods * i + col)

        def turned_los(dst, hi, blocks=TB, chunks=KC):
            for r in range(blocks * chunks // 4):
                t, j = divmod(r, chunks // 4)
                dve.wait_ge(turned_hi, turns(turned_hi))
                lo_part(dst[:, 4 * j:4 * j + 4, P * t:P * t + P],
                        ps[:, 4 + r % 4, :].rearrange("p (c q) -> p c q", c=4),
                        hi[:, 4 * j:4 * j + 4, P * t:P * t + P]).then_inc(turned_free, 1)

        def row_stats(x, t, stats, mv):
            stored(nc.vector.bn_stats(stats[:, t, 1, :], x[:, t, 512:1024]))
            return nc.vector.bn_aggr(mv[:, t, :], stats[:, t, :, :])

        def mean_square(t, mv):
            return nc.vector.scalar_tensor_tensor(out=mv[:, t, 1:2], in0=mv[:, t, 0:1], scalar=mv[:, t, 0:1],
                                                  in1=mv[:, t, 1:2], op0=ALU.mult, op1=ALU.add)

        def norm_block(t):
            dve.wait_ge(h_ready, turns.seen["h_ready"])
            nc.vector.bn_stats(norm_stats[:, t, 0, :], h[:, t, 0:512])
            stored(row_stats(h, t, norm_stats, norm_mv))
            mean_square(t, norm_mv).then_inc(norm_moments, 1)

        def residual_norm(kc=KC, mods=0, col=0, then_norm=False):
            units = -(-kc // 4)

            def finish(t):
                dve.wait_ge(rstd_ready, turns(rstd_ready))
                x = h[:, t, :]
                stored(nc.vector.tensor_scalar(x, x, mean_var[:, t, 0:1], rstd[:, t:t + 1], ALU.subtract, ALU.mult))
                stored(nc.vector.tensor_tensor(x, x, gb[:, 0, :], ALU.mult))
                nc.vector.tensor_tensor(x, x, gb[:, 1, :], ALU.add).then_inc(h_ready, 1)
                turns(h_ready)
                if then_norm:
                    norm_block(t)

            for i in range(2):
                early = -(-mods // 2)
                mod_units(0, early)
                for u in range(units - 1):
                    split(u % 2)
                mod_units(early, mods - early)
                turns(marks, units - 1)
                if i:
                    dve.wait_ge(gb_in, turns(gb_in, 32))
                for t in range(TB):
                    dve.wait_ge(marks, turns(marks))
                    x = h[:, t, 512 * i:512 * i + 512]
                    nc.vector.scalar_tensor_tensor(out=x, in0=x, scalar=ALPHA, in1=ps[:, t, :], op0=ALU.mult,
                                                   op1=ALU.add).then_inc(h_sum, 1)
                    dve.wait_ge(h_sum, FREE0 + turns(h_sum))
                    if i == 0:
                        nc.vector.bn_stats(stats[:, t, 0, :], x)
                    else:
                        row_stats(h, t, stats, mean_var).then_inc(moments, 1)
                        if t == TB - 1 and mods:
                            mod_store(mods, 2 * mods * i + col)
                        if t:
                            finish(t - 1)
                if i == 0:
                    split(1)
                    if mods:
                        mod_store(mods, col)
            finish(TB - 1)

        def stick_breaking():
            with turns.loop(dve, 4, {z_ready: 12, log_ready: 4, evac_hi: 2}) as i:
                for pair in range(2):
                    for hd in range(2):
                        for strips in ((0,), (1, 3), (2,)):
                            dve.wait_ge(z_ready, turns(z_ready))
                            for sb in strips:
                                bank, c0, off, n = strip(sb)
                                last = nc.vector.tensor_scalar(sp_e[:, hd, off:off + n],
                                                               ps[:, 3 * hd + bank, c0:c0 + n], SOFTPLUS_MAX, None,
                                                               ALU.min)
                        last.then_inc(capped, 1)
                    for hd in range(2):
                        dve.wait_ge(log_ready, turns(log_ready))
                        for sb in range(TB):
                            bank, c0, off, n = strip(sb)
                            last = nc.vector.scalar_tensor_tensor(
                                out=sp[:, hd, off:off + n], in0=ps[:, 3 * hd + bank, c0:c0 + n], scalar=1.0,
                                in1=sp_e[:, hd, off:off + n], op0=ALU.mult, op1=ALU.max)
                        last.then_inc(sp_ready, 1)
                    dve.wait_ge(evac_hi, turns(evac_hi))
                    lo_part(actl[:, 2 * i + pair, :], ps[:, 6 + pair, :], acth[:, 2 * i + pair, :]) \
                        .then_inc(o_free, 1)

        def cross_attention():
            def maxima(hd):
                b = 4 * (hd % 2)
                for k in range(2):
                    dve.wait_ge(scores, 2 * hd + k + 1)
                    last = nc.vector.tensor_reduce(small[:, 16 + b + 2 * k:18 + b + 2 * k],
                                                   ps[:, 2 * (hd % 2) + k, :].rearrange("p (t m) -> p t m", t=2),
                                                   AX.X, ALU.max)
                last.then_inc(dve_step, 1)
                dve.wait_ge(dve_step, turns(dve_step))
                nc.vector.tensor_scalar(small[:, b:b + 4], small[:, 16 + b:20 + b], -1.0, None, ALU.mult) \
                    .then_inc(score_max, 1)

            def normalise(hd):
                b = 4 * (hd % 2)
                dve.wait_ge(probs, 4 * hd + 4)
                nc.vector.reciprocal(small[:, 24 + b:28 + b], small[:, 8 + b:12 + b]).then_inc(dve_step, 1)
                dve.wait_ge(dve_step, turns(dve_step))
                nc.vector.tensor_tensor(px[:, hd % 2, :, :], px[:, hd % 2, :, :],
                                        small[:, 24 + b:28 + b].unsqueeze(2).to_broadcast([P, TB, MEM]),
                                        ALU.mult).then_inc(probs_normed, 1)

            maxima(0)
            for hd in range(XA_HEADS):
                if hd + 1 < XA_HEADS:
                    maxima(hd + 1)
                normalise(hd)
                for c in range(2):
                    dve.wait_ge(evac_hi, turns(evac_hi))
                    lo_part(actl[:, 2 * hd + c, :], ps[:, 6 + c, :], acth[:, 2 * hd + c, :]).then_inc(heads_free, 1)

        def conv_ffn():
            with turns.loop(dve, FC // 2, {hi_ready: 2, taps: 4, dve_step: 4, gated: 2, evac_hi: 2,
                                           conv_done: 4, marks: 4}) as i:
                turns(marks, 4)
                for u in range(2):
                    for tap, shift in ((1, 1), (0, 2)):
                        for j in range(2):
                            if tap:
                                dve.wait_ge(taps, turns(taps))
                            w = cols[:, bass.ds(C_CW + 2 * FC * tap + FC * u + 2 * i + j, 1)]
                            x = conv_t[:, 2 * u + j, shift:]
                            last = nc.vector.scalar_tensor_tensor(out=x, in0=ps[:, 2 * u + j, 0:SEQ - shift],
                                                                  scalar=w, in1=x, op0=ALU.mult, op1=ALU.add)
                            last.then_inc(dve_step if tap else conv_done, 1)
                        if tap:
                            dve.wait_ge(dve_step, turns(dve_step, 2))
                    if u == 0:
                        split(0)
                dve.wait_ge(conv_done, FREE0 + turns(conv_done, 4))
                for j in range(2):
                    dve.wait_ge(gated, turns(gated))
                    nc.vector.tensor_tensor(conv_t[:, j, :], conv_t[:, j, :], conv_t[:, 2 + j, :], ALU.mult) \
                        .then_inc(hid_value, 1)
                split(1)
                for j in range(2):
                    dve.wait_ge(evac_hi, turns(evac_hi))
                    lo_part(hid_l[:, 2 * i + j, :], conv_t[:, j, :], hid_h[:, 2 * i + j, :]).then_inc(hid_ready, 1)

        def stored(ins):
            ins.then_inc(dve_step, 1)
            dve.wait_ge(dve_step, turns(dve_step))

        def modulated_los(lo, hi, chunks=KC, shape=None):
            turned_before = turns.seen["turned_hi"]
            for r in range(TB * chunks // 4):
                t, j = divmod(r, chunks // 4)
                temporary = modulated[:, r % 2, :].rearrange("p (c q) -> p c q", c=4)
                if shape and j == 0:
                    gain, shift = shape
                    other = modulated[:, (r + 1) % 2, :].rearrange("p (c q) -> p c q", c=4)
                    dve.wait_ge(turned, turned_before + r + 2)
                    dve.wait_ge(turned_free, TURNED0 + turns.seen["turned_hi"])
                    stored(nc.vector.tensor_tensor(
                        other, ps[:, 4 + (r + 1) % 4, :].rearrange("p (c q) -> p c q", c=4),
                        gains[:, gain, 4:8].unsqueeze(2).to_broadcast([P, 4, P]), ALU.mult))
                    nc.vector.tensor_tensor(other, other,
                                            modv[:, shift + 4:shift + 8].unsqueeze(2).to_broadcast([P, 4, P]),
                                            ALU.add).then_inc(shaped, 1)
                dve.wait_ge(turned_hi, turns(turned_hi))
                lo_part(lo[:, 4 * j:4 * j + 4, P * t:P * t + P], temporary, hi[:, 4 * j:4 * j + 4, P * t:P * t + P]) \
                    .then_inc(turned_free, 1)

        def gate_gain(gate):
            dve.drain()
            make_diag(gate)
            dve.wait_ge(gate_rows, turns(gate_rows))
            dve.wait_ge(gb_in, turns(gb_in, 16))
            nc.vector.tensor_tensor(gb[:, 0, :].rearrange("p (b c) -> p b c", b=2), ps[:, 4:6, :],
                                    gb[:, 1, :].rearrange("p (b c) -> p b c", b=2), ALU.mult) \
                .then_inc(dve_step, 1)
            dve.wait_ge(dve_step, turns(dve_step))

        def branch_norm(kc, branch=branch, last=False):
            units = -(-kc // 4)

            def finish(t):
                dve.wait_ge(rstd_ready, turns(rstd_ready))
                x = branch[:, t, :]
                stored(nc.vector.scalar_tensor_tensor(out=x, in0=x, scalar=rstd[:, t:t + 1], in1=gb[:, 0, :],
                                                      op0=ALU.mult, op1=ALU.mult))
                nc.vector.tensor_tensor(h[:, t, :], h[:, t, :], x, ALU.add).then_inc(h_ready, 1)
                turns(h_ready)
                if not last:
                    norm_block(t)

            for i in range(2):
                for u in range(units - 1):
                    if not (last and i == 1 and u >= units - 2):
                        split(u % 2)
                for t in range(TB):
                    dve.wait_ge(branch_out, FREE0 + turns(branch_out))
                    if i == 0:
                        nc.vector.bn_stats(stats[:, t, 0, :], branch[:, t, 0:512])
                    else:
                        stored(row_stats(branch, t, stats, mean_var))
                        mean_square(t, mean_var).then_inc(moments, 1)
                        if t:
                            finish(t - 1)
                if i == 0:
                    split(1)
            finish(TB - 1)

        def gated_ffn(gate, last=False):
            with turns.loop(dve, FC // 2, {hi_ready: 2, gated: 2, evac_hi: 2, marks: 4}) as i:
                split(0)
                turns(marks, 2)
                for j in range(2):
                    dve.wait_ge(marks, turns(marks))
                    dve.wait_ge(gated, turns(gated))
                    nc.vector.tensor_tensor(conv_t[:, j, :], conv_t[:, j, :], ps[:, 2 + j, :], ALU.mult) \
                        .then_inc(hid_value, 1)
                split(1)
                for j in range(2):
                    dve.wait_ge(evac_hi, turns(evac_hi))
                    lo_part(hid_l[:, 2 * i + j, :], conv_t[:, j, :], hid_h[:, 2 * i + j, :]).then_inc(hid_ready, 1)
            gate_gain(gate)
            branch_norm(FC, last=last)

        def conv_pairs(pairs, first):
            with turns.loop(dve, pairs, {hi_ready: 2, taps: 4, dve_step: 8, marks: 4}) as i:
                turns(marks, 4)
                for u in range(2):
                    for tap, shift in ((2, 1), (1, 2), (0, 3)):
                        for j in range(2):
                            b = 2 * u + j
                            if tap == 2:
                                dve.wait_ge(taps, turns(taps))
                            x = conv4[:, b, shift:]
                            last = nc.vector.scalar_tensor_tensor(
                                out=x, in0=ps[:, b, 0:SEQ - shift],
                                scalar=cols[:, bass.ds(C_SCW + 24 * tap + 4 * i + (first + b), 1)], in1=x,
                                op0=ALU.mult, op1=ALU.add)
                            last.then_inc(dve_step if tap else conv_done, 1)
                        if tap:
                            dve.wait_ge(dve_step, turns(dve_step, 2))
                    if u == 0:
                        split(0)
                split(1)

        def per_head(x):
            return x.unsqueeze(2).to_broadcast([P, HPG, 64])

        def by_head(x):
            return x.rearrange("p (h d) -> p h d", h=HPG)

        def dt_and_sums():
            dve.wait_ge(a_ready, 1)
            nc.vector.tensor_scalar(heads[:, 1, :], heads[:, 1, :], -1.0, None, ALU.mult)
            dve.wait_ge(dt_turned, 1)
            stored(nc.vector.tensor_tensor(dt[:], ps[:, 6, 0:P].rearrange("p (t h) -> p t h", t=TB),
                                           heads[:, 0:1, :].to_broadcast([P, TB, SSM_H]), ALU.add))
            nc.vector.tensor_scalar(dt_e[:], dt[:], SOFTPLUS_MAX, None, ALU.min).then_inc(dt_cap, 1)
            dve.wait_ge(dt_log, 1)
            stored(nc.vector.tensor_tensor(dt[:], dt[:], dt_e[:], ALU.max))
            nc.vector.tensor_tensor(dta[:], dt[:], heads[:, 1:2, :].to_broadcast([P, TB, SSM_H]), ALU.mult) \
                .then_inc(dta_ready, 1)
            dve.wait_ge(acs_ready, 1)
            stored(nc.vector.tensor_copy(acs[:], ps[:, 5, 0:P].rearrange("p (t h) -> p t h", t=TB)))
            nc.vector.tensor_tensor(tail[:], ps[:, 5:6, P:P + SSM_H].to_broadcast([P, 2, SSM_H]), acs[:, 0:2, :],
                                    ALU.subtract).then_inc(acs_out, 1)

        def scan():
            dve.wait_ge(tail_ready, 1)
            with turns.loop(dve, SSM_G, {heads_staged: 2, dve_step: 4, cb_ready: 1, acs_rows: 8, head_y: 8,
                                         dx_ready: 4}) as g:
                cols_g, heads_g = bass.ds(512 * g, 512), bass.ds(HPG * g, HPG)
                for t in range(TB):
                    last = nc.vector.tensor_tensor(by_head(xdt[:, t, :]), by_head(tok[:, t, cols_g]),
                                                   per_head(dt[:, t, heads_g]), ALU.mult)
                stored(last)
                for t in range(2):
                    last = nc.vector.tensor_tensor(by_head(xdt_tail[:, t, :]), by_head(xdt[:, t, :]),
                                                   per_head(tail[:, t, heads_g]), ALU.mult)
                last.then_inc(xdt_ready, 1)
                dve.wait_ge(cb_ready, turns(cb_ready))
                for ch in range(2):
                    c = slice(3 * P * ch, 3 * P * ch + 3 * P)
                    nc.vector.tensor_tensor(cbm[:, c], ps[:, 6 + ch, 0:3 * P], causal6[:, c], ALU.mult)
                nc.vector.tensor_copy(state[:], ps[:, 5, :]).then_inc(cb_out, 1)
                dve.wait_ge(heads_staged, turns(heads_staged, 2))
                for hd in range(HPG):
                    dve.wait_ge(acs_rows, turns(acs_rows))
                    if hd >= 2:
                        dve.wait_ge(head_y, turns(head_y))
                    for t in range(TB):
                        ch, b = t // 2, t % 2
                        off, n = 384 * ch + 256 * b, 256 - P * b
                        last = nc.vector.tensor_scalar(decay[:, hd % 2, off:off + n],
                                                       ps[:, 6 + hd % 2, 256 * ch + P * b:256 * ch + 256],
                                                       acsg[:, t, hd:hd + 1], 0.0, ALU.subtract, ALU.min)
                    last.then_inc(decay_arg, 1)
                dve.wait_ge(head_y, turns(head_y, 2))
                for t in range(TB):
                    dve.wait_ge(dx_ready, turns(dx_ready))
                    nc.vector.tensor_tensor(dx[:, t, :], dx[:, t, :], ps[:, t, :], ALU.add)
                for t in (2, 3):
                    last = nc.vector.tensor_tensor(by_head(xdt[:, t, :]), by_head(ps[:, 2 + t, :]),
                                                   per_head(eacs[:, t, heads_g]), ALU.mult)
                stored(last)
                for t in (2, 3):
                    last = nc.vector.tensor_tensor(dx[:, t, :], dx[:, t, :], xdt[:, t, :], ALU.add)
                stored(last)
                for t in range(TB):
                    last = nc.vector.tensor_tensor(gate_z[:, t, cols_g], gate_z[:, t, cols_g], dx[:, t, :], ALU.mult)
                stored(last)
                for t in range(TB):
                    last = nc.vector.bn_stats(gstats[:, t, g, :], gate_z[:, t, cols_g])
                last.then_inc(group_y, 1)

        def group_norm():
            dve.wait_ge(group_y, DONE0 + SSM_G)
            for n in range(TB * SSM_G):
                last = nc.vector.bn_aggr(gmv[:, n, :], gstats[:, n // SSM_G, n % SSM_G, :])
            stored(last)
            stored(nc.vector.tensor_tensor(gmv[:, :, 0], gmv[:, :, 0], gmv[:, :, 0], ALU.mult))
            nc.vector.tensor_tensor(ginv[:], gmv[:, :, 1], gmv[:, :, 0], ALU.add).then_inc(moments, 1)
            dve.wait_ge(rstd_ready, turns(rstd_ready))
            for n in range(TB * SSM_G):
                x = gate_z[:, n // SSM_G, 512 * (n % SSM_G):512 * (n % SSM_G) + 512]
                last = nc.vector.tensor_scalar(x, x, ginv[:, n:n + 1], None, ALU.mult)
                if n % SSM_G == SSM_G - 1:
                    last.then_inc(normed_ready, 1)

        def rotate(src, chunks, outputs, hi, lo, table):
            def split_out(c):
                for n in range(outputs * c, outputs * c + outputs):
                    dve.wait_ge(rot_hi, turns(rot_hi))
                    bank = 4 + (turns.seen["rot_hi"] - 1) % 4
                    lo_part(lo[:, n, :], ps[:, bank, :], hi[:, n, :]).then_inc(rot_free, 1)

            for c in range(chunks):
                if c >= 2:
                    split_out(c - 2)
                for n in range(2):
                    nc.vector.tensor_tensor(rot_t[:, c % 2, n, :], src[:, c, :], table[:, n, :], ALU.mult) \
                        .then_inc(rot_in, 1)
            split_out(chunks - 2)
            split_out(chunks - 1)

        def compression():
            dve.wait_ge(nsa_in, 16 * NSA_PARAMS)
            for n in range(2 * KV):
                w, g = n // KV, n % KV
                dve.wait_ge(dup_ready, n + 1)
                for half in range(2):
                    rows = slice(HD * half, HD * half + HD)
                    x = ps[rows, 4 + n % 4, :].rearrange("p (n b two) -> p two b n", b=8, two=2)
                    for e in range(2):
                        pos = cols[rows, C_POS[w] + 8 * e:C_POS[w] + 8 * e + 8]
                        last = nc.vector.tensor_tensor(kcp[rows, w, 8 * e:8 * e + 8, N_CMP * g:N_CMP * g + N_CMP],
                                                       x[:, half, :, e:e + N_CMP],
                                                       pos.unsqueeze(2).to_broadcast([HD, 8, N_CMP]), ALU.add)
                last.then_inc(dup_free, 1)
            for w in range(2):
                dve.wait_ge(blocks_hi, w + 1)
                lo_part(kcpl[:, w, :, :], kcp[:, w, :, :], kcph[:, w, :, :]).then_inc(blocks_lo, 1)
            dve.wait_ge(blocks_lo, 2)
            rotate(kv8[:, 4:8, :], 4, 2, kdup_h, kdup_l, rotary)
            for w in range(2):
                split(0)
                split(1)
            turns(marks, 6)
            dve.wait_ge(cmp_ready, 1)
            nc.vector.tensor_copy(kcmp[:], ps[:, 4, 0:P].rearrange("p (g c) -> p g c", g=KV))
            same = cmp_mask[:, TB * CMP:].unsqueeze(2).to_broadcast([P, QG, HD])
            for g in range(KV):
                last = nc.vector.tensor_tensor(vbd[:, g, :].rearrange("p (h d) -> p h d", h=QG),
                                               ps[:, 5:6, HD * g:HD * g + HD].to_broadcast([P, QG, HD]), same, ALU.mult)
            last.then_inc(cmp_kept, 1)

        def compressed_weights():
            stat = lambda n: cst2[:, n, :]
            by_token = lambda x: x.rearrange("p (t h) -> p t h", t=TB)
            wide = lambda n: by_token(stat(n)).unsqueeze(3).to_broadcast([P, TB, 4 * QG, CMP])
            every = pc[:].rearrange("p t h c -> p (t h) c")
            dve.wait_ge(c_scores, 1)
            mask = cmp_mask[:, 0:TB * CMP].rearrange("p (t c) -> p t c", t=TB).unsqueeze(2)
            for side in range(2):
                for b in range(2):
                    last = nc.vector.tensor_tensor(
                        pc[:, 2 * b:2 * b + 2].rearrange("p t (pair side) c -> p side t pair c", side=2)[:, side],
                        ps[:, 2 * side + b, :].rearrange("p (t pair c) -> p t pair c", t=2, pair=KC),
                        mask[:, 2 * b:2 * b + 2].to_broadcast([P, 2, KC, CMP]), ALU.add)
            stored(last)
            stored(nc.vector.tensor_reduce(stat(0), every, AX.X, ALU.max))
            stored(nc.vector.tensor_scalar(stat(0), stat(0), -1.0e20, None, ALU.max))
            nc.vector.tensor_tensor(pc[:], pc[:], wide(0), ALU.subtract).then_inc(c_args, 1)
            dve.wait_ge(c_exps, 1)
            stored(nc.vector.tensor_reduce(stat(1), every, AX.X, ALU.add))
            stored(nc.vector.tensor_scalar(stat(1), stat(1), 0.5, None, ALU.max))
            stored(nc.vector.reciprocal(stat(2), stat(1)))
            dve.wait_ge(gates_ready, 1)
            gate = gates[:].rearrange("p t (h branch) -> p branch t h", branch=3)
            stored(nc.vector.tensor_tensor(by_token(stat(3)), by_token(stat(2)), gate[:, 0], ALU.mult))
            nc.vector.tensor_tensor(pc[:], pc[:], wide(3), ALU.mult).then_inc(c_probs, 1)

        def nsa_attention():
            def maximum(n, tb):
                dve.wait_ge(n_scores, turns(n_scores))
                nc.vector.tensor_reduce(nst[:, n % 2, 0, tb:tb + 1], ps[:, tb, 0:P * tb + P], AX.X, ALU.max,
                                        negate=True).then_inc(n_max, 1)

            with turns.loop(dve, KV, {dve_step: 8, n_scores: 32, n_hi: 24, n_exps: 32, n_out_hi: 2}) as g:
                for tb in T_STRIPS:
                    maximum(0, tb)
                for n in range(2 * QG):
                    s = n % 2
                    if n + 1 < 2 * QG:
                        for tb in (3, 2, 0):
                            maximum(n + 1, tb)
                    dve.wait_ge(n_exps, turns(n_exps, 4))
                    stored(nc.vector.reciprocal(nst[:, s, 2, :], nst[:, s, 1, :]))
                    nc.vector.tensor_tensor(nst[:, s, 3, :].unsqueeze(2), nst[:, s, 2, :].unsqueeze(2),
                                            gates[:, :, bass.ds(12 * g + (3 * query_head(n) + 1 + n % 2), 1)],
                                            ALU.mult) \
                        .then_inc(n_fac, 1)
                    if n + 1 < 2 * QG:
                        maximum(n + 1, 1)
                    for r, blocks in enumerate(ROUNDS):
                        dve.wait_ge(n_hi, turns(n_hi))
                        c = slice(512 * r, 512 * r + P * len(blocks))
                        lo_part(pnt_l[:, c], ps[:, 4 + (3 * n + r) % 2, 0:P * len(blocks)], pnt_h[:, c]) \
                            .then_inc(n_lo, 1)
                    if n in (QG, 2 * QG - 1):
                        pair = int(n > QG)
                        dve.wait_ge(n_out_hi, turns(n_out_hi))
                        lo_part(actl[:, 2 * g + pair, :], ps[:, 6 + pair, :], acth[:, 2 * g + pair, :]) \
                            .then_inc(n_taken, 1)

        def make_diag(gate):
            last = nc.vector.tensor_tensor(gate_diag[:], ident[:].unsqueeze(1).to_broadcast([P, KC, P]),
                                           modv[:, gate:gate + KC].unsqueeze(2).to_broadcast([P, KC, P]), ALU.mult)
            return last.then_inc(diag_ready, 1)

        dve.sem_inc(bank_free, FREE0)
        dve.sem_inc(h_sum, FREE0)
        dve.sem_inc(conv_done, FREE0)
        dve.sem_inc(branch_out, FREE0)
        dve.sem_inc(tok_free, 4)
        dve.sem_inc(hid_value, HID0)
        dve.sem_inc(group_y, DONE0)
        dve.sem_inc(n_taken, PAIRS0)
        dve.sem_inc(mod_acc, MODS)
        dve.sem_inc(turned_free, 4)
        dve.sem_inc(o_free, 2)
        dve.sem_inc(unit_ready, SLOTS)
        nc.vector.memset(neg_ones[:], -1.0).then_inc(set_up, 1)
        nc.vector.memset(ones_c[:], 1.0).then_inc(set_up, 1)
        dve.wait_ge(ident_in, 16)
        nc.vector.tensor_copy(ident_b[:], ident[:]).then_inc(set_up, 1)
        turned_los(actl, acth)
        split(0)
        split(1)
        dve.wait_ge(turned_hi, turns(turned_hi))
        nc.vector.tensor_copy(small[:, 0:1], cols[:, 0:1]).then_inc(turned_free, 1)
        dve.wait_ge(c_ready, 1)
        splits(4, mods=QK_MODS, col=0)
        token_banks(2, lambda i, t: nc.vector.tensor_copy(v_s[:, t, bass.ds(512 * i, 512)], ps[:, t, :]),
                    mods=4, col=8 * QK_MODS)
        stick_breaking()
        turned_los(meml, memh, MB)
        splits(2, mods=2, col=48)
        token_banks(2, lambda i, t: nc.vector.tensor_copy(vx[:, t, bass.ds(512 * i, 512)], ps[:, t, :]), nt=MB,
                    mods=2, col=56)
        residual_norm(mods=4, col=64)
        turned_los(actl, acth)
        split(1)
        splits(2, mods=4, col=80)
        cross_attention()
        residual_norm(mods=4, col=96)
        turned_los(actl, acth)
        split(1)
        dve.wait_ge(mod_done, 16)
        for n, (scale, g) in enumerate(((8, C_PRE_MIX), (56, C_PRE_MIX + KC), (32, C_PRE_FFN), (80, C_PRE_FFN + KC),
                                        (104, C_KVN))):
            nc.vector.scalar_tensor_tensor(out=gains[:, n, :], in0=modv[:, scale:scale + KC], scalar=1.0,
                                           in1=cols[:, g:g + KC], op0=ALU.add, op1=ALU.mult)
        conv_ffn()
        residual_norm(FC, then_norm=True)
        modulated_los(actl, acth, shape=(0, 0))
        split(1)
        conv_pairs(4, 0)
        conv_pairs(1, 16)
        conv_pairs(1, 20)
        dve.wait_ge(wdt_hi, 1)
        lo_part(wdt_l[:], wdt[:], wdt_h[:]).then_inc(wdt_lo, 1)
        with turns.loop(dve, 4, {hi_ready: 2}):
            split(0)
            split(1)
        turns(marks, 20)
        dt_and_sums()
        scan()
        group_norm()
        modulated_los(yl, yh, DI // P)
        gate_gain(16)
        branch_norm(DI // P, branch_low)
        modulated_los(actl, acth, shape=(2, 24))
        split(1)
        turns(marks, 8 + 6)
        gated_ffn(40)
        turns(marks, 18)
        modulated_los(actl, acth, shape=(4, 96))
        split(1)
        splits(2)
        split(0)
        for t in range(TB):
            dve.wait_ge(v_hi, t + 1)
            lo_part(v_l[:, t, :], ps[:, t, :], v_h[:, t, :]).then_inc(bank_free, 1)
        split(1)
        turns(marks, 5)
        compression()
        dve.wait_ge(gate_hi, 1)
        lo_part(w_gate_l[:], w_gate[:], w_gate_h[:]).then_inc(gate_lo, 1)
        modulated_los(actl, acth, shape=(1, 48))
        splits(2)
        compressed_weights()
        dve.wait_ge(c_turned, KV)
        dve.wait_ge(rotary_in, 16)
        rotate(q_u, KC, 1, acth, actl, rotary_q)
        nsa_attention()
        gate_gain(64)
        branch_norm(KC, branch_low)
        modulated_los(actl, acth, shape=(3, 72))
        split(1)
        turns(marks, 10)
        gated_ffn(88, last=True)

    @block.gpsimd
    def _(pool):
        turns = Turns()

        def inverse_roots(eps, src=mean_var[:, :, 1], dst=rstd[:], n=TB):
            pool.wait_ge(moments, turns(moments))
            nc.gpsimd.tensor_scalar(dst, src, eps, None, ALU.add).then_inc(pool_step, 1)
            pool.wait_ge(pool_step, turns(pool_step))
            nc.gpsimd.tensor_tensor(dst, dst, neg_half[:, 0:n], ALU.pow).then_inc(rstd_ready, 1)
            pool.wait_ge(rstd_ready, turns(rstd_ready))

        def block_root(t, eps, ready, mv, dst, done):
            pool.wait_ge(ready, turns(ready))
            nc.gpsimd.tensor_scalar(dst[:, t:t + 1], mv[:, t, 1:2], eps, None, ALU.add).then_inc(pool_step, 1)
            pool.wait_ge(pool_step, turns(pool_step))
            nc.gpsimd.tensor_tensor(dst[:, t:t + 1], dst[:, t:t + 1], neg_half[:, 0:1], ALU.pow).then_inc(done, 1)
            pool.wait_ge(done, turns(done))

        def block_roots(eps, then_norm):
            for t in range(TB):
                block_root(t, eps, moments, mean_var, rstd, rstd_ready)
                if t and then_norm:
                    block_root(t - 1, RMS_EPS, norm_moments, norm_mv, norm_rstd, norm_root)
            if then_norm:
                block_root(TB - 1, RMS_EPS, norm_moments, norm_mv, norm_rstd, norm_root)

        def mod_loads(turns_, units, w, first):
            v = w.rearrange("(k p) c -> p k c", p=P)
            with turns.loop(pool, turns_, {mod_acc: units}) as i:
                for u in range(units):
                    pool.wait_ge(mod_acc, turns(mod_acc))
                    pool.dma_start(mraw[:, u % 2, :, :], v[:, :, bass.ds(256 * units * i + 256 * (first + u), 256)]) \
                        .then_inc(mod_raw[u % 2], 16)

        def scan():
            pool.wait_ge(acs_out, 1)
            pool.wait_ge(tok_free, 4 + 20)
            with turns.loop(pool, SSM_G, {group_y: 1, heads_staged: 2, decay_exp: 8, cb_out: 1, mixed: 8,
                                          dx_ready: 4}) as g:
                pool.wait_ge(group_y, turns(group_y) - 1 + DONE0)
                for dst, src in ((dtag[:], dta[:, :, bass.ds(HPG * g, HPG)]),
                                 (acsg[:], acs[:, :, bass.ds(HPG * g, HPG)])):
                    nc.gpsimd.tensor_copy(dst, src).then_inc(heads_staged, 1)
                    pool.wait_ge(heads_staged, turns(heads_staged))
                pool.wait_ge(cb_out, turns(cb_out))
                for hd in range(HPG):
                    pool.wait_ge(decay_exp, turns(decay_exp))
                    nc.gpsimd.tensor_tensor(decay[:, hd % 2, :], decay[:, hd % 2, :], cbm[:], ALU.mult) \
                        .then_inc(mixed, 1)
                    pool.wait_ge(mixed, turns(mixed))
                    if hd < TB:
                        nc.gpsimd.tensor_tensor(
                            dx[:, hd, :].rearrange("p (h d) -> p h d", h=HPG),
                            tok[:, hd, bass.ds(512 * g, 512)].rearrange("p (h d) -> p h d", h=HPG),
                            heads[:, 2, bass.ds(HPG * g, HPG)].unsqueeze(2).to_broadcast([P, HPG, 64]), ALU.mult) \
                            .then_inc(dx_ready, 1)
                        pool.wait_ge(dx_ready, turns(dx_ready))

        nc.gpsimd.memset(x_in[96:P, 2:4, :], 0.0).then_inc(pool_step, 1)
        pool.wait_ge(pool_step, turns(pool_step))
        nc.gpsimd.memset(neg_half[:], -0.5).then_inc(pool_step, 1)
        pool.wait_ge(pool_step, turns(pool_step))
        nc.gpsimd.memset(strict_b[:], 0.0).then_inc(pool_step, 1)
        pool.wait_ge(pool_step, turns(pool_step))
        nc.gpsimd.affine_select(out=strict_b[:], in_=strict_b[:], pattern=[[1, P]], compare_op=ALU.is_gt, fill=NEG,
                                base=0, channel_multiplier=-1).then_inc(set_up, 1)
        nc.gpsimd.memset(causal_b[:], 0.0).then_inc(pool_step, 1)
        pool.wait_ge(pool_step, turns(pool_step))
        nc.gpsimd.affine_select(out=causal_b[:], in_=causal_b[:], pattern=[[-1, P]], compare_op=ALU.is_ge, fill=NEG,
                                base=0, channel_multiplier=1).then_inc(set_up, 1)
        mod_loads(4, QK_MODS, a["mod_w_2"][0], 0)
        mod_loads(2, 4, a["mod_w_2"][0], 16)
        pool.wait_ge(bank_free, 4 + 24)
        with turns.loop(pool, 4, {o_free: 2, staged: 6}) as i:
            for pair in range(2):
                pool.wait_ge(o_free, turns(o_free))
                c = 2 * i + pair
                nc.gpsimd.tensor_copy(qst[:, pair, :], q_t[:, c, :]).then_inc(staged, 1)
                pool.wait_ge(staged, turns(staged))
                nc.gpsimd.tensor_copy(kst[:, pair, :], k_t[:, c, :]).then_inc(staged, 1)
                pool.wait_ge(staged, turns(staged))
                nc.gpsimd.tensor_copy(vst[:, pair, :, :], v_s[:, :, bass.ds(P * c, P)]).then_inc(staged, 1)
                pool.wait_ge(staged, turns(staged))
        pool.wait_ge(o_free, 2 + KC)
        mod_loads(2, 2, a["mod_w_2"][1], 0)
        mod_loads(2, 2, a["mod_w_2"][1], 4)
        mod_loads(2, 4, a["mod_w_2"][1], 8)
        block_roots(LN_EPS, False)
        mod_loads(2, 4, a["mod_w_2"][1], 16)
        mod_loads(2, 4, a["kv_mod_w_2"], 0)
        block_roots(LN_EPS, False)
        block_roots(LN_EPS, True)
        for kind in range(2):
            for j in range(4):
                pool.wait_ge(convolved, 16 + 4 * kind + j + 1)
                nc.gpsimd.tensor_copy(bct[:, 4 * kind + j, :], conv4[:, j, :]).then_inc(bc_copied, 1)
                pool.wait_ge(bc_copied, turns(bc_copied))
        scan()
        inverse_roots(RMS_EPS, ginv[:], ginv[:], TB * SSM_G)
        block_roots(RMS_EPS, True)
        block_roots(RMS_EPS, True)
        for x in (hid_k, hid_v):
            nc.gpsimd.memset(x[:], 0.0).then_inc(hid_padded, 1)
            pool.wait_ge(hid_padded, turns(hid_padded))
        pool.wait_ge(c_copied, KV)
        pool.wait_ge(rot_free, 2 * KV + KC)
        nc.gpsimd.memset(v_st[:].bitcast(F32), 0.0).then_inc(pool_step, 1)
        pool.wait_ge(pool_step, turns(pool_step))
        with turns.loop(pool, KV, {n_taken: 2, v_in: 2, n_diag: 8, n_fac: 8}) as g:
            for n in range(2 * QG):
                if n == 0:
                    pool.wait_ge(n_taken, turns(n_taken, 2) - 2 + PAIRS0)
                    nc.gpsimd.tensor_copy(vb_g[:], vbd[:, g, :]).then_inc(v_in, 1)
                    pool.wait_ge(v_in, turns(v_in))
                    nc.gpsimd.tensor_copy(v_st[:, :, :, :, 1, :].rearrange("p s t w c -> p (s t) w c"),
                                          v_hl[:].rearrange("p s t (w c) -> p (s t) w c", w=2)
                                          [:, :, :, bass.ds(HD * g, HD)]).then_inc(v_in, 1)
                    pool.wait_ge(v_in, turns(v_in))
                pool.wait_ge(n_fac, turns(n_fac))
                nc.gpsimd.tensor_tensor(diag[:, n % 2, :, :], ident[:].unsqueeze(1).to_broadcast([P, TB, P]),
                                        nst[:, n % 2, 3, :].unsqueeze(2).to_broadcast([P, TB, P]), ALU.mult) \
                    .then_inc(n_diag, 1)
                pool.wait_ge(n_diag, turns(n_diag))
        block_roots(RMS_EPS, True)
        block_roots(RMS_EPS, False)

    engines.close()
    ctx.close()


_INS = (
    "x mem ln_g ln_b mix_wo sb_win xa_wq xa_wkv xa_wo ffn_up ffn_conv ffn_conv_b ffn_down c_2 mod_w_2 mod_b_2 "
    "norm_pre_mix_2 norm_post_mix_2 norm_pre_ffn_2 norm_post_ffn_2 ffn_w_in_2 ffn_w_out_2 ssm_w_in_2 "
    "ssm_conv_w_2 ssm_conv_b_2 ssm_dt_bias_2 ssm_a_log_2 ssm_d_2 ssm_norm_2 ssm_w_out_2 kv_norm_2 kv_mod_w_2 "
    "kv_mod_b_2 w_kv_2 cmp_pos_k_2 cmp_w1_k_2 cmp_w2_k_2 cmp_pos_v_2 cmp_w1_v_2 cmp_w2_v_2 nsa_w_q_2 nsa_w_o_2"
).split()


def kernel(**inputs):
    import concourse.bacc as _bacc
    from concourse.bass_utils import run_bass_kernel_spmd as _run

    nc = _bacc.Bacc("TRN2", target_bir_lowering=False, num_devices=1)
    arrays, dram = {}, {}
    given = {name: np.ascontiguousarray(inputs[name]) for name in _INS}
    given.update(shape_constants())
    for name, array in given.items():
        arrays[f"in_{name}"] = array
        dram[name] = nc.dram_tensor(f"in_{name}", array.shape, mybir.dt.from_np(array.dtype),
                                    kind="ExternalInput").ap()
    out = nc.dram_tensor("out", (1, SEQ, D), F32, kind="ExternalOutput").ap()
    build(nc, dram, out)
    r = _run(nc, [arrays], core_ids=[0])
    return r.results[0]["out"]
```
